# Optimizing a Trainium2 kernel written in Bass

```python
import math
import jax, jax.numpy as jnp
from jax import lax
import numpy as np

D_MODEL = 1024
BATCH = 1
SEQ = 1024
DEPTH = 2

N_META = 16
BLOCK = 128
PAD_FRONT = BLOCK - N_META
HEAD_DIM = 64
SB_HEADS = 4
DIFF_HEADS = 4
CONV_GROUPS = 8
SB_W = SB_HEADS * HEAD_DIM
DIFF_W = DIFF_HEADS * HEAD_DIM
CONV_W = CONV_GROUPS * HEAD_DIM
MIX_W = SB_W + DIFF_W + CONV_W
IN_COLS = 3 * SB_W + 3 * DIFF_W + 3 * CONV_W
DIFF_SUB = HEAD_DIM // 2
ROPE_DIM = DIFF_SUB // 4
ROPE_THETA = 500000.0
CONV_K = 3
N_EXPERTS = 16
N_GROUPS = 4
EXPERTS_PER_GROUP = N_EXPERTS // N_GROUPS
TOP_K = 2
D_FF_EXPERT = 128
ALPHA = (2.0 * DEPTH) ** 0.25
BETA_INIT = (8.0 * DEPTH) ** -0.25
LN_EPS = 1e-5
NEG_BIG = -1e30

kernel_name = "hybrid_sb_diff_conv_grouped_moe"

def layer_norm(x, g, b):
    xf = x.astype(jnp.float32)
    mu = jnp.mean(xf, axis=-1, keepdims=True)
    xc = xf - mu
    var = jnp.mean(xc * xc, axis=-1, keepdims=True)
    y = xc * lax.rsqrt(var + LN_EPS) * g.astype(jnp.float32) + b.astype(jnp.float32)
    return y.astype(x.dtype)

def rms_norm(x, g):
    xf = x.astype(jnp.float32)
    y = xf * lax.rsqrt(jnp.mean(xf * xf, axis=-1, keepdims=True) + LN_EPS) * g.astype(jnp.float32)
    return y.astype(x.dtype)

def rope_tables(length, dtype):
    pos = (jnp.arange(length) - PAD_FRONT).astype(jnp.float32)
    inv = jnp.power(jnp.float32(ROPE_THETA), -jnp.arange(0, ROPE_DIM, 2, dtype=jnp.float32) / ROPE_DIM)
    ang = pos[:, None] * inv[None, :]
    return jnp.cos(ang).astype(dtype), jnp.sin(ang).astype(dtype)

def partial_rope(t, cos, sin):
    half = ROPE_DIM // 2
    x1, x2, rest = t[..., :half], t[..., half:ROPE_DIM], t[..., ROPE_DIM:]
    return jnp.concatenate([x1 * cos - x2 * sin, x1 * sin + x2 * cos, rest], axis=-1)

def _heads(t, n):
    b, l, _ = t.shape
    return t.reshape(b, l, n, -1).transpose(0, 2, 1, 3)

def _unheads(t):
    b, h, l, d = t.shape
    return t.transpose(0, 2, 1, 3).reshape(b, l, h * d)

def _strict_lower(n):
    return (jnp.arange(n)[:, None] > jnp.arange(n)[None, :]).astype(jnp.float32)

def stick_breaking_attention(q, k, v):
    b, h, length, _ = q.shape
    nb = length // BLOCK
    scale = HEAD_DIM ** -0.5
    tri_in = _strict_lower(BLOCK)
    outs = []
    for i in range(nb):
        nk = i + 1
        lk = nk * BLOCK
        qb = q[:, :, i * BLOCK:(i + 1) * BLOCK]
        kp, vp = k[:, :, :lk], v[:, :, :lk]
        z = jnp.einsum('bhqd,bhkd->bhqk', qb, kp).astype(jnp.float32) * scale
        q_idx = i * BLOCK + jnp.arange(BLOCK)
        key_idx = jnp.arange(lk)
        m = (key_idx[None, :] < q_idx[:, None]) & (key_idx[None, :] >= PAD_FRONT)
        log_beta = jax.nn.log_sigmoid(z)
        log_rem = jnp.where(m, log_beta - z, 0.0).reshape(b, h, BLOCK, nk, BLOCK)
        intra = jnp.einsum('bhqnj,js->bhqns', log_rem, tri_in)
        later = jnp.einsum('bhqn,nm->bhqm', log_rem.sum(-1), _strict_lower(nk))
        after = (intra + later[..., None]).reshape(b, h, BLOCK, lk)
        w = jnp.where(m, jnp.exp(log_beta + after), 0.0)
        outs.append(jnp.einsum('bhqk,bhkd->bhqd', w.astype(v.dtype), vp))
    return jnp.concatenate(outs, axis=2)

def differential_attention(q, k, v, lq1, lk1, lq2, lk2, norm_g, lam_init, cos, sin):
    b, length, _ = q.shape
    q = partial_rope(q.reshape(b, length, DIFF_HEADS, 2, DIFF_SUB).transpose(0, 2, 3, 1, 4), cos, sin)
    k = partial_rope(k.reshape(b, length, DIFF_HEADS, 2, DIFF_SUB).transpose(0, 2, 3, 1, 4), cos, sin)
    q1, q2 = q[:, :, 0], q[:, :, 1]
    k1, k2 = k[:, :, 0], k[:, :, 1]
    v = _heads(v, DIFF_HEADS)
    f32 = jnp.float32
    lam = (jnp.exp(jnp.sum(lq1.astype(f32) * lk1.astype(f32)))
           - jnp.exp(jnp.sum(lq2.astype(f32) * lk2.astype(f32))) + lam_init)
    scale = DIFF_SUB ** -0.5
    nb = length // BLOCK
    outs = []
    for i in range(nb):
        lk = (i + 1) * BLOCK
        sl = slice(i * BLOCK, (i + 1) * BLOCK)
        q_idx = i * BLOCK + jnp.arange(BLOCK)
        key_idx = jnp.arange(lk)
        m = (key_idx[None, :] <= q_idx[:, None]) & (key_idx[None, :] >= PAD_FRONT)
        s1 = jnp.einsum('bhqd,bhkd->bhqk', q1[:, :, sl], k1[:, :, :lk]).astype(f32) * scale
        s2 = jnp.einsum('bhqd,bhkd->bhqk', q2[:, :, sl], k2[:, :, :lk]).astype(f32) * scale
        a = (jax.nn.softmax(jnp.where(m, s1, NEG_BIG), axis=-1)
             - lam * jax.nn.softmax(jnp.where(m, s2, NEG_BIG), axis=-1))
        outs.append(jnp.einsum('bhqk,bhkd->bhqd', a.astype(v.dtype), v[:, :, :lk]))
    out = jnp.concatenate(outs, axis=2)
    out = rms_norm(out, norm_g) * jnp.asarray(1.0 - lam_init, out.dtype)
    return _unheads(out)

def short_gated_conv(gate_b, gate_c, h, conv_w, valid):
    length = h.shape[1]
    u = gate_c * h * valid[None, :, None].astype(h.dtype)
    u_pad = jnp.pad(u, ((0, 0), (CONV_K - 1, 0), (0, 0)))
    conv = sum(conv_w[j] * u_pad[:, j:j + length] for j in range(CONV_K))
    return gate_b * conv

def grouped_moe(h, router_w, router_bias, w_gate, w_up, w_down):
    f32 = jnp.float32
    logits = jnp.einsum('bld,de->ble', h, router_w).astype(f32)
    probs = jax.nn.softmax(logits, axis=-1)
    sel = probs + router_bias.astype(f32)
    sel_g = sel.reshape(sel.shape[:-1] + (N_GROUPS, EXPERTS_PER_GROUP))
    group_score = lax.top_k(sel_g, TOP_K)[0].sum(-1)
    g = jnp.argmax(group_score, axis=-1)
    in_g = jnp.take_along_axis(sel_g, g[..., None, None], axis=-2)[..., 0, :]
    _, local = lax.top_k(in_g, TOP_K)
    eidx = g[..., None] * EXPERTS_PER_GROUP + local
    wsel = jnp.take_along_axis(probs, eidx, axis=-1)
    wsel = wsel / jnp.sum(wsel, axis=-1, keepdims=True)
    gates = jnp.sum(jax.nn.one_hot(eidx, N_EXPERTS, dtype=f32) * wsel[..., None], axis=-2).astype(h.dtype)
    hid = (jax.nn.silu(jnp.einsum('bld,edf->blef', h, w_gate))
           * jnp.einsum('bld,edf->blef', h, w_up) * gates[..., None])
    return jnp.einsum('blef,efd->bld', hid, w_down)

def setup_inputs(seed: int = 0) -> dict:
    key = jax.random.key(seed)
    ks = jax.random.split(key, 20)
    nrm = jax.random.normal
    f32 = jnp.float32
    return {
        "x": nrm(ks[0], (BATCH, SEQ, D_MODEL), f32),
        "meta_tokens": nrm(ks[1], (N_META, D_MODEL), f32),
        "w_in": nrm(ks[2], (DEPTH, D_MODEL, IN_COLS), f32) * D_MODEL ** -0.5,
        "conv_w": nrm(ks[3], (DEPTH, CONV_K, CONV_W), f32) * CONV_K ** -0.5,
        "lambda_q1": nrm(ks[4], (DEPTH, DIFF_SUB), f32) * 0.1,
        "lambda_k1": nrm(ks[5], (DEPTH, DIFF_SUB), f32) * 0.1,
        "lambda_q2": nrm(ks[6], (DEPTH, DIFF_SUB), f32) * 0.1,
        "lambda_k2": nrm(ks[7], (DEPTH, DIFF_SUB), f32) * 0.1,
        "diff_norm_g": 1.0 + 0.02 * nrm(ks[8], (DEPTH, HEAD_DIM), f32),
        "w_out": nrm(ks[9], (DEPTH, MIX_W, D_MODEL), f32) * MIX_W ** -0.5 * BETA_INIT,
        "ln1_g": 1.0 + 0.02 * nrm(ks[10], (DEPTH, D_MODEL), f32),
        "ln1_b": 0.02 * nrm(ks[11], (DEPTH, D_MODEL), f32),
        "router_w": nrm(ks[12], (D_MODEL, N_EXPERTS), f32) * D_MODEL ** -0.5,
        "router_bias": 0.01 * nrm(ks[13], (N_EXPERTS,), f32),
        "w_gate": nrm(ks[14], (DEPTH, N_EXPERTS, D_MODEL, D_FF_EXPERT), f32) * D_MODEL ** -0.5,
        "w_up": nrm(ks[15], (DEPTH, N_EXPERTS, D_MODEL, D_FF_EXPERT), f32) * D_MODEL ** -0.5,
        "w_down": nrm(ks[16], (DEPTH, N_EXPERTS, D_FF_EXPERT, D_MODEL), f32) * D_FF_EXPERT ** -0.5 * BETA_INIT,
        "ln2_g": 1.0 + 0.02 * nrm(ks[17], (DEPTH, D_MODEL), f32),
        "ln2_b": 0.02 * nrm(ks[18], (DEPTH, D_MODEL), f32),
    }

def reference(x, meta_tokens, w_in, conv_w, lambda_q1, lambda_k1, lambda_q2, lambda_k2,
              diff_norm_g, w_out, ln1_g, ln1_b, router_w, router_bias, w_gate, w_up, w_down,
              ln2_g, ln2_b):
    b = x.shape[0]
    lead = jnp.concatenate([
        jnp.zeros((PAD_FRONT, D_MODEL), x.dtype), meta_tokens.astype(x.dtype)], axis=0)
    h = jnp.concatenate([jnp.broadcast_to(lead[None], (b, BLOCK, D_MODEL)), x], axis=1)
    length = h.shape[1]
    valid = jnp.arange(length) >= PAD_FRONT
    cos, sin = rope_tables(length, x.dtype)
    o1 = 3 * SB_W
    o2 = o1 + 3 * DIFF_W
    for l in range(DEPTH):
        lam_init = 0.8 - 0.6 * math.exp(-0.3 * l)
        proj = h @ w_in[l]
        sq, sk, sv = jnp.split(proj[..., :o1], 3, axis=-1)
        dq, dk, dv = jnp.split(proj[..., o1:o2], 3, axis=-1)
        cb, cc, ch = jnp.split(proj[..., o2:], 3, axis=-1)
        y_sb = _unheads(stick_breaking_attention(_heads(sq, SB_HEADS), _heads(sk, SB_HEADS), _heads(sv, SB_HEADS)))
        y_diff = differential_attention(dq, dk, dv, lambda_q1[l], lambda_k1[l], lambda_q2[l], lambda_k2[l],
                                        diff_norm_g[l], lam_init, cos, sin)
        y_conv = short_gated_conv(cb, cc, ch, conv_w[l], valid)
        mix = jnp.concatenate([y_sb, y_diff, y_conv], axis=-1) @ w_out[l]
        h = layer_norm(ALPHA * h + mix, ln1_g[l], ln1_b[l])
        ffn = grouped_moe(h, router_w, router_bias, w_gate[l], w_up[l], w_down[l])
        h = layer_norm(ALPHA * h + ffn, ln2_g[l], ln2_b[l])
    return h[:, BLOCK:]


_drawn_inputs = setup_inputs


def setup_inputs(seed=0):
    import zlib

    import numpy as np

    out = dict(_drawn_inputs(seed))
    spreads = {}
    factors = {'lambda_q2': 7.088, 'diff_norm_g': 3.249}
    for name, (base, spread) in spreads.items():
        noise = np.random.default_rng([zlib.crc32(name.encode()), seed]).standard_normal(out[name].shape)
        drawn = base * np.exp(spread * noise) if base else spread * noise
        out[name] = __import__('jax').numpy.asarray(drawn.astype(out[name].dtype))
    for name, factor in factors.items():
        out[name] = (out[name] * factor).astype(out[name].dtype)
    return out
```

```python
import math
from contextlib import ExitStack

import numpy as np

import concourse.bass as bass
from concourse import mybir

F32 = mybir.dt.float32
F32R = mybir.dt.float32r
BF16 = mybir.dt.bfloat16
I32 = mybir.dt.int32
U32 = mybir.dt.uint32
ALU = mybir.AluOpType
ACT = mybir.ActivationFunctionType
AX = mybir.AxisListType.X
ds = bass.ds

P = 128
D = 1024
KD = D // P
SEQ = 1024
N_META = 16
TOK = SEQ + N_META
TILES = -(-TOK // P)
ROWS = TILES * P
XT = SEQ // P
META0 = SEQ
DEPTH = 2
IN_COLS = 3072
HD = 64
QKV_TILES = 12
CONV_TILES = 4
CONV0 = QKV_TILES * P
CONV_W = CONV_TILES * P
SB_Q, SB_K, SB_V, DF_Q, DF_K, DF_V = range(0, 12, 2)
SUB = 32
ROPE = 8
N_EXP = 16
N_GRP = 4
FF = 128
BLOCKS = N_EXP + (2 * TOK - N_EXP) // P
ALPHA = (2.0 * DEPTH) ** 0.25
EPS = 1e-5
NEG = -1e30
SB_SCALE = HD ** -0.5
DF_SCALE = SUB ** -0.5

CHUNKS = [(0, 348), (348, 694), (694, TOK)]

CONST_COLS = dict(ident=P, suffix=P, prefix=P, ones=P, rotate=P, negmask=P + 4, iota=P, tokid=TILES,
                  valid=TILES, prio16=16, prio4=4, thr=TILES, thr_blk=BLOCKS, half=1)


def const_slices():
    at, out = 0, {}
    for name, n in CONST_COLS.items():
        out[name] = slice(at, at + n)
        at += n
    return out, at


def shape_constants():
    where, total = const_slices()
    c = np.zeros((P, total), np.float32)
    r = np.arange(P)
    c[:, where["ident"]] = np.eye(P)
    c[:, where["suffix"]] = r[:, None] >= r[None, :]
    c[:, where["prefix"]] = r[:, None] < r[None, :]
    c[:, where["ones"]] = 1.0
    rot = np.zeros((P, P), np.float32)
    for p in range(P):
        j = p % SUB
        if j < ROPE // 2:
            rot[p + ROPE // 2, p] = -1.0
        elif j < ROPE:
            rot[p - ROPE // 2, p] = 1.0
    c[:, where["rotate"]] = rot
    neg = np.full((P, P + 4), NEG, np.float32)
    neg[:, :P] = np.where(r[None, :] <= r[:, None], 0.0, NEG)
    c[:, where["negmask"]] = neg
    c[:, where["iota"]] = r[None, :]
    tok = np.arange(TILES)[None, :] * P + r[:, None]
    c[:, where["tokid"]] = tok
    c[:, where["valid"]] = tok < TOK
    c[:, where["prio16"]] = 16 - np.arange(16)
    c[:, where["prio4"]] = 4 - np.arange(4)
    c[:, where["thr"]] = np.arange(TILES) * P
    c[:, where["thr_blk"]] = (np.arange(BLOCKS) + 1) * P
    c[:, where["half"]] = -0.5
    return c


def rope_constants():
    pos = np.concatenate([np.arange(SEQ) + N_META, np.arange(N_META)]).astype(np.float32)
    inv = (500000.0 ** (-np.arange(0, ROPE, 2) / ROPE)).astype(np.float32)
    ang = (pos[None, :] * inv[:, None]).astype(np.float32).astype(np.float64)
    cos, sin = np.ones((P, TOK)), np.zeros((P, TOK))
    for p in range(P):
        j = p % SUB
        if j < ROPE:
            cos[p], sin[p] = np.cos(ang[j % (ROPE // 2)]), np.sin(ang[j % (ROPE // 2)])
    return np.stack([cos, sin]).astype(np.float32)


def layer_constants():
    lam = [0.8 - 0.6 * math.exp(-0.3 * l) for l in range(DEPTH)]
    return np.array([[v, 1.0 - v] for v in lam], np.float32)


def row_pieces(i):
    if i == XT:
        return 1, N_META
    keys = N_META + (i + 1) * P
    n = -(-keys // 512)
    w = -(-keys // n)
    return n, w + w % 2


DIFF_ROWS = [XT] + list(range(XT))
DIFF_KEYS = max(n * w for n, w in map(row_pieces, DIFF_ROWS))


def key_tiles(i):
    out = [(XT, 0, N_META)]
    if i < XT:
        out += [(n, N_META + n * P, P) for n in range(i + 1)]
    return out


def sb_steps():
    out = []
    for first_tile in (4, 0):
        for n in list(range(first_tile + 3, -1, -1)) + [XT]:
            lo = max(0, n - first_tile) * P if n < XT else 0
            out.append(dict(tile0=first_tile, lo=lo, hi=512, key=n,
                            diag=n < XT and n >= first_tile,
                            first=n == first_tile + 3, last=n == XT))
    out.append(dict(tile0=XT, lo=0, hi=P, key=XT, diag=True, first=True, last=True))
    return out


SB_STEPS = [dict(s, head=h) for s in sb_steps() for h in range(2)]


class Map:

    def __init__(self, nc, at, end):
        self.nc, self.at, self.end = nc, at, end

    def put(self, name, shape, dt, size=4):
        n = size
        for s in shape[1:]:
            n *= s
        t = self.nc.alloc_sbuf_tensor_at(name, shape, dt, offset=self.at)
        self.at += (n + 31) // 32 * 32
        assert self.at <= self.end, (name, self.at, self.end)
        return t


def f32(ap):
    return ap.bitcast(F32)


def wait_apart(eng, sem, value, passed):
    eng.wait_ge(sem, value)
    eng.sem_inc(passed, 1)


class Link:

    def __init__(self, eng, sem, base=0):
        self.eng, self.sem, self.base, self.n = eng, sem, base, 0

    def __call__(self, ins):
        self.n += 1
        ins.then_inc(self.sem, 1)
        self.eng.wait_ge(self.sem, self.base + self.n)


def three_passes(pe, out, stat_hi, stat_lo, mov_hi, mov_lo, start, stop):
    pe.matmul(out, stat_lo, mov_hi, start=start, stop=False)
    pe.matmul(out, stat_hi, mov_lo, start=False, stop=False)
    return pe.matmul(out, stat_hi, mov_hi, start=False, stop=stop)


def build_trunk(nc, x, meta_tokens, w_in, conv_w, lambda_q1, lambda_k1, lambda_q2, lambda_k2,
                diff_norm_g, w_out, ln1_g, ln1_b, router_w, router_bias, w_gate, w_up, w_down,
                ln2_g, ln2_b, consts, rope, lam_consts, out):
    h_dram = nc.dram_tensor("h_rows", [ROWS, D], F32, kind="Internal").ap()
    h1_dram = nc.dram_tensor("h1_rows", [ROWS, D], F32, kind="Internal").ap()
    y_dram = nc.dram_tensor("y_slots", [BLOCKS * P, D], F32, kind="Internal").ap()

    ctx = ExitStack()
    with ctx:
        base = (nc.sbuf_base + 63) // 64 * 64
        end = nc.sbuf_usable_end
        m = Map(nc, base, end)
        where, n_const = const_slices()
        cst = m.put("cst", [P, n_const], F32)
        C = {k: cst[:, v] for k, v in where.items()}
        suffix = m.put("suffix", [P, P], F32R)
        prefix = m.put("prefix", [P, P], F32R)
        ident_bf = m.put("ident_bf", [P, P], BF16, 2)
        negmask_bf = m.put("negmask_bf", [P, P + 4], BF16, 2)
        router = m.put("router", [P, KD, N_EXP], F32)
        rbias = m.put("rbias", [P, N_EXP], F32)
        logits = m.put("logits", [P, TILES, N_EXP], F32)
        slot_u = m.put("slot_u", [P, 2, TILES], U32)
        tokmap = m.put("tokmap", [P, BLOCKS], U32)
        gatemap = m.put("gatemap", [P, BLOCKS], F32)
        idx = [m.put(f"idx{i}", [P, 1], U32) for i in range(2)]
        f_idx_t = [m.put(f"f_idx_t{i}", [P, 2], U32) for i in range(3)]
        blk_exp = m.put("blk_exp", [P, BLOCKS], I32)
        stat = m.put("stat", [P, 3, 16], F32)
        m.at = (m.at + 63) // 64 * 64
        at0 = m.at
        act_hi = m.put("act_hi", [P, KD, ROWS], F32R)
        act_lo = m.put("act_lo", [P, KD, ROWS], F32R)
        under = m.at

        a = Map(nc, under, end)
        qkv = a.put("qkv", [P, QKV_TILES, TOK], F32)
        conv_y = a.put("conv_y", [P, CONV_TILES, TOK], F32)
        after_qkv = a.at
        w_raw = [a.put(f"w_raw{b}", [P, KD, P], F32) for b in range(3)]
        w_hi = [a.put(f"w_hi{b}", [P, KD, P], F32R) for b in range(3)]
        w_lo = [a.put(f"w_lo{b}", [P, KD, P], F32R) for b in range(3)]
        gate_b = a.put("gate_b", [P, TOK], F32)
        gate_c = a.put("gate_c", [P, TOK], F32)
        conv_u = a.put("conv_u", [P, TOK + 2], F32)
        conv_t = a.put("conv_t", [P, TOK], F32)
        taps = a.put("taps", [P, CONV_TILES, 3], F32)

        b = Map(nc, after_qkv, end)
        v_rows = b.put("v_rows", [P, TILES, 512], F32)
        y_sb = b.put("y_sb", [P, TILES, 256], F32)
        y_df = b.put("y_df", [P, TILES, 256], F32)
        q_hi_at = b.at
        q_hi = b.put("q_hi", [P, ROWS], F32R)
        q_lo = b.put("q_lo", [P, ROWS], F32R)
        lam_in = b.put("lam_in", [P, 4, SUB], F32)
        lam = b.put("lam", [P, 8], F32)
        norm_g = b.put("norm_g", [P, HD], F32)
        t = Map(nc, at0, under)
        k_hi = t.put("k_hi", [P, ROWS], F32R)
        k_lo = t.put("k_lo", [P, ROWS], F32R)
        after_k = t.at
        zs = [t.put(f"zs{i}", [P, 512], F32) for i in range(4)]
        ez = [t.put(f"ez{i}", [P, 512], F32) for i in range(2)]
        sp = [t.put(f"sp{i}", [P, 512], F32) for i in range(2)]
        sp_hi = [t.put(f"sp_hi{i}", [P, 512], F32R) for i in range(4)]
        sp_lo = [t.put(f"sp_lo{i}", [P, 512], F32R) for i in range(4)]
        wt = [t.put(f"wt{i}", [P, 512], F32) for i in range(4)]
        t = Map(nc, after_k, under)
        cos_t = t.put("cos_t", [P, TOK], F32)
        sin_t = t.put("sin_t", [P, TOK], F32)
        rot_a = t.put("rot_a", [P, TOK], F32)
        rot_b = t.put("rot_b", [P, TOK], F32)
        prob = [[t.put(f"prob{u}{s}", [P, DIFF_KEYS], F32) for s in range(2)] for u in range(2)]
        a_t = [t.put(f"a_t{u}", [P, TILES, P], F32) for u in range(2)]
        df_stat = [t.put(f"df_stat{u}", [P, 16], F32) for u in range(2)]
        t = Map(nc, q_hi_at, b.at)
        sq = t.put("sq", [P, TILES * 4, HD], F32)
        t = Map(nc, b.at, end)
        ms = t.put("ms", [P, TILES * 4], F32)
        rms = t.put("rms", [P, TILES * 4], F32)

        c = Map(nc, under, end)
        wo_hi = c.put("wo_hi", [P, KD, D], F32R)
        wo_lo = c.put("wo_lo", [P, KD, D], F32R)
        after_wo = c.at
        wo_raw = [c.put(f"wo_raw{i}", [P, D], F32) for i in range(2)]
        ln_g = c.put("ln_g", [P, D], F32)
        ln_b = c.put("ln_b", [P, D], F32)
        res = [c.put(f"res{i}", [P, D], F32) for i in range(3)]
        nrm = [c.put(f"nrm{i}", [P, D], F32) for i in range(3)]
        h1_t = c.put("h1_t", [P, KD, P], F32)
        f = Map(nc, under, after_wo)
        y_a = [f.put(f"y_a{i}", [P, D], F32) for i in range(3)]
        y_b = [f.put(f"y_b{i}", [P, D], F32) for i in range(3)]

        d = Map(nc, at0, under)
        sel = d.put("sel", [P, TILES, N_EXP], F32)
        prb = d.put("prb", [P, TILES, N_EXP], F32)
        tmp = [d.put(f"tmp{i}", [P, TILES, BLOCKS], F32) for i in range(3)]
        pair = d.put("pair", [P, TILES * N_GRP, 6], F32)
        small = d.put("small", [P, 16, TILES, N_GRP], F32)
        onehot = [d.put(f"onehot{i}", [P, TILES, N_EXP], F32) for i in range(2)]
        member = d.put("member", [P, TILES, N_EXP], F32)
        before = d.put("before", [P, TILES + 1, N_EXP], F32)
        slots = d.put("slots", [P, TILES, N_EXP], F32)
        blk = d.put("blk", [P, 8, N_EXP], F32)
        cnt_ge = d.put("cnt_ge", [P, N_EXP, BLOCKS], F32)
        at_pos = [d.put(f"at_pos{i}", [P, TILES, P], F32) for i in range(2)]
        at_blk = [d.put(f"at_blk{i}", [P, TILES, 2, BLOCKS], F32) for i in range(2)]

        e = Map(nc, under, end)
        e_raw = [e.put(f"e_raw{i}", [P, 3, D], F32) for i in range(2)]
        gu_hi = [e.put(f"gu_hi{i}", [P, KD, 2, FF], F32R) for i in range(2)]
        gu_lo = [e.put(f"gu_lo{i}", [P, KD, 2, FF], F32R) for i in range(2)]
        dn_hi = [e.put(f"dn_hi{i}", [P, D], F32R) for i in range(2)]
        dn_lo = [e.put(f"dn_lo{i}", [P, D], F32R) for i in range(2)]
        y_out = [e.put(f"y_out{i}", [P, D], F32) for i in range(2)]
        e = Map(nc, at0, under)
        xg = [e.put(f"xg{i}", [P, D], F32) for i in range(2)]
        xt_hi = [e.put(f"xt_hi{i}", [P, KD, P], F32R) for i in range(2)]
        xt_lo = [e.put(f"xt_lo{i}", [P, KD, P], F32R) for i in range(2)]
        hid = [e.put(f"hid{i}", [P, 3, FF], F32) for i in range(2)]
        hid_hi = [e.put(f"hid_hi{i}", [P, P], F32R) for i in range(2)]
        hid_lo = [e.put(f"hid_lo{i}", [P, P], F32R) for i in range(2)]

        ps = ctx.enter_context(nc.psum_tensor("ps", [P, 8, 512], F32))

        pre = {n: ctx.enter_context(nc.semaphore("pre_" + n)) for n in
               ("const", "vec", "tile0", "tile1", "tile2", "trans", "hi", "lo", "h_saved", "pad")}
        xg_in = [ctx.enter_context(nc.semaphore(f"xg_in{i}")) for i in range(2)]
        fy_in = [ctx.enter_context(nc.semaphore(f"fy_in{i}")) for i in range(3)]
        layer_sems = []

        def sem(name):
            s = ctx.enter_context(nc.semaphore(name))
            layer_sems.append(s)
            return s

        with nc.Block() as block:
            @block.sync
            def _(sp_):
                sp_.dma_start(cst[:], consts).then_inc(pre["const"], 16)
                sp_.dma_start(router[:], router_w.rearrange("(k p) e -> p k e", p=P)).then_inc(pre["const"], 16)
                sp_.dma_start(rbias[:], router_bias.rearrange("(a e) -> a e", a=1).to_broadcast([P, N_EXP])) \
                    .then_inc(pre["const"], 16)
                for n in range(TILES):
                    if n >= 3:
                        sp_.wait_ge(pre["trans"], 2 * (n - 3) + 2)
                        sp_.wait_ge(pre["h_saved"], 16 * (n - 2))
                    if n < XT:
                        sp_.dma_start(res[n % 3][:], x[0, n * P:(n + 1) * P, :]).then_inc(pre[f"tile{n % 3}"], 16)
                    else:
                        sp_.wait_ge(pre["pad"], 1)
                        sp_.dma_start(res[n % 3][0:N_META, :], meta_tokens).then_inc(pre[f"tile{n % 3}"], 16)
                    sp_.wait_ge(pre[f"tile{n % 3}"], 16 * (n // 3 + 1))
                    sp_.dma_start(h_dram[n * P:(n + 1) * P, :], res[n % 3][:]).then_inc(pre["h_saved"], 16)
                sp_.wait_ge(pre["h_saved"], 16 * TILES)

            @block.gpsimd
            def _(pool):
                pool.wait_ge(pre["trans"], 2 * (TILES - 4) + 2)
                pool.wait_ge(pre["h_saved"], 16 * (TILES - 3))
                pool.memset(res[XT % 3][:], 0.0).then_inc(pre["pad"], 1)

            @block.scalar
            def _(act):
                act.preload_act_table_set("natural_log_exp_and_others")
                for n in range(TILES):
                    for j in range(2):
                        act.wait_ge(pre["trans"], 2 * n + j + 1)
                        act.activation(act_hi[:, 4 * j:4 * j + 4, n * P:(n + 1) * P],
                                       ps[:, 2 * (n % 2) + j, :].rearrange("p (k t) -> p k t", k=4),
                                       ACT.Copy).then_inc(pre["hi"], 1)

            @block.vector
            def _(dve):
                dve.wait_ge(pre["const"], 48)
                dve.tensor_copy(suffix[:], C["suffix"]).then_inc(pre["vec"], 1)
                dve.tensor_copy(prefix[:], C["prefix"]).then_inc(pre["vec"], 1)
                dve.tensor_copy(ident_bf[:], C["ident"]).then_inc(pre["vec"], 1)
                dve.tensor_copy(negmask_bf[:], C["negmask"]).then_inc(pre["vec"], 1)
                for n in range(TILES):
                    for j in range(2):
                        dve.wait_ge(pre["hi"], 2 * n + j + 1)
                        dve.tensor_tensor(act_lo[:, 4 * j:4 * j + 4, n * P:(n + 1) * P],
                                          ps[:, 2 * (n % 2) + j, :].rearrange("p (k t) -> p k t", k=4),
                                          f32(act_hi[:, 4 * j:4 * j + 4, n * P:(n + 1) * P]),
                                          ALU.subtract).then_inc(pre["lo"], 1)

            @block.tensor
            def _(pe):
                pe.wait_ge(pre["const"], 48)
                for n in range(TILES):
                    pe.wait_ge(pre[f"tile{n % 3}"], 16 * (n // 3 + 1))
                    if n >= 2:
                        pe.wait_ge(pre["lo"], 2 * (n - 2) + 2)
                    for j in range(2):
                        for k in range(4):
                            last = pe.transpose(ps[:, 2 * (n % 2) + j, k * P:(k + 1) * P],
                                                res[n % 3][:, (4 * j + k) * P:(4 * j + k + 1) * P], C["ident"])
                        last.then_inc(pre["trans"], 1)


        pool_passed, dve_passed, pe_passed = sem("pool_passed"), sem("dve_passed"), sem("pe_passed")

        with nc.Fori(0, DEPTH) as layer:
            L = ds(layer, 1)

            w_loaded = [sem(f"w_loaded{i}") for i in range(3)]
            acc_taken = [sem(f"acc_taken{i}") for i in range(3)]
            w_hi_ready, w_lo_ready, acc_ready, conv_done, conv_link, taps_in = map(sem, (
                "w_hi_ready", "w_lo_ready", "acc_ready", "conv_done", "conv_link", "taps_in"))
            with nc.Block() as block:
                @block.sync
                def _(sp_):
                    sp_.dma_start(taps[:], conv_w[L].rearrange("a p (j t) -> p (a j) t", t=3)).then_inc(taps_in, 16)

                    def load(tile, r, col):
                        sp_.wait_ge(w_lo_ready, tile + 1)
                        sp_.dma_start(w_raw[r][:], w_in[L, :, ds(col, P)].rearrange(
                            "a (k p) c -> p (a k) c", p=P)).then_inc(w_loaded[r], 16)

                    with sp_.Fori(0, QKV_TILES // 3) as i:
                        for r in range(3):
                            load(3 * i + r, r, (3 * i + r) * P)
                    with sp_.Fori(0, CONV_TILES) as j:
                        for r in range(3):
                            load(QKV_TILES + 3 * j + r, r, CONV0 + r * CONV_W + j * P)

                @block.gpsimd
                def _(pool):
                    pool.sem_inc(w_lo_ready, 3)
                    with pool.Fori(0, (QKV_TILES + 3 * CONV_TILES) // 3) as i:
                        for r in range(3):
                            tile = 3 * i + r
                            wait_apart(pool, acc_ready, 3 * tile + 3, pool_passed)
                            wait_apart(pool, w_loaded[r], 16 * (i + 1), pool_passed)
                            pool.tensor_copy(w_hi[r][:], w_raw[r][:]).then_inc(w_hi_ready, 1)
                            pool.wait_ge(w_hi_ready, tile + 1)
                            pool.tensor_tensor(w_lo[r][:], w_raw[r][:], f32(w_hi[r][:]), ALU.subtract) \
                                .then_inc(w_lo_ready, 1)

                @block.tensor
                def _(pe):
                    pe.sem_inc(acc_ready, 9)
                    with pe.Fori(0, (QKV_TILES + 3 * CONV_TILES) // 3) as i:
                        for r in range(3):
                            tile = 3 * i + r
                            pe.wait_ge(w_lo_ready, 3 + tile + 1)
                            for n, (c0, c1) in enumerate(CHUNKS):
                                pe.wait_ge(acc_taken[n], tile + 1)
                                for k in range(KD):
                                    last = three_passes(pe, ps[:, n, 0:c1 - c0], w_hi[r][:, k, :],
                                                        w_lo[r][:, k, :], act_hi[:, k, c0:c1],
                                                        act_lo[:, k, c0:c1], k == 0, k == KD - 1)
                                last.then_inc(acc_ready, 1)

                @block.scalar
                def _(act):
                    for n in range(3):
                        act.sem_inc(acc_taken[n], 1)

                    def take(tile, n, dst):
                        act.wait_ge(acc_ready, 9 + 3 * tile + n + 1)
                        c0, c1 = CHUNKS[n]
                        act.activation(dst, ps[:, n, 0:c1 - c0], ACT.Copy).then_inc(acc_taken[n], 1)

                    with act.Fori(0, QKV_TILES // 3) as i:
                        for r in range(3):
                            for n, (c0, c1) in enumerate(CHUNKS):
                                take(3 * i + r, n, qkv[:, ds(3 * i + r, 1), c0:c1].rearrange("p a t -> p (a t)"))
                    with act.Fori(0, CONV_TILES) as j:
                        act.wait_ge(conv_done, j + 1)
                        for r, dst in enumerate((gate_b, gate_c)):
                            for n, (c0, c1) in enumerate(CHUNKS):
                                take(QKV_TILES + 3 * j + r, n, dst[:, c0:c1])

                @block.vector
                def _(dve):
                    dve.sem_inc(conv_done, 1)
                    dve.memset(conv_u[:, 0:2], 0.0).then_inc(conv_link, 1)
                    dve.wait_ge(conv_link, 1)
                    dve.wait_ge(taps_in, 16)
                    with dve.Fori(0, CONV_TILES) as j:
                        link = Link(dve, conv_link, 1 + 5 * j)
                        tile = QKV_TILES + 3 * j + 2
                        for n, (c0, c1) in enumerate(CHUNKS):
                            dve.wait_ge(acc_taken[n], tile + 1)
                            dve.wait_ge(acc_ready, 9 + 3 * tile + n + 1)
                            xs = min(c1, META0) - c0
                            if c1 > META0:
                                link(dve.tensor_tensor(conv_u[:, 2:2 + N_META], ps[:, n, xs:c1 - c0],
                                                       gate_c[:, META0:TOK], ALU.mult))
                            dve.tensor_tensor(conv_u[:, 2 + N_META + c0:2 + N_META + c0 + xs], ps[:, n, 0:xs],
                                              gate_c[:, c0:c0 + xs], ALU.mult).then_inc(acc_taken[n], 1)
                        dve.wait_ge(acc_taken[2], tile + 2)
                        tap = [taps[:, ds(j, 1), q:q + 1].rearrange("p a b -> p (a b)") for q in range(3)]
                        link(dve.tensor_scalar(conv_t[:], conv_u[:, 0:TOK], tap[0], None, ALU.mult))
                        for q in (1, 2):
                            link(dve.scalar_tensor_tensor(conv_t[:], conv_u[:, q:q + TOK], tap[q], conv_t[:],
                                                          ALU.mult, ALU.add))
                        y = conv_y[:, ds(j, 1), :].rearrange("p a t -> p (a t)")
                        dve.tensor_tensor(y[:, 0:SEQ], conv_t[:, N_META:TOK], gate_b[:, 0:SEQ], ALU.mult)
                        link(dve.tensor_tensor(y[:, META0:TOK], conv_t[:, 0:N_META], gate_b[:, META0:TOK], ALU.mult))
                        dve.sem_inc(conv_done, 1)

            v_trans, v_taken, q_hi_ready, q_lo_ready, k_pad = map(sem, (
                "v_trans", "v_taken", "q_hi_ready", "q_lo_ready", "k_pad"))
            z_ready, zs_ready, abs_ready, exp_ready, ln_ready = map(sem, (
                "z_ready", "zs_ready", "abs_ready", "exp_ready", "ln_ready"))
            sp_ready, sp_masked, sp_hi_ready, sp_lo_ready, tri_done = map(sem, (
                "sp_ready", "sp_masked", "sp_hi_ready", "sp_lo_ready", "tri_done"))
            tmp_ready, w_ready, w_masked, pv_done, o_taken = map(sem, (
                "tmp_ready", "w_ready", "w_masked", "pv_done", "o_taken"))
            S = len(SB_STEPS)
            DIAG = [n for n, s in enumerate(SB_STEPS) if s["diag"]]
            ENDS = [n for n, s in enumerate(SB_STEPS) if s["last"]]
            Z, SUM, OUT = 0, 2, 4

            def rows_of(s):
                return N_META if s["key"] == XT else P

            with nc.Block() as block:
                @block.tensor
                def _(pe):
                    for n in range(TILES):
                        rows = P if n < XT else N_META
                        if n >= 2:
                            pe.wait_ge(v_taken, n - 1)
                        for j in range(4):
                            tile = (SB_V, SB_V + 1, DF_V, DF_V + 1)[j]
                            last = pe.transpose(ps[0:rows, 6 + n % 2, j * P:(j + 1) * P],
                                                qkv[:, tile, n * P:n * P + rows], C["ident"])
                        last.then_inc(v_trans, 1)
                    pe.wait_ge(v_taken, TILES)
                    with pe.Fori(0, 2) as pr:
                        pe.wait_ge(q_lo_ready, pr + 1)

                        def scores(n):
                            s = SB_STEPS[n]
                            if n >= 2:
                                pe.wait_ge(zs_ready, pr * S + n - 1)
                            h0 = s["head"] * HD
                            key = slice(s["key"] * P, (s["key"] + 1) * P)
                            q = slice(s["tile0"] * P + s["lo"], s["tile0"] * P + s["hi"])
                            three_passes(pe, ps[:, Z + n % 2, s["lo"]:s["hi"]],
                                         k_hi[h0:h0 + HD, key], k_lo[h0:h0 + HD, key],
                                         q_hi[h0:h0 + HD, q], q_lo[h0:h0 + HD, q], True, True) \
                                .then_inc(z_ready, 1)

                        def sums(n):
                            s, bank = SB_STEPS[n], SUM + SB_STEPS[n]["head"]
                            if n >= 2:
                                pe.wait_ge(tmp_ready, pr * S + n - 1)
                            if not s["first"]:
                                b, r = SB_STEPS[n - 2], rows_of(SB_STEPS[n - 2])
                                for part in (sp_hi, sp_lo):
                                    pe.matmul(ps[:, bank, b["lo"]:b["hi"]], prefix[0:r, :],
                                              part[(n - 2) % 4][0:r, b["lo"]:b["hi"]],
                                              start=False, stop=True, skip_group_check=True)
                            pe.wait_ge(sp_lo_ready, pr * S + n + 1)
                            r = rows_of(s)
                            for j, part in enumerate((sp_hi, sp_lo)):
                                last = pe.matmul(ps[:, bank, s["lo"]:s["hi"]], suffix[0:r, :],
                                                 part[n % 4][0:r, s["lo"]:s["hi"]],
                                                 start=s["first"] and j == 0, stop=True, skip_group_check=True)
                            last.then_inc(tri_done, 1)

                        def weighted(n):
                            s, r = SB_STEPS[n], rows_of(SB_STEPS[n])
                            if s["diag"]:
                                pe.wait_ge(w_masked, pr * len(DIAG) + DIAG.index(n) + 1)
                            if s["first"] and n >= 2:
                                e_ = [x for x in ENDS if x < n and SB_STEPS[x]["head"] == s["head"]]
                                if e_:
                                    pe.wait_ge(o_taken, pr * len(ENDS) + ENDS.index(e_[-1]) + 1)
                            if s["key"] == XT:
                                wait_apart(pe, w_ready, pr * S + n + 1, pe_passed)
                            else:
                                pe.wait_ge(w_ready, pr * S + n + 1)
                            for t0 in range(s["lo"], s["hi"], P):
                                v = v_rows[0:r, s["key"], ds(pr * P + s["head"] * HD, HD)]
                                last = pe.matmul(ps[:, OUT + s["head"], t0 // 2:t0 // 2 + HD],
                                                 wt[n % 4][0:r, t0:t0 + P], v,
                                                 start=s["first"] and t0 == s["lo"], stop=True,
                                                 skip_group_check=True)
                            last.then_inc(pv_done, 1)

                        for n in range(S + 4):
                            if n < S:
                                scores(n)
                            if 0 <= n - 2 < S:
                                sums(n - 2)
                            if 0 <= n - 4 < S:
                                weighted(n - 4)

                @block.scalar
                def _(act):
                    for n in range(TILES):
                        rows = P if n < XT else N_META
                        act.wait_ge(v_trans, n + 1)
                        act.activation(v_rows[0:rows, n, :], ps[0:rows, 6 + n % 2, :], ACT.Copy).then_inc(v_taken, 1)
                    with act.Fori(0, 2) as pr:
                        act.wait_ge(pv_done, pr * S + 1)
                        act.activation(q_hi[:, 0:TOK], qkv[:, ds(SB_Q + pr, 1), :].rearrange("p a t -> p (a t)"),
                                       ACT.Copy, scale=SB_SCALE).then_inc(q_hi_ready, 1)
                        act.activation(k_hi[:, 0:TOK], qkv[:, ds(SB_K + pr, 1), :].rearrange("p a t -> p (a t)"),
                                       ACT.Copy).then_inc(q_hi_ready, 1)

                        def part(buf, n):
                            s = SB_STEPS[n]
                            return buf[0:rows_of(s), s["lo"]:s["hi"]]

                        for n in range(S + 3):
                            if n < S:
                                s = SB_STEPS[n]
                                if n >= 4:
                                    act.wait_ge(tmp_ready, pr * S + n - 3)
                                act.wait_ge(z_ready, pr * S + n + 1)
                                act.activation(part(zs[n % 4], n), ps[0:rows_of(s), Z + n % 2, s["lo"]:s["hi"]],
                                               ACT.Copy).then_inc(zs_ready, 1)
                            if 0 <= n - 1 < S:
                                b = n - 1
                                act.wait_ge(abs_ready, pr * S + b + 1)
                                act.activation(part(ez[b % 2], b), part(ez[b % 2], b), ACT.Exp, scale=-1.0) \
                                    .then_inc(exp_ready, 1)
                            if 0 <= n - 3 < S:
                                b = n - 3
                                act.wait_ge(tmp_ready, pr * S + b + 1)
                                act.activation(part(wt[b % 4], b), part(wt[b % 4], b), ACT.Exp).then_inc(w_ready, 1)
                            if 0 <= n - 1 < S:
                                b = n - 1
                                act.wait_ge(exp_ready, pr * S + b + 1)
                                act.activation(part(ez[b % 2], b), part(ez[b % 2], b), ACT.Ln, bias=1.0) \
                                    .then_inc(ln_ready, 1)

                @block.gpsimd
                def _(pool):
                    pool.memset(f32(q_hi[:, TOK:ROWS]), 0.0)
                    pool.memset(f32(q_lo[:, TOK:ROWS]), 0.0)
                    pool.memset(f32(k_hi[:, TOK:ROWS]), 0.0)
                    pool.memset(f32(k_lo[:, TOK:ROWS]), 0.0).then_inc(k_pad, 1)
                    pool.sem_inc(tri_done, 4)
                    with pool.Fori(0, 2) as pr:
                        def low_triangle(buf, n, sem_in, sem_out):
                            r, lo = rows_of(SB_STEPS[n]), SB_STEPS[n]["lo"]
                            wait_apart(pool, sem_in, pr * S + n + 1, pool_passed)
                            part = buf[0:r, lo:lo + P]
                            pool.affine_select(out=part, in_=part, pattern=[[1, P]], compare_op=ALU.is_gt,
                                               fill=0.0, base=0, channel_multiplier=-1).then_inc(sem_out, 1)

                        for n in range(S + 3):
                            if 0 <= n - 1 < S:
                                b = n - 1
                                s, r = SB_STEPS[b], rows_of(SB_STEPS[b])
                                if s["diag"]:
                                    low_triangle(sp[b % 2], b, sp_ready, sp_masked)
                                    wait_apart(pool, sp_masked, pr * len(DIAG) + DIAG.index(b) + 1, pool_passed)
                                wait_apart(pool, sp_ready, pr * S + b + 1, pool_passed)
                                wait_apart(pool, tri_done, pr * S + b - 1 + 4 if b >= 4 else pr * S + 4, pool_passed)
                                pool.tensor_copy(sp_hi[b % 4][0:r, s["lo"]:s["hi"]], sp[b % 2][0:r, s["lo"]:s["hi"]]) \
                                    .then_inc(sp_hi_ready, 1)
                            if 0 <= n - 3 < S and SB_STEPS[n - 3]["diag"]:
                                low_triangle(wt[(n - 3) % 4], n - 3, w_ready, w_masked)

                @block.vector
                def _(dve):
                    dve.sem_inc(pv_done, 1)
                    dve.wait_ge(k_pad, 1)
                    with dve.Fori(0, 2) as pr:
                        dve.wait_ge(q_hi_ready, 2 * pr + 2)
                        dve.scalar_tensor_tensor(q_lo[:, 0:TOK], qkv[:, ds(SB_Q + pr, 1), :].rearrange("p a t -> p (a t)"),
                                                 SB_SCALE, f32(q_hi[:, 0:TOK]), ALU.mult, ALU.subtract)
                        dve.tensor_tensor(k_lo[:, 0:TOK], qkv[:, ds(SB_K + pr, 1), :].rearrange("p a t -> p (a t)"),
                                          f32(k_hi[:, 0:TOK]), ALU.subtract).then_inc(q_lo_ready, 1)

                        def part(buf, n):
                            s = SB_STEPS[n]
                            return buf[0:rows_of(s), s["lo"]:s["hi"]]

                        def take_out(n):
                            s = SB_STEPS[n]
                            tiles = (s["hi"] - s["lo"]) // P
                            dve.wait_ge(pv_done, pr * S + n + 2)
                            dve.tensor_copy(y_sb[:, s["tile0"]:s["tile0"] + tiles, ds(pr * P + s["head"] * HD, HD)],
                                            ps[:, OUT + s["head"], 0:tiles * HD].rearrange("p (t c) -> p t c", c=HD)) \
                                .then_inc(o_taken, 1)

                        for n in range(S + 5):
                            if n < S:
                                if n >= 2:
                                    dve.wait_ge(sp_ready, pr * S + n - 1)
                                dve.wait_ge(zs_ready, pr * S + n + 1)
                                dve.tensor_scalar(part(ez[n % 2], n).bitcast(U32), part(zs[n % 4], n).bitcast(U32),
                                                  0x7FFFFFFF, None, ALU.bitwise_and) \
                                    .then_inc(abs_ready, 1)
                            if 0 <= n - 3 < S:
                                b = n - 3
                                s = SB_STEPS[b]
                                dve.wait_ge(tri_done, pr * S + b + 1 + 4)
                                if b >= 4:
                                    dve.wait_ge(pv_done, pr * S + b - 3 + 1)
                                dve.tensor_tensor(part(wt[b % 4], b), part(zs[b % 4], b),
                                                  ps[0:rows_of(s), SUM + s["head"], s["lo"]:s["hi"]],
                                                  ALU.subtract).then_inc(tmp_ready, 1)
                            if 0 <= n - 2 < S:
                                b = n - 2
                                dve.wait_ge(sp_hi_ready, pr * S + b + 1)
                                dve.tensor_tensor(part(sp_lo[b % 4], b), part(sp[b % 2], b),
                                                  f32(part(sp_hi[b % 4], b)), ALU.subtract).then_inc(sp_lo_ready, 1)
                            if 0 <= n - 1 < S:
                                b = n - 1
                                if b >= 2:
                                    dve.wait_ge(sp_lo_ready, pr * S + b - 1)
                                dve.wait_ge(ln_ready, pr * S + b + 1)
                                dve.scalar_tensor_tensor(part(sp[b % 2], b), part(zs[b % 4], b), 0.0,
                                                         part(ez[b % 2], b), ALU.max, ALU.add).then_inc(sp_ready, 1)
                            if n - 5 in ENDS:
                                take_out(n - 5)

            (df_loaded, df_link, lam_sum, lam_exp, rot_ready, rot_taken, rot_cos, rot_sum, dq_hi, dq_lo) = map(sem, (
                "df_loaded", "df_link", "lam_sum", "lam_exp", "rot_ready", "rot_taken", "rot_cos", "rot_sum",
                "dq_hi", "dq_lo"))
            s_ready = [sem(f"s_ready{i}") for i in range(2)]
            m_ready = [sem(f"m_ready{i}") for i in range(2)]
            p_ready = [sem(f"p_ready{i}") for i in range(2)]
            a_ready, at_ready, at_taken, dpv_done, df_o_taken = map(sem, (
                "a_ready", "at_ready", "at_taken", "dpv_done", "df_o_taken"))
            UNITS = [(i, hh) for i in DIFF_ROWS for hh in range(2)]
            U = len(UNITS)
            GROUPS = [-(-len(key_tiles(i)) // 4) for i, _ in UNITS]
            G0 = [sum(GROUPS[:u]) for u in range(U + 1)]
            AT_BANK, DO_BANK = 6, 7

            with nc.Block() as block:
                @block.sync
                def _(sp_):
                    for n, v in enumerate((lambda_q1, lambda_k1, lambda_q2, lambda_k2)):
                        sp_.dma_start(lam_in[:, n, :], v[L].to_broadcast([P, SUB])).then_inc(df_loaded, 16)
                    sp_.dma_start(lam[:, 4:6], lam_consts[L].to_broadcast([P, 2])).then_inc(df_loaded, 16)
                    sp_.dma_start(norm_g[:], diff_norm_g[L].to_broadcast([P, HD])).then_inc(df_loaded, 16)
                    sp_.dma_start(cos_t[:], rope[0]).then_inc(df_loaded, 16)
                    sp_.dma_start(sin_t[:], rope[1]).then_inc(df_loaded, 16)

                @block.tensor
                def _(pe):
                    with pe.Fori(0, 2) as pr:
                        for j, first in enumerate((DF_Q, DF_K)):
                            for n, (c0, c1) in enumerate(CHUNKS):
                                last = pe.matmul(ps[:, 3 * j + n, 0:c1 - c0], C["rotate"],
                                                 qkv[:, ds(first + pr, 1), c0:c1].rearrange("p a t -> p (a t)"),
                                                 start=True, stop=True)
                            last.then_inc(rot_ready, 1)
                        pe.wait_ge(dq_lo, 2 * pr + 2)

                        def scores(u, s):
                            i, hh = UNITS[u]
                            pieces, w = row_pieces(i)
                            if u >= 1:
                                pe.wait_ge(p_ready[s], pr * U + u)
                            r0 = hh * HD + s * SUB
                            mask0 = N_META + i * P if i < XT else 0
                            for n in range(pieces):
                                bank = 3 * s + n
                                a0, a1 = max(mask0, n * w), (n + 1) * w
                                last = three_passes(pe, ps[:, bank, 0:w],
                                                    q_hi[r0:r0 + SUB, i * P:(i + 1) * P],
                                                    q_lo[r0:r0 + SUB, i * P:(i + 1) * P],
                                                    k_hi[r0:r0 + SUB, n * w:(n + 1) * w],
                                                    k_lo[r0:r0 + SUB, n * w:(n + 1) * w], True, True)
                                if a0 < a1:
                                    last = pe.matmul(ps[:, bank, a0 - n * w:a1 - n * w], ident_bf[:],
                                                     negmask_bf[:, a0 - mask0:a1 - mask0],
                                                     start=False, stop=True, skip_group_check=True)
                            last.then_inc(s_ready[s], 1)

                        def weighted(u):
                            i, hh = UNITS[u]
                            tiles = key_tiles(i)
                            pe.wait_ge(a_ready, pr * U + u + 1)
                            for g in range(GROUPS[u]):
                                if G0[u] + g >= 1:
                                    pe.wait_ge(at_taken, pr * G0[U] + G0[u] + g)
                                for j, (_, k0, nk) in enumerate(tiles[4 * g:4 * g + 4]):
                                    last = pe.transpose(ps[0:nk, AT_BANK, j * P:(j + 1) * P],
                                                        prob[u % 2][0][:, k0:k0 + nk], C["ident"])
                                last.then_inc(at_ready, 1)
                            if u >= 1:
                                pe.wait_ge(df_o_taken, pr * U + u)
                            wait_apart(pe, at_taken, pr * G0[U] + G0[u + 1], pe_passed)
                            for j, (vt, _, nk) in enumerate(tiles):
                                last = pe.matmul(ps[:, DO_BANK, 0:HD], a_t[u % 2][0:nk, j, :],
                                                 v_rows[0:nk, vt, ds(256 + pr * P + hh * HD, HD)],
                                                 start=j == 0, stop=j == len(tiles) - 1)
                            last.then_inc(dpv_done, 1)

                        for u in range(U + 1):
                            if u < U:
                                scores(u, 0)
                                scores(u, 1)
                            if u >= 1:
                                weighted(u - 1)

                @block.scalar
                def _(act):
                    act.wait_ge(lam_sum, 1)
                    act.activation(lam[:, 2:4], lam[:, 0:2], ACT.Exp).then_inc(lam_exp, 1)
                    with act.Fori(0, 2) as pr:
                        act.wait_ge(rot_sum, 2 * pr + 1)
                        act.activation(q_hi[:, 0:TOK], rot_a[:], ACT.Copy).then_inc(dq_hi, 1)
                        act.wait_ge(rot_sum, 2 * pr + 2)
                        act.activation(k_hi[:, 0:N_META], rot_a[:, META0:TOK], ACT.Copy)
                        act.activation(k_hi[:, N_META:TOK], rot_a[:, 0:SEQ], ACT.Copy).then_inc(dq_hi, 1)

                        def exps(u, s):
                            pieces, w = row_pieces(UNITS[u][0])
                            if u >= 2:
                                act.wait_ge(at_ready, pr * G0[U] + G0[u - 1])
                            act.wait_ge(m_ready[s], pr * U + u + 1)
                            st = df_stat[u % 2]
                            act.activation(prob[u % 2][s][:, 0:pieces * w].rearrange("p (n w) -> p n w", w=w),
                                           ps[:, 3 * s:3 * s + pieces, 0:w], ACT.Exp, bias=st[:, 2 + s:3 + s],
                                           scale=DF_SCALE, accum_out=st[:, 4 + s:5 + s]).then_inc(p_ready[s], 1)

                        for u in range(U + 1):
                            if u < U:
                                exps(u, 0)
                                exps(u, 1)
                            if u >= 1:
                                b_ = u - 1
                                nt = len(key_tiles(UNITS[b_][0]))
                                for g in range(GROUPS[b_]):
                                    n = min(4, nt - 4 * g)
                                    if b_ >= 2:
                                        act.wait_ge(dpv_done, pr * U + b_ - 1)
                                    act.wait_ge(at_ready, pr * G0[U] + G0[b_] + g + 1)
                                    act.activation(a_t[b_ % 2][:, 4 * g:4 * g + n, :],
                                                   ps[:, AT_BANK, 0:n * P].rearrange("p (n k) -> p n k", k=P),
                                                   ACT.Copy).then_inc(at_taken, 1)

                @block.gpsimd
                def _(pool):
                    pool.wait_ge(df_loaded, 16 * 8)
                    with pool.Fori(0, 2) as pr:
                        for j, first in enumerate((DF_Q, DF_K)):
                            wait_apart(pool, rot_taken, 2 * pr + j + 1, pool_passed)
                            pool.tensor_tensor(rot_b[:], qkv[:, ds(first + pr, 1), :].rearrange("p a t -> p (a t)"),
                                               cos_t[:], ALU.mult).then_inc(rot_cos, 1)

                @block.vector
                def _(dve):
                    dve.wait_ge(df_loaded, 16 * 8)
                    dve.sem_inc(rot_taken, 1)
                    link = Link(dve, df_link)
                    for n in (0, 2):
                        link(dve.tensor_tensor(lam_in[:, n, :], lam_in[:, n, :], lam_in[:, n + 1, :], ALU.mult))
                    dve.tensor_reduce(lam[:, 0:2], lam_in[:, 0:4:2, :], AX, ALU.add).then_inc(lam_sum, 1)
                    dve.wait_ge(lam_exp, 1)
                    link(dve.tensor_tensor(lam[:, 6:7], lam[:, 2:3], lam[:, 3:4], ALU.subtract))
                    link(dve.tensor_tensor(lam[:, 6:7], lam[:, 6:7], lam[:, 4:5], ALU.add))
                    link(dve.tensor_scalar(norm_g[:], norm_g[:], lam[:, 5:6], None, ALU.mult))
                    with dve.Fori(0, 2) as pr:
                        LINKS = 2 * 3 + U * 5
                        link = Link(dve, df_link, 5 + pr * LINKS)
                        for j in range(2):
                            dve.wait_ge(rot_ready, 2 * pr + j + 1)
                            for n, (c0, c1) in enumerate(CHUNKS):
                                link(dve.tensor_tensor(rot_a[:, c0:c1], ps[:, 3 * j + n, 0:c1 - c0], sin_t[:, c0:c1],
                                                       ALU.mult))
                            dve.wait_ge(rot_cos, 2 * pr + j + 1)
                            dve.tensor_tensor(rot_a[:], rot_b[:], rot_a[:], ALU.add).then_inc(rot_sum, 1)
                            dve.wait_ge(dq_hi, 2 * pr + j + 1)
                            if j == 0:
                                dve.tensor_tensor(q_lo[:, 0:TOK], rot_a[:], f32(q_hi[:, 0:TOK]), ALU.subtract) \
                                    .then_inc(dq_lo, 1)
                            else:
                                dve.tensor_tensor(k_lo[:, 0:N_META], rot_a[:, META0:TOK], f32(k_hi[:, 0:N_META]),
                                                  ALU.subtract)
                                dve.tensor_tensor(k_lo[:, N_META:TOK], rot_a[:, 0:SEQ], f32(k_hi[:, N_META:TOK]),
                                                  ALU.subtract).then_inc(dq_lo, 1)
                            dve.wait_ge(dq_lo, 2 * pr + j + 1)
                            dve.sem_inc(rot_taken, 1)

                        def maxima(u, s):
                            pieces, w = row_pieces(UNITS[u][0])
                            st = df_stat[u % 2]
                            dve.wait_ge(s_ready[s], pr * U + u + 1)
                            link(dve.tensor_reduce(st[:, s:s + 1], ps[:, 3 * s:3 * s + pieces, 0:w],
                                                   mybir.AxisListType.XY, ALU.max))
                            dve.tensor_scalar(st[:, 2 + s:3 + s], st[:, s:s + 1], -DF_SCALE, None, ALU.mult) \
                                .then_inc(m_ready[s], 1)

                        def difference(u):
                            pieces, w = row_pieces(UNITS[u][0])
                            st, (p0, p1) = df_stat[u % 2], [x[:, 0:pieces * w] for x in prob[u % 2]]
                            for s in range(2):
                                dve.wait_ge(p_ready[s], pr * U + u + 1)
                            link(dve.reciprocal(st[:, 6:8], st[:, 4:6]))
                            link(dve.tensor_tensor(st[:, 8:9], st[:, 7:8], lam[:, 6:7], ALU.mult))
                            link(dve.tensor_scalar(p1, p1, st[:, 8:9], None, ALU.mult))
                            dve.scalar_tensor_tensor(p0, p0, st[:, 6:7], p1, ALU.mult, ALU.subtract) \
                                .then_inc(a_ready, 1)

                        for u in range(U + 1):
                            if u < U:
                                maxima(u, 0)
                                maxima(u, 1)
                                difference(u)
                            if u >= 1:
                                i, hh = UNITS[u - 1]
                                dve.wait_ge(dpv_done, pr * U + u)
                                dve.tensor_copy(y_df[:, i, ds(pr * P + hh * HD, HD)], ps[:, DO_BANK, 0:HD]) \
                                    .then_inc(df_o_taken, 1)
                        assert link.n == LINKS, (link.n, LINKS)

            mix_link, mix_var, mix_rms, mix_normed, mix_trans, mix_hi, mix_lo, conv_hi, mix_pad = map(sem, (
                "mix_link", "mix_var", "mix_rms", "mix_normed", "mix_trans", "mix_hi", "mix_lo", "conv_hi", "mix_pad"))
            y_heads = y_df[:].rearrange("p t (h c) -> p (t h) c", c=HD)
            with nc.Block() as block:
                @block.gpsimd
                def _(pool):
                    pool.memset(f32(act_hi[:, :, TOK:ROWS]), 0.0)
                    pool.memset(f32(act_lo[:, :, TOK:ROWS]), 0.0).then_inc(mix_pad, 1)
                    pool.wait_ge(mix_var, 1)
                    pool.tensor_tensor(rms[:], ms[:], C["half"].to_broadcast([P, TILES * 4]), ALU.pow) \
                        .then_inc(mix_rms, 1)
                    pool.wait_ge(mix_pad, 1)

                @block.tensor
                def _(pe):
                    pe.wait_ge(mix_normed, 1)
                    for n in range(TILES):
                        rows = P if n < XT else N_META
                        if n >= 2:
                            pe.wait_ge(mix_lo, n - 1)
                        for j in range(4):
                            src = (y_sb, y_sb, y_df, y_df)[j]
                            last = pe.transpose(ps[:, n % 2, j * P:j * P + rows],
                                                src[0:rows, n, (j % 2) * P:(j % 2 + 1) * P], C["ident"][0:rows, 0:rows])
                        last.then_inc(mix_trans, 1)

                @block.scalar
                def _(act):
                    for j in range(CONV_TILES):
                        act.activation(act_hi[:, 4 + j, 0:TOK], conv_y[:, j, :], ACT.Copy).then_inc(conv_hi, 1)
                    for n in range(TILES):
                        rows = P if n < XT else N_META
                        act.wait_ge(mix_trans, n + 1)
                        act.activation(act_hi[:, 0:4, n * P:n * P + rows],
                                       ps[:, n % 2, :].rearrange("p (k t) -> p k t", k=4)[:, :, 0:rows],
                                       ACT.Copy).then_inc(mix_hi, 1)

                @block.vector
                def _(dve):
                    link = Link(dve, mix_link)
                    link(dve.tensor_tensor(sq[:], y_heads, y_heads, ALU.mult))
                    link(dve.tensor_reduce(ms[:], sq[:], AX, ALU.add))
                    dve.tensor_scalar(ms[:], ms[:], 1.0 / HD, EPS, ALU.mult, ALU.add).then_inc(mix_var, 1)
                    dve.wait_ge(mix_rms, 1)
                    link(dve.tensor_tensor(y_heads, y_heads, rms[:].unsqueeze(2).to_broadcast([P, TILES * 4, HD]),
                                           ALU.mult))
                    dve.tensor_tensor(y_heads, y_heads, norm_g[:].unsqueeze(1).to_broadcast([P, TILES * 4, HD]),
                                      ALU.mult).then_inc(mix_normed, 1)
                    for j in range(CONV_TILES):
                        dve.wait_ge(conv_hi, j + 1)
                        dve.tensor_tensor(act_lo[:, 4 + j, 0:TOK], conv_y[:, j, :], f32(act_hi[:, 4 + j, 0:TOK]),
                                          ALU.subtract)
                    for n in range(TILES):
                        rows = P if n < XT else N_META
                        dve.wait_ge(mix_hi, n + 1)
                        dve.tensor_tensor(act_lo[:, 0:4, n * P:n * P + rows],
                                          ps[:, n % 2, :].rearrange("p (k t) -> p k t", k=4)[:, :, 0:rows],
                                          f32(act_hi[:, 0:4, n * P:n * P + rows]), ALU.subtract).then_inc(mix_lo, 1)

            wo_loaded = [sem(f"wo_loaded{i}") for i in range(2)]
            res_in = [sem(f"res_in{i}") for i in range(3)]
            h1_saved = [sem(f"h1_saved{i}") for i in range(3)]
            (wo_hi_ready, wo_lo_ready, ln_in, mix_ready, res_ready, ln_link, var_ready, rstd_ready, scaled, normed,
             h1_trans, h1_taken, lg_ready, lg_taken) = map(sem, (
                 "wo_hi_ready", "wo_lo_ready", "ln_in", "mix_ready", "res_ready", "ln_link", "var_ready",
                 "rstd_ready", "scaled", "normed", "h1_trans", "h1_taken", "lg_ready", "lg_taken"))
            T_BANK, LG_BANK = 6, 7

            def norm_statistics(dve, link, rows_in, st, var_sem):
                link(dve.bn_stats(st[:, 0:6], rows_in[:, 0:512]))
                link(dve.bn_stats(st[:, 6:12], rows_in[:, 512:1024]))
                dve.sem_inc(dve_passed, 1)
                link(dve.bn_aggr(st[:, 12:14], st[:, 0:12]))
                dve.tensor_scalar(st[:, 14:15], st[:, 13:14], EPS, None, ALU.add).then_inc(var_sem, 1)

            with nc.Block() as block:
                @block.sync
                def _(sp_):
                    with sp_.Fori(0, KD // 2) as i:
                        for r in range(2):
                            sp_.wait_ge(wo_lo_ready, 2 * i + r + 1)
                            sp_.dma_start(wo_raw[r][:], w_out[L, ds((2 * i + r) * P, P), :].rearrange(
                                "a p n -> p (a n)")).then_inc(wo_loaded[r], 16)
                    sp_.dma_start(ln_g[:], ln1_g[L].to_broadcast([P, D])).then_inc(ln_in, 16)
                    sp_.dma_start(ln_b[:], ln1_b[L].to_broadcast([P, D])).then_inc(ln_in, 16)
                    with sp_.Fori(0, TILES // 3) as i:
                        for r in range(3):
                            n = 3 * i + r
                            sp_.wait_ge(scaled, n + 1)
                            sp_.dma_start(res[r][:], h_dram[ds(n * P, P), :]).then_inc(res_in[r], 16)

                @block.gpsimd
                def _(pool):
                    pool.wait_ge(ln_in, 32)
                    with pool.Fori(0, TILES // 3) as i:
                        for r in range(3):
                            n = 3 * i + r
                            pool.wait_ge(var_ready, n + 1)
                            pool.tensor_tensor(stat[:, r, 15:16], stat[:, r, 14:15], C["half"], ALU.pow) \
                                .then_inc(rstd_ready, 1)
                            pool.wait_ge(scaled, 3 + n + 1)
                            pool.tensor_tensor(nrm[r][:], nrm[r][:], ln_b[:], ALU.add).then_inc(normed, 1)

                @block.tensor
                def _(pe):
                    pe.sem_inc(h1_trans, 6)

                    def project(n):
                        for half in range(2):
                            bank = 2 * (n % 3) + half
                            if half == 0 and n >= 3:
                                pe.wait_ge(res_ready, n - 2)
                            for k in range(KD):
                                if n == 0 and half == 0:
                                    pe.wait_ge(wo_lo_ready, 2 + k + 1)
                                cols = slice(512 * half, 512 * half + 512)
                                rows = slice(n * P, (n + 1) * P)
                                last = three_passes(pe, ps[:, bank, :], act_hi[:, k, rows], act_lo[:, k, rows],
                                                    wo_hi[:, k, cols], wo_lo[:, k, cols], k == 0, k == KD - 1)
                        last.then_inc(mix_ready, 1)

                    def route(n):
                        pe.wait_ge(normed, n + 1)
                        for j in range(2):
                            if 2 * n + j >= 1:
                                pe.wait_ge(h1_taken, 2 * n + j)
                            for k in range(4):
                                kk = 4 * j + k
                                last = pe.transpose(ps[:, T_BANK, k * P:(k + 1) * P],
                                                    nrm[n % 3][:, kk * P:(kk + 1) * P], C["ident"])
                            last.then_inc(h1_trans, 1)
                        if n >= 1:
                            pe.wait_ge(lg_taken, n)
                        pe.wait_ge(h1_taken, 2 * n + 2)
                        for k in range(KD):
                            last = pe.matmul(ps[:, LG_BANK, 0:N_EXP], h1_t[:, k, :], router[:, k, :],
                                             start=k == 0, stop=k == KD - 1)
                        last.then_inc(lg_ready, 1)

                    for n in range(TILES + 1):
                        if n < TILES:
                            project(n)
                        if n >= 1:
                            route(n - 1)

                @block.scalar
                def _(act):
                    with act.Fori(0, KD // 2) as i:
                        for r in range(2):
                            act.wait_ge(wo_loaded[r], 16 * (i + 1))
                            act.activation(wo_hi[:, ds(2 * i + r, 1), :].rearrange("p a n -> p (a n)"), wo_raw[r][:],
                                           ACT.Copy).then_inc(wo_hi_ready, 1)
                    for r in range(3):
                        act.sem_inc(h1_saved[r], 16)
                    with act.Fori(0, TILES // 3) as i:
                        for r in range(3):
                            n = 3 * i + r
                            for j in range(2):
                                act.wait_ge(h1_trans, 6 + 2 * n + j + 1)
                                act.activation(h1_t[:, 4 * j:4 * j + 4, :],
                                               ps[:, T_BANK, :].rearrange("p (k t) -> p k t", k=4), ACT.Copy) \
                                    .then_inc(h1_taken, 1)
                            act.dma_start(h1_dram[ds(n * P, P), :], nrm[r][:]).then_inc(h1_saved[r], 16)
                            act.wait_ge(lg_ready, n + 1)
                            act.activation(logits[:, ds(n, 1), :].rearrange("p a e -> p (a e)"),
                                           ps[:, LG_BANK, 0:N_EXP], ACT.Copy).then_inc(lg_taken, 1)
                    for r in range(3):
                        act.wait_ge(h1_saved[r], 16 + 16 * TILES // 3)
                    act.wait_ge(lg_taken, TILES)

                @block.vector
                def _(dve):
                    dve.sem_inc(wo_lo_ready, 2)
                    dve.sem_inc(scaled, 3)
                    with dve.Fori(0, KD // 2) as i:
                        for r in range(2):
                            dve.wait_ge(wo_hi_ready, 2 * i + r + 1)
                            k = ds(2 * i + r, 1)
                            dve.tensor_tensor(wo_lo[:, k, :].rearrange("p a n -> p (a n)"), wo_raw[r][:],
                                              f32(wo_hi[:, k, :]).rearrange("p a n -> p (a n)"), ALU.subtract) \
                                .then_inc(wo_lo_ready, 1)
                    dve.wait_ge(ln_in, 32)

                    def norm_tile(n, r, link, link_base):
                        dve.wait_ge(res_in[r], 16 * (link_base + 1))
                        dve.wait_ge(mix_ready, n + 1)
                        dve.scalar_tensor_tensor(res[r][:, 0:512], res[r][:, 0:512], ALPHA, ps[:, 2 * r, :],
                                                 ALU.mult, ALU.add)
                        dve.scalar_tensor_tensor(res[r][:, 512:1024], res[r][:, 512:1024], ALPHA, ps[:, 2 * r + 1, :],
                                                 ALU.mult, ALU.add).then_inc(res_ready, 1)
                        dve.wait_ge(res_ready, n + 1)
                        norm_statistics(dve, link, res[r], stat[:, r, :], var_ready)
                        dve.wait_ge(rstd_ready, n + 1)

                    with dve.Fori(0, TILES // 3) as i:
                        link = Link(dve, ln_link, 12 * i)
                        for r in range(3):
                            n = 3 * i + r
                            norm_tile(n, r, link, i)
                            dve.wait_ge(h1_saved[r], 16 * i + 16)
                            dve.wait_ge(h1_trans, 2 * n + 2)
                            link(dve.tensor_scalar(nrm[r][:], res[r][:], stat[:, r, 12:13], stat[:, r, 15:16],
                                                   ALU.subtract, ALU.mult))
                            dve.tensor_tensor(nrm[r][:], nrm[r][:], ln_g[:], ALU.mult).then_inc(scaled, 1)

            rt_link, rt_shifted, rt_exp, rt_member, rt_counts, rt_places, rt_maps = map(sem, (
                "rt_link", "rt_shifted", "rt_exp", "rt_member", "rt_counts", "rt_places", "rt_maps"))

            with nc.Block() as block:
                @block.scalar
                def _(act):
                    act.wait_ge(rt_shifted, 1)
                    act.activation(prb[:], sel[:], ACT.Exp).then_inc(rt_exp, 1)

                @block.tensor
                def _(pe):
                    pe.wait_ge(rt_member, 1)
                    pe.matmul(ps[:, 0, 0:TILES * N_EXP], C["prefix"], member[:], start=True, stop=True)
                    pe.matmul(ps[:, 1, 0:TILES * N_EXP], C["ones"], member[:], start=True, stop=True) \
                        .then_inc(rt_counts, 1)
                    pe.wait_ge(rt_places, 1)
                    for k in range(2):
                        for n in range(TILES):
                            last = pe.matmul(ps[:, 2, 0:2 * BLOCKS], at_pos[k][:, n, :], at_blk[k][:, n, :, :],
                                             start=k == 0 and n == 0, stop=k == 1 and n == TILES - 1)
                    last.then_inc(rt_maps, 1)

                @block.vector
                def _(dve):
                    link = Link(dve, rt_link)
                    tt, red = dve.tensor_tensor, dve.tensor_reduce
                    wide = [P, TILES, N_EXP]
                    col = [small[:, n, :, 0] for n in range(16)]
                    grp = lambda n: small[:, n, :, :]

                    def over(ap, shape):
                        return ap.unsqueeze(2).to_broadcast(shape)

                    def first_max(vals, prio, n, out_oh, c0, c1):
                        shape = [P, TILES, n]
                        link(red(col[c0], vals, AX, ALU.max))
                        link(tt(out_oh, vals, over(col[c0], shape), ALU.is_ge))
                        link(tt(out_oh, out_oh, prio.unsqueeze(1).to_broadcast(shape), ALU.mult))
                        link(red(col[c1], out_oh, AX, ALU.max))
                        link(tt(out_oh, out_oh, over(col[c1], shape), ALU.is_equal))

                    link(red(col[0], logits[:], AX, ALU.max))
                    tt(sel[:], logits[:], over(col[0], wide), ALU.subtract).then_inc(rt_shifted, 1)
                    dve.wait_ge(rt_exp, 1)
                    link(red(col[0], prb[:], AX, ALU.add))
                    link(dve.reciprocal(col[1], col[0]))
                    link(tt(prb[:], prb[:], over(col[1], wide), ALU.mult))
                    link(tt(sel[:], prb[:], rbias[:].unsqueeze(1).to_broadcast(wide), ALU.add))
                    g4 = sel[:].rearrange("p t (g e) -> p (t g) e", e=4)
                    tt(pair[:, :, 0:2], g4[:, :, 0:2], g4[:, :, 2:4], ALU.add)
                    tt(pair[:, :, 2:4], g4[:, :, 0:4:2], g4[:, :, 1:4:2], ALU.add)
                    tt(pair[:, :, 4:5], g4[:, :, 0:1], g4[:, :, 3:4], ALU.add)
                    link(tt(pair[:, :, 5:6], g4[:, :, 1:2], g4[:, :, 2:3], ALU.add))
                    link(red(grp(14).rearrange("p t g -> p (t g)"), pair[:], AX, ALU.max))
                    first_max(grp(14), C["prio4"], N_GRP, grp(15), 2, 3)
                    pen = grp(14).rearrange("p t g -> p (t g)")
                    link(dve.tensor_scalar(pen, grp(15).rearrange("p t g -> p (t g)"), -NEG, NEG, ALU.mult, ALU.add))
                    link(tt(g4, g4, pen.unsqueeze(2).to_broadcast([P, TILES * N_GRP, 4]), ALU.add))
                    first_max(sel[:], C["prio16"], N_EXP, onehot[0][:], 2, 3)
                    t0, t1 = tmp[0][:, :, 0:N_EXP], tmp[1][:, :, 0:N_EXP]
                    link(dve.tensor_scalar(t0, onehot[0][:], 4 * NEG, None, ALU.mult))
                    link(tt(sel[:], sel[:], t0, ALU.add))
                    first_max(sel[:], C["prio16"], N_EXP, onehot[1][:], 2, 3)
                    for k in range(2):
                        link(tt(t0, prb[:], onehot[k][:], ALU.mult))
                        link(red(col[4 + k], t0, AX, ALU.add))
                    link(tt(col[6], col[4], col[5], ALU.add))
                    link(dve.reciprocal(col[7], col[6]))
                    for k in range(2):
                        link(tt(col[4 + k], col[4 + k], col[7], ALU.mult))
                        link(tt(col[4 + k], col[4 + k], C["valid"], ALU.mult))
                        link(tt(onehot[k][:], onehot[k][:], over(C["valid"], wide), ALU.mult))
                    tt(member[:], onehot[0][:], onehot[1][:], ALU.add).then_inc(rt_member, 1)
                    dve.wait_ge(rt_counts, 1)
                    link(dve.memset(before[:, 0, :], 0.0))
                    for n in range(TILES):
                        link(tt(before[:, n + 1, :], before[:, n, :], ps[:, 1, n * N_EXP:(n + 1) * N_EXP], ALU.add))
                    link(tt(slots[:], ps[:, 0, 0:TILES * N_EXP].rearrange("p (t e) -> p t e", e=N_EXP),
                            before[:, 0:TILES, :], ALU.add))
                    nb, cum, excl, start = (blk[:, n, :] for n in range(4))
                    ge = cnt_ge[:, :, 0:TILES]
                    link(tt(ge, over(before[:, TILES, :], [P, N_EXP, TILES]),
                            C["thr"].unsqueeze(1).to_broadcast([P, N_EXP, TILES]), ALU.is_gt))
                    link(red(nb, ge, AX, ALU.add))
                    link(dve.tensor_scalar(nb, nb, 1.0, None, ALU.max))
                    link(dve.tensor_tensor_scan(cum, C["ones"][:, 0:N_EXP], nb, 0.0, ALU.mult, ALU.add))
                    link(tt(excl, cum, nb, ALU.subtract))
                    link(dve.tensor_scalar(start, excl, float(P), None, ALU.mult))
                    link(tt(slots[:], slots[:], start.unsqueeze(1).to_broadcast(wide), ALU.add))
                    cge = cnt_ge[:].rearrange("p e b -> p b e")
                    link(dve.tensor_scalar(tmp[2][:, 0, :], C["thr_blk"], 1.0 / P, -1.0, ALU.mult, ALU.add))
                    link(tt(cge, tmp[2][:, 0, :].unsqueeze(2).to_broadcast([P, BLOCKS, N_EXP]),
                            cum.unsqueeze(1).to_broadcast([P, BLOCKS, N_EXP]), ALU.is_ge))
                    link(red(tmp[2][:, 1, :], cge, AX, ALU.add))
                    link(dve.tensor_scalar(blk_exp[:], tmp[2][:, 1, :], N_EXP - 1.0, None, ALU.min))
                    for k in range(2):
                        s_, b_, p_ = col[8], col[9], col[10]
                        link(tt(t0, slots[:], onehot[k][:], ALU.mult))
                        link(red(s_, t0, AX, ALU.add))
                        link(dve.tensor_copy(slot_u[:, k, :], s_))
                        shape = [P, TILES, BLOCKS]
                        link(tt(tmp[0][:], over(s_, shape), C["thr_blk"].unsqueeze(1).to_broadcast(shape), ALU.is_ge))
                        link(red(b_, tmp[0][:], AX, ALU.add))
                        link(dve.scalar_tensor_tensor(p_, b_, -float(P), s_, ALU.mult, ALU.add))
                        link(tt(at_pos[k][:], over(p_, [P, TILES, P]),
                                C["iota"].unsqueeze(1).to_broadcast([P, TILES, P]), ALU.is_equal))
                        link(tt(tmp[0][:], over(b_, shape),
                                C["iota"][:, 0:BLOCKS].unsqueeze(1).to_broadcast(shape), ALU.is_equal))
                        link(tt(col[11], C["tokid"], C["valid"], ALU.mult))
                        link(tt(at_blk[k][:, :, 0, :], tmp[0][:], over(col[11], shape), ALU.mult))
                        ins = tt(at_blk[k][:, :, 1, :], tmp[0][:], over(col[4 + k], shape), ALU.mult)
                        if k == 0:
                            link(ins)
                    ins.then_inc(rt_places, 1)
                    dve.wait_ge(rt_maps, 1)
                    dve.tensor_copy(tokmap[:], ps[:, 2, 0:BLOCKS])
                    link(dve.tensor_copy(gatemap[:], ps[:, 2, BLOCKS:2 * BLOCKS]))

            e_gu_in = [sem(f"e_gu_in{i}") for i in range(2)]
            e_dn_in = [sem(f"e_dn_in{i}") for i in range(2)]
            y_saved = [sem(f"y_saved{i}") for i in range(2)]
            (idx_ready, gu_hi_ready, gu_lo_ready, dn_hi_ready, dn_lo_ready, xt_trans, xt_hi_ready, xt_lo_ready,
             gu_ready, e_exp, e_link, hid_ready, ht_trans, ht_hi_ready, ht_lo_ready, dn_ready, y_half, y_ready) = \
                map(sem, ("idx_ready", "gu_hi_ready", "gu_lo_ready", "dn_hi_ready", "dn_lo_ready", "xt_trans",
                          "xt_hi_ready", "xt_lo_ready", "gu_ready", "e_exp", "e_link", "hid_ready", "ht_trans",
                          "ht_hi_ready", "ht_lo_ready", "dn_ready", "y_half", "y_ready"))
            XT_BANK, GU_BANK, HT_BANK, DN_BANK = 0, 2, 4, 5

            def block_steps(eng, step):
                step(0, 0, False)
                with eng.Fori(0, (BLOCKS - 2) // 2) as i:
                    for r in range(2):
                        step(2 * i + 1 + r, (1 + r) % 2, False)
                step(BLOCKS - 1, (BLOCKS - 1) % 2, True)

            with nc.Block() as block:
                @block.sync
                def _(sp_):
                    with sp_.Fori(0, BLOCKS // 2) as i:
                        for u in range(2):
                            b_ = 2 * i + u
                            ex = sp_.value_load(blk_exp[0:1, ds(b_, 1)], min_val=0, max_val=N_EXP - 1)
                            sp_.wait_ge(gu_lo_ready, b_ + 1)
                            for j, wsrc in enumerate((w_gate, w_up)):
                                sp_.dma_start(e_raw[u][:, j, :].rearrange("p (k f) -> p k f", f=FF),
                                              wsrc[L, ds(ex, 1)].rearrange("a e (k p) f -> p (a e k) f", p=P)) \
                                    .then_inc(e_gu_in[u], 16)
                            sp_.wait_ge(dn_lo_ready, b_ + 1)
                            sp_.dma_start(e_raw[u][:, 2, :], w_down[L, ds(ex, 1)].rearrange("a e f n -> (a e f) n")) \
                                .then_inc(e_dn_in[u], 16)

                @block.gpsimd
                def _(pool):
                    with pool.Fori(0, BLOCKS // 2) as i:
                        for u in range(2):
                            b_ = 2 * i + u
                            wait_apart(pool, xt_trans, 2 * b_ + 2, pool_passed)
                            pool.tensor_copy(idx[u][:], tokmap[:, ds(b_, 1)]).then_inc(idx_ready, 1)
                            wait_apart(pool, idx_ready, b_ + 1, pool_passed)
                            pool.indirect_dma_start(xg[u][:], None, h1_dram, bass.IndirectOffsetOnAxis(
                                ap=idx[u][:], axis=0)).then_inc(xg_in[u], 16)
                            wait_apart(pool, e_gu_in[u], 32 * i + 32, pool_passed)
                            wait_apart(pool, gu_ready, b_ + 1, pool_passed)
                            for j in range(2):
                                last = pool.tensor_copy(gu_hi[u][:, :, j, :],
                                                        e_raw[u][:, j, :].rearrange("p (k f) -> p k f", f=FF))
                            last.then_inc(gu_hi_ready, 1)

                @block.tensor
                def _(pe):
                    pe.sem_inc(xt_trans, 4)
                    pe.sem_inc(gu_ready, 2)
                    pe.sem_inc(dn_ready, 2)

                    def rows_in(b_, u, i):
                        pe.wait_ge(xg_in[u], layer * (16 * BLOCKS // 2) + 16 * i + 16)
                        pe.wait_ge(xt_lo_ready, 2 * b_ + 1)
                        for j in range(2):
                            if j:
                                pe.wait_ge(xt_lo_ready, 2 * b_ + 2)
                            for k in range(4):
                                kk = 4 * j + k
                                last = pe.transpose(ps[:, XT_BANK + j, k * P:(k + 1) * P],
                                                    xg[u][:, kk * P:(kk + 1) * P], C["ident"])
                            last.then_inc(xt_trans, 1)

                    def gate_up(b_, u):
                        pe.wait_ge(gu_lo_ready, 2 + b_ + 1)
                        pe.wait_ge(xt_lo_ready, 2 + 2 * b_ + 2)
                        pe.wait_ge(hid_ready, b_ + 1)
                        for k in range(KD):
                            last = three_passes(pe, ps[:, GU_BANK + u, 0:2 * FF], xt_hi[u][:, k, :], xt_lo[u][:, k, :],
                                                gu_hi[u][:, k, :, :], gu_lo[u][:, k, :, :], k == 0, k == KD - 1)
                        last.then_inc(gu_ready, 1)

                    def hidden_in(b_, u):
                        pe.wait_ge(hid_ready, 2 + b_ + 1)
                        pe.wait_ge(ht_lo_ready, b_ + 1)
                        pe.transpose(ps[:, HT_BANK, 0:P], hid[u][:, 2, :], C["ident"]).then_inc(ht_trans, 1)

                    def down(b_, u):
                        pe.wait_ge(ht_lo_ready, 1 + b_ + 1)
                        pe.wait_ge(dn_lo_ready, 2 + b_ + 1)
                        pe.wait_ge(y_half, b_ + 1)
                        pe.wait_ge(y_ready, b_ + 1)
                        for half in range(2):
                            cols = slice(512 * half, 512 * half + 512)
                            last = three_passes(pe, ps[:, DN_BANK + half, :], hid_hi[u][:], hid_lo[u][:],
                                                dn_hi[u][:, cols], dn_lo[u][:, cols], True, True)
                        last.then_inc(dn_ready, 1)

                    rows_in(0, 0, 0)
                    rows_in(1, 1, 0)
                    gate_up(0, 0)
                    with pe.Fori(0, (BLOCKS - 2) // 2) as i:
                        for r in range(2):
                            b_, u = 2 * i + 1 + r, (1 + r) % 2
                            rows_in(b_ + 1, 1 - u, i + 1)
                            hidden_in(b_ - 1, 1 - u)
                            gate_up(b_, u)
                            down(b_ - 1, 1 - u)
                    b_, u = BLOCKS - 1, (BLOCKS - 1) % 2
                    hidden_in(b_ - 1, 1 - u)
                    gate_up(b_, u)
                    down(b_ - 1, 1 - u)
                    hidden_in(b_, u)
                    down(b_, u)

                def xt_high(act, b_, u):
                    for j in range(2):
                        act.wait_ge(xt_trans, 4 + 2 * b_ + j + 1)
                        act.wait_ge(gu_ready, b_ + 1)
                        act.activation(xt_hi[u][:, 4 * j:4 * j + 4, :],
                                       ps[:, XT_BANK + j, :].rearrange("p (k t) -> p k t", k=4), ACT.Copy) \
                            .then_inc(xt_hi_ready, 1)

                @block.scalar
                def _(act):
                    def ht_high(b_, u):
                        act.wait_ge(ht_trans, b_ + 1)
                        act.wait_ge(dn_ready, b_ + 1)
                        act.activation(hid_hi[u][:], ps[:, HT_BANK, 0:P], ACT.Copy).then_inc(ht_hi_ready, 1)

                    def down_high(b_, u, i):
                        act.wait_ge(e_dn_in[u], 16 * i + 16)
                        act.wait_ge(dn_ready, b_ + 1)
                        act.activation(dn_hi[u][:], e_raw[u][:, 2, :], ACT.Copy).then_inc(dn_hi_ready, 1)

                    def gate_exp(b_, u):
                        act.wait_ge(gu_ready, 2 + b_ + 1)
                        act.activation(hid[u][:, 0, :], ps[:, GU_BANK + u, 0:FF], ACT.Exp, scale=-1.0) \
                            .then_inc(e_exp, 1)

                    def y_high_half(b_, u, i):
                        act.wait_ge(dn_ready, 2 + b_ + 1)
                        act.wait_ge(y_saved[u], 16 * i + 16)
                        act.activation(y_out[u][:, 512:1024], ps[:, DN_BANK + 1, :], ACT.Copy).then_inc(y_half, 1)

                    def y_store(b_, u):
                        act.wait_ge(y_ready, 1 + b_ + 1)
                        act.wait_ge(y_half, 1 + b_ + 1)
                        act.dma_start(y_dram[ds(b_ * P, P), :], y_out[u][:]).then_inc(y_saved[u], 16)

                    for u in range(2):
                        act.sem_inc(y_saved[u], 16)
                    act.sem_inc(y_half, 1)
                    xt_high(act, 0, 0)
                    xt_high(act, 1, 1)
                    down_high(0, 0, 0)
                    gate_exp(0, 0)
                    with act.Fori(0, (BLOCKS - 2) // 2) as i:
                        for r in range(2):
                            b_, u = 2 * i + 1 + r, (1 + r) % 2
                            xt_high(act, b_ + 1, 1 - u)
                            ht_high(b_ - 1, 1 - u)
                            down_high(b_, u, i + r)
                            gate_exp(b_, u)
                            y_high_half(b_ - 1, 1 - u, i)
                            y_store(b_ - 1, 1 - u)
                    b_, u, i = BLOCKS - 1, (BLOCKS - 1) % 2, BLOCKS // 2 - 1
                    ht_high(b_ - 1, 1 - u)
                    down_high(b_, u, i)
                    gate_exp(b_, u)
                    y_high_half(b_ - 1, 1 - u, i)
                    y_store(b_ - 1, 1 - u)
                    ht_high(b_, u)
                    y_high_half(b_, u, i)
                    y_store(b_, u)
                    for u in range(2):
                        act.wait_ge(y_saved[u], 16 + 16 * BLOCKS // 2)

                @block.vector
                def _(dve):
                    def xt_low(b_, u):
                        for j in range(2):
                            dve.wait_ge(xt_hi_ready, 2 * b_ + j + 1)
                            part = slice(4 * j, 4 * j + 4)
                            dve.tensor_tensor(xt_lo[u][:, part, :], ps[:, XT_BANK + j, :].rearrange("p (k t) -> p k t", k=4),
                                              f32(xt_hi[u][:, part, :]), ALU.subtract).then_inc(xt_lo_ready, 1)

                    def ht_low(b_, u):
                        dve.wait_ge(ht_hi_ready, b_ + 1)
                        dve.tensor_tensor(hid_lo[u][:], ps[:, HT_BANK, 0:P], f32(hid_hi[u][:]), ALU.subtract) \
                            .then_inc(ht_lo_ready, 1)

                    def gu_low(b_, u):
                        dve.wait_ge(gu_hi_ready, b_ + 1)
                        for j in range(2):
                            last = dve.tensor_tensor(gu_lo[u][:, :, j, :],
                                                     e_raw[u][:, j, :].rearrange("p (k f) -> p k f", f=FF),
                                                     f32(gu_hi[u][:, :, j, :]), ALU.subtract)
                        last.then_inc(gu_lo_ready, 1)

                    def down_low(b_, u):
                        dve.wait_ge(dn_hi_ready, b_ + 1)
                        dve.tensor_tensor(dn_lo[u][:], e_raw[u][:, 2, :], f32(dn_hi[u][:]), ALU.subtract) \
                            .then_inc(dn_lo_ready, 1)

                    def hidden(b_, u):
                        link = Link(dve, e_link, 3 * b_)
                        dve.wait_ge(e_exp, b_ + 1)
                        link(dve.tensor_scalar(hid[u][:, 1, :], hid[u][:, 0, :], 1.0, None, ALU.add))
                        link(dve.reciprocal(hid[u][:, 0, :], hid[u][:, 1, :]))
                        link(dve.tensor_tensor(hid[u][:, 1, :], ps[:, GU_BANK + u, 0:FF], hid[u][:, 0, :], ALU.mult))
                        dve.scalar_tensor_tensor(hid[u][:, 2, :], ps[:, GU_BANK + u, FF:2 * FF],
                                                 gatemap[:, ds(b_, 1)], hid[u][:, 1, :], ALU.mult, ALU.mult) \
                            .then_inc(hid_ready, 1)

                    def y_low_half(b_, u, i):
                        dve.wait_ge(dn_ready, 2 + b_ + 1)
                        dve.wait_ge(y_saved[u], 16 * i + 16)
                        dve.tensor_copy(y_out[u][:, 0:512], ps[:, DN_BANK, :]).then_inc(y_ready, 1)

                    dve.sem_inc(gu_lo_ready, 2)
                    dve.sem_inc(dn_lo_ready, 2)
                    dve.sem_inc(xt_lo_ready, 2)
                    dve.sem_inc(hid_ready, 2)
                    dve.sem_inc(ht_lo_ready, 1)
                    dve.sem_inc(y_ready, 1)
                    xt_low(0, 0)
                    gu_low(0, 0)
                    xt_low(1, 1)
                    gu_low(1, 1)
                    down_low(0, 0)
                    hidden(0, 0)
                    with dve.Fori(0, (BLOCKS - 2) // 2) as i:
                        for r in range(2):
                            b_, u = 2 * i + 1 + r, (1 + r) % 2
                            xt_low(b_ + 1, 1 - u)
                            ht_low(b_ - 1, 1 - u)
                            gu_low(b_ + 1, 1 - u)
                            down_low(b_, u)
                            hidden(b_, u)
                            y_low_half(b_ - 1, 1 - u, i)
                    b_, u, i = BLOCKS - 1, (BLOCKS - 1) % 2, BLOCKS // 2 - 1
                    ht_low(b_ - 1, 1 - u)
                    down_low(b_, u)
                    hidden(b_, u)
                    y_low_half(b_ - 1, 1 - u, i)
                    ht_low(b_, u)
                    y_low_half(b_, u, i)

            f_in = [sem(f"f_in{i}") for i in range(3)]
            f_saved = [sem(f"f_saved{i}") for i in range(3)]
            (f_ln_in, f_idx, f_link, f_summed, f_var, f_rstd, f_scaled, f_normed, f_trans, f_hi, f_lo) = map(sem, (
                "f_ln_in", "f_idx", "f_link", "f_summed", "f_var", "f_rstd", "f_scaled", "f_normed", "f_trans",
                "f_hi", "f_lo"))

            with nc.Block() as block:
                @block.sync
                def _(sp_):
                    sp_.dma_start(ln_g[:], ln2_g[L].to_broadcast([P, D])).then_inc(f_ln_in, 16)
                    sp_.dma_start(ln_b[:], ln2_b[L].to_broadcast([P, D])).then_inc(f_ln_in, 16)
                    with sp_.Fori(0, TILES // 3) as i:
                        for r in range(3):
                            n = 3 * i + r
                            sp_.wait_ge(f_scaled, n + 1)
                            sp_.dma_start(res[r][:], h1_dram[ds(n * P, P), :]).then_inc(f_in[r], 16)

                @block.gpsimd
                def _(pool):
                    pool.wait_ge(f_ln_in, 32)

                    def gather(n, r):
                        wait_apart(pool, f_summed, n + 1, pool_passed)
                        pool.tensor_copy(f_idx_t[r][:, 0:1], slot_u[:, 0, ds(n, 1)])
                        pool.tensor_copy(f_idx_t[r][:, 1:2], slot_u[:, 1, ds(n, 1)]).then_inc(f_idx, 1)
                        wait_apart(pool, f_idx, n + 1, pool_passed)
                        for k, y in enumerate((y_a, y_b)):
                            pool.indirect_dma_start(y[r][:], None, y_dram, bass.IndirectOffsetOnAxis(
                                ap=f_idx_t[r][:, k:k + 1], axis=0)).then_inc(fy_in[r], 16)

                    def finish(n, r):
                        pool.wait_ge(f_var, n + 1)
                        pool.tensor_tensor(stat[:, r, 15:16], stat[:, r, 14:15], C["half"], ALU.pow).then_inc(f_rstd, 1)
                        pool.wait_ge(f_scaled, 3 + n + 1)
                        pool.tensor_tensor(nrm[r][:], nrm[r][:], ln_b[:], ALU.add).then_inc(f_normed, 1)

                    gather(0, 0)
                    gather(1, 1)
                    with pool.Fori(0, TILES // 3 - 1) as i:
                        for r in range(3):
                            gather(3 * i + r + 2, (r + 2) % 3)
                            finish(3 * i + r, r)
                    gather(TILES - 1, 2)
                    for r in range(3):
                        finish(TILES - 3 + r, r)

                @block.tensor
                def _(pe):
                    pe.sem_inc(f_trans, 6)
                    with pe.Fori(0, TILES // 3) as i:
                        for r in range(3):
                            n = 3 * i + r
                            pe.wait_ge(f_normed, n + 1)
                            pe.wait_ge(f_lo, 2 * n + 2)
                            for j in range(2):
                                for k in range(4):
                                    kk = 4 * j + k
                                    last = pe.transpose(ps[:, 2 * r + j, k * P:(k + 1) * P],
                                                        nrm[r][:, kk * P:(kk + 1) * P], C["ident"])
                                last.then_inc(f_trans, 1)

                @block.scalar
                def _(act):
                    for r in range(3):
                        act.sem_inc(f_saved[r], 32)
                    act.wait_ge(f_ln_in, 32)

                    def tile(n, r, with_out):
                        act.wait_ge(f_normed, n + 1)
                        act.dma_start(h_dram[ds(n * P, P), :], nrm[r][:]).then_inc(f_saved[r], 16)
                        if with_out:
                            act.dma_start(out[0, ds(n * P, P), :], nrm[r][:]).then_inc(f_saved[r], 16)
                        for j in range(2):
                            act.wait_ge(f_trans, 6 + 2 * n + j + 1)
                            act.activation(act_hi[:, 4 * j:4 * j + 4, ds(n * P, P)],
                                           ps[:, 2 * r + j, :].rearrange("p (k t) -> p k t", k=4), ACT.Copy) \
                                .then_inc(f_hi, 1)

                    with act.Fori(0, TILES // 3 - 1) as i:
                        for r in range(3):
                            tile(3 * i + r, r, True)
                    for n in range(TILES - 3, TILES):
                        tile(n, n % 3, n < XT)
                    for r in range(3):
                        act.wait_ge(f_saved[r], 32 + 32 * TILES // 3 - 16 * (r == XT % 3))
                    act.wait_ge(f_hi, 2 * TILES)

                @block.vector
                def _(dve):
                    dve.sem_inc(f_summed, 3)
                    dve.sem_inc(f_scaled, 3)
                    dve.sem_inc(f_lo, 6)
                    dve.wait_ge(f_ln_in, 32)
                    with dve.Fori(0, TILES // 3) as i:
                        link = Link(dve, f_link, 15 * i)
                        for r in range(3):
                            n = 3 * i + r
                            dve.wait_ge(fy_in[r], layer * (32 * TILES // 3) + 32 * i + 32)
                            dve.tensor_tensor(y_a[r][:], y_a[r][:], y_b[r][:], ALU.add).then_inc(f_summed, 1)
                            dve.wait_ge(f_in[r], 16 * i + 16)
                            dve.wait_ge(f_summed, 3 + n + 1)
                            link(dve.scalar_tensor_tensor(res[r][:], res[r][:], ALPHA, y_a[r][:], ALU.mult, ALU.add))
                            norm_statistics(dve, link, res[r], stat[:, r, :], f_var)
                            dve.wait_ge(f_rstd, n + 1)
                            dve.wait_ge(f_saved[r], 32 * i + 32)
                            dve.wait_ge(f_trans, 2 * n + 2)
                            link(dve.tensor_scalar(nrm[r][:], res[r][:], stat[:, r, 12:13], stat[:, r, 15:16],
                                                   ALU.subtract, ALU.mult))
                            dve.tensor_tensor(nrm[r][:], nrm[r][:], ln_g[:], ALU.mult).then_inc(f_scaled, 1)
                            for j in range(2):
                                dve.wait_ge(f_hi, 2 * n + j + 1)
                                dve.tensor_tensor(act_lo[:, 4 * j:4 * j + 4, ds(n * P, P)],
                                                  ps[:, 2 * r + j, :].rearrange("p (k t) -> p k t", k=4),
                                                  f32(act_hi[:, 4 * j:4 * j + 4, ds(n * P, P)]), ALU.subtract) \
                                    .then_inc(f_lo, 1)

            nc.all_engine_barrier()
            nc.gpsimd.sem_clear(range(layer_sems[0].num, layer_sems[-1].num + 1))
            nc.all_engine_barrier()


_INS = ["x", "meta_tokens", "w_in", "conv_w", "lambda_q1", "lambda_k1", "lambda_q2", "lambda_k2", "diff_norm_g",
        "w_out", "ln1_g", "ln1_b", "router_w", "router_bias", "w_gate", "w_up", "w_down", "ln2_g", "ln2_b"]


def kernel(**inputs):
    import numpy as _np
    import concourse.bacc as _bacc
    from concourse import mybir as _mybir
    from concourse.bass_utils import run_bass_kernel_spmd as _run

    nc = _bacc.Bacc("TRN2", target_bir_lowering=False, num_devices=1)
    arrays, args = {}, []
    given = {name: inputs[name] for name in _INS}
    given["conv_w"] = _np.asarray(inputs["conv_w"]).reshape(DEPTH, 3, CONV_TILES, P).transpose(0, 3, 2, 1) \
        .reshape(DEPTH, P, CONV_TILES * 3)
    given.update(consts=shape_constants(), rope=rope_constants(), lam_consts=layer_constants())
    for name, value in given.items():
        a = _np.ascontiguousarray(value)
        arrays[f"in_{name}_dram"] = a
        args.append(nc.dram_tensor(f"in_{name}_dram", a.shape, _mybir.dt.from_np(a.dtype), kind="ExternalInput").ap())
    args.append(nc.dram_tensor("out_0_dram", (1, SEQ, D), _mybir.dt.float32, kind="ExternalOutput").ap())
    build_trunk(nc, *args)
    r = _run(nc, [arrays], core_ids=[0])
    return r.results[0]["out_0_dram"]
```

```python
import math
from contextlib import ExitStack

import numpy as np

import concourse.bass as bass
from concourse import mybir

F32 = mybir.dt.float32
F32R = mybir.dt.float32r
BF16 = mybir.dt.bfloat16
I32 = mybir.dt.int32
U32 = mybir.dt.uint32
ALU = mybir.AluOpType
ACT = mybir.ActivationFunctionType
AX = mybir.AxisListType.X
ds = bass.ds

P = 128
D = 1024
KD = D // P
SEQ = 1024
N_META = 16
TOK = SEQ + N_META
TILES = -(-TOK // P)
ROWS = TILES * P
XT = SEQ // P
META0 = SEQ
DEPTH = 2
IN_COLS = 3072
HD = 64
QKV_TILES = 12
CONV_TILES = 4
CONV0 = QKV_TILES * P
CONV_W = CONV_TILES * P
SB_Q, SB_K, SB_V, DF_Q, DF_K, DF_V = range(0, 12, 2)
SUB = 32
ROPE = 8
N_EXP = 16
N_GRP = 4
FF = 128
BLOCKS = N_EXP + (2 * TOK - N_EXP) // P
MIN_BLOCKS = 2 * -(-2 * TOK // (2 * P))
ALPHA = (2.0 * DEPTH) ** 0.25
EPS = 1e-5
NEG = -1e30
SB_SCALE = HD ** -0.5
DF_SCALE = SUB ** -0.5

CHUNKS = [(0, 348), (348, 694), (694, TOK)]

CONST_COLS = dict(ident=P, suffix=P, prefix=P, ones=P, rotate=P, negmask=P + 4, iota=P, tokid=TILES,
                  valid=TILES, prio16=16, prio4=4, thr=TILES, thr_blk=BLOCKS, half=1)


def const_slices():
    at, out = 0, {}
    for name, n in CONST_COLS.items():
        out[name] = slice(at, at + n)
        at += n
    return out, at


def shape_constants():
    where, total = const_slices()
    c = np.zeros((P, total), np.float32)
    r = np.arange(P)
    c[:, where["ident"]] = np.eye(P)
    c[:, where["suffix"]] = r[:, None] >= r[None, :]
    c[:, where["prefix"]] = r[:, None] < r[None, :]
    c[:, where["ones"]] = 1.0
    rot = np.zeros((P, P), np.float32)
    for p in range(P):
        j = p % SUB
        if j < ROPE // 2:
            rot[p + ROPE // 2, p] = -1.0
        elif j < ROPE:
            rot[p - ROPE // 2, p] = 1.0
    c[:, where["rotate"]] = rot
    neg = np.full((P, P + 4), NEG, np.float32)
    neg[:, :P] = np.where(r[None, :] <= r[:, None], 0.0, NEG)
    c[:, where["negmask"]] = neg
    c[:, where["iota"]] = r[None, :]
    tok = np.arange(TILES)[None, :] * P + r[:, None]
    c[:, where["tokid"]] = tok
    c[:, where["valid"]] = tok < TOK
    c[:, where["prio16"]] = 16 - np.arange(16)
    c[:, where["prio4"]] = 4 - np.arange(4)
    c[:, where["thr"]] = np.arange(TILES) * P
    c[:, where["thr_blk"]] = (np.arange(BLOCKS) + 1) * P
    c[:, where["half"]] = -0.5
    return c


def rope_constants():
    pos = np.concatenate([np.arange(SEQ) + N_META, np.arange(N_META)]).astype(np.float32)
    inv = (500000.0 ** (-np.arange(0, ROPE, 2) / ROPE)).astype(np.float32)
    ang = (pos[None, :] * inv[:, None]).astype(np.float32).astype(np.float64)
    cos, sin = np.ones((P, TOK)), np.zeros((P, TOK))
    for p in range(P):
        j = p % SUB
        if j < ROPE:
            cos[p], sin[p] = np.cos(ang[j % (ROPE // 2)]), np.sin(ang[j % (ROPE // 2)])
    return np.stack([cos, sin]).astype(np.float32)


def layer_constants():
    lam = [0.8 - 0.6 * math.exp(-0.3 * l) for l in range(DEPTH)]
    return np.array([[v, 1.0 - v] for v in lam], np.float32)


def row_pieces(i):
    if i == XT:
        return 1, N_META
    keys = N_META + (i + 1) * P
    n = -(-keys // 512)
    w = -(-keys // n)
    return n, w + w % 2


DIFF_ROWS = [XT] + list(range(XT))
DIFF_KEYS = max(n * w for n, w in map(row_pieces, DIFF_ROWS))


def key_tiles(i):
    out = [(XT, 0, N_META)]
    if i < XT:
        out += [(n, N_META + n * P, P) for n in range(i + 1)]
    return out


def sb_steps():
    out = []
    for first_tile in (4, 0):
        for n in list(range(first_tile + 3, -1, -1)) + [XT]:
            lo = max(0, n - first_tile) * P if n < XT else 0
            out.append(dict(tile0=first_tile, lo=lo, hi=512, key=n,
                            diag=n < XT and n >= first_tile,
                            first=n == first_tile + 3, last=n == XT))
    out.append(dict(tile0=XT, lo=0, hi=P, key=XT, diag=True, first=True, last=True))
    return out


SB_STEPS = [dict(s, head=h) for s in sb_steps() for h in range(2)]


class Map:

    def __init__(self, nc, at, end):
        self.nc, self.at, self.end = nc, at, end

    def put(self, name, shape, dt, size=4):
        n = size
        for s in shape[1:]:
            n *= s
        t = self.nc.alloc_sbuf_tensor_at(name, shape, dt, offset=self.at)
        self.at += (n + 31) // 32 * 32
        assert self.at <= self.end, (name, self.at, self.end)
        return t


def f32(ap):
    return ap.bitcast(F32)


def wait_apart(eng, sem, value, passed):
    eng.wait_ge(sem, value)
    eng.sem_inc(passed, 1)


class Link:

    def __init__(self, eng, sem, base=0):
        self.eng, self.sem, self.base, self.n = eng, sem, base, 0

    def __call__(self, ins):
        self.n += 1
        ins.then_inc(self.sem, 1)
        self.eng.wait_ge(self.sem, self.base + self.n)


def three_passes(pe, out, stat_hi, stat_lo, mov_hi, mov_lo, start, stop):
    pe.matmul(out, stat_lo, mov_hi, start=start, stop=False)
    pe.matmul(out, stat_hi, mov_lo, start=False, stop=False)
    return pe.matmul(out, stat_hi, mov_hi, start=False, stop=stop)


def build_trunk(nc, x, meta_tokens, w_in, conv_w, lambda_q1, lambda_k1, lambda_q2, lambda_k2,
                diff_norm_g, w_out, ln1_g, ln1_b, router_w, router_bias, w_gate, w_up, w_down,
                ln2_g, ln2_b, consts, rope, lam_consts, out):
    h_dram = nc.dram_tensor("h_rows", [ROWS, D], F32, kind="Internal").ap()
    h1_dram = nc.dram_tensor("h1_rows", [ROWS, D], F32, kind="Internal").ap()
    y_dram = nc.dram_tensor("y_slots", [BLOCKS * P, D], F32, kind="Internal").ap()

    ctx = ExitStack()
    with ctx:
        base = (nc.sbuf_base + 63) // 64 * 64
        end = nc.sbuf_usable_end
        m = Map(nc, base, end)
        where, n_const = const_slices()
        cst = m.put("cst", [P, n_const], F32)
        C = {k: cst[:, v] for k, v in where.items()}
        suffix = m.put("suffix", [P, P], F32R)
        prefix = m.put("prefix", [P, P], F32R)
        ident_bf = m.put("ident_bf", [P, P], BF16, 2)
        negmask_bf = m.put("negmask_bf", [P, P + 4], BF16, 2)
        router = m.put("router", [P, KD, N_EXP], F32)
        rbias = m.put("rbias", [P, N_EXP], F32)
        logits = m.put("logits", [P, TILES, N_EXP], F32)
        slot_u = m.put("slot_u", [P, 2, TILES], U32)
        tokmap = m.put("tokmap", [P, BLOCKS], U32)
        gatemap = m.put("gatemap", [P, BLOCKS], F32)
        idx = [m.put(f"idx{i}", [P, 1], U32) for i in range(2)]
        f_idx_t = [m.put(f"f_idx_t{i}", [P, 2], U32) for i in range(3)]
        pair_word = m.put("pair_word", [P, BLOCKS // 2], I32)
        counts = m.put("counts", [P, 2], I32)
        gathers = m.put("gathers", [P, 2], F32)
        stat = m.put("stat", [P, 3, 16], F32)
        m.at = (m.at + 63) // 64 * 64
        at0 = m.at
        act_hi = m.put("act_hi", [P, KD, ROWS], F32R)
        act_lo = m.put("act_lo", [P, KD, ROWS], F32R)
        under = m.at

        x_rows = Map(nc, under, end).put("x_rows", [P, TILES, D], F32)

        a = Map(nc, under, end)
        qkv = a.put("qkv", [P, QKV_TILES, TOK], F32)
        conv_y = a.put("conv_y", [P, CONV_TILES, TOK], F32)
        after_qkv = a.at
        w_raw = [a.put(f"w_raw{b}", [P, KD, P], F32) for b in range(3)]
        w_hi = [a.put(f"w_hi{b}", [P, KD, P], F32R) for b in range(3)]
        w_lo = [a.put(f"w_lo{b}", [P, KD, P], F32R) for b in range(3)]
        gate_b = a.put("gate_b", [P, TOK], F32)
        gate_c = a.put("gate_c", [P, TOK], F32)
        conv_u = a.put("conv_u", [P, TOK + 2], F32)
        conv_t = a.put("conv_t", [P, TOK], F32)
        taps = a.put("taps", [P, CONV_TILES, 3], F32)

        b = Map(nc, after_qkv, end)
        v_rows = b.put("v_rows", [P, TILES, 512], F32)
        y_sb = b.put("y_sb", [P, TILES, 256], F32)
        y_df = b.put("y_df", [P, TILES, 256], F32)
        q_hi_at = b.at
        q_hi = b.put("q_hi", [P, ROWS], F32R)
        q_lo = b.put("q_lo", [P, ROWS], F32R)
        lam_in = b.put("lam_in", [P, 4, SUB], F32)
        lam = b.put("lam", [P, 8], F32)
        norm_g = b.put("norm_g", [P, HD], F32)
        t = Map(nc, at0, under)
        k_hi = t.put("k_hi", [P, ROWS], F32R)
        k_lo = t.put("k_lo", [P, ROWS], F32R)
        after_k = t.at
        zs = [t.put(f"zs{i}", [P, 512], F32) for i in range(4)]
        ez = [t.put(f"ez{i}", [P, 512], F32) for i in range(2)]
        sp = [t.put(f"sp{i}", [P, 512], F32) for i in range(2)]
        sp_hi = [t.put(f"sp_hi{i}", [P, 512], F32R) for i in range(4)]
        sp_lo = [t.put(f"sp_lo{i}", [P, 512], F32R) for i in range(4)]
        wt = [t.put(f"wt{i}", [P, 512], F32) for i in range(4)]
        t = Map(nc, after_k, under)
        cos_t = t.put("cos_t", [P, TOK], F32)
        sin_t = t.put("sin_t", [P, TOK], F32)
        rot_a = t.put("rot_a", [P, TOK], F32)
        rot_b = t.put("rot_b", [P, TOK], F32)
        prob = [[t.put(f"prob{u}{s}", [P, DIFF_KEYS], F32) for s in range(2)] for u in range(2)]
        a_t = [t.put(f"a_t{u}", [P, TILES, P], F32) for u in range(2)]
        df_stat = [t.put(f"df_stat{u}", [P, 16], F32) for u in range(2)]
        t = Map(nc, q_hi_at, b.at)
        sq = t.put("sq", [P, TILES * 4, HD], F32)
        t = Map(nc, b.at, end)
        ms = t.put("ms", [P, TILES * 4], F32)
        rms = t.put("rms", [P, TILES * 4], F32)

        c = Map(nc, under, end)
        wo_hi = c.put("wo_hi", [P, KD, D], F32R)
        wo_lo = c.put("wo_lo", [P, KD, D], F32R)
        after_wo = c.at
        wo_raw = [c.put(f"wo_raw{i}", [P, D], F32) for i in range(2)]
        ln_g = c.put("ln_g", [P, D], F32)
        ln_b = c.put("ln_b", [P, D], F32)
        res = [c.put(f"res{i}", [P, D], F32) for i in range(3)]
        nrm = [c.put(f"nrm{i}", [P, D], F32) for i in range(3)]
        h1_t = c.put("h1_t", [P, KD, P], F32)
        f = Map(nc, under, after_wo)
        y_a = [f.put(f"y_a{i}", [P, D], F32) for i in range(3)]
        y_b = [f.put(f"y_b{i}", [P, D], F32) for i in range(3)]

        d = Map(nc, at0, under)
        sel = d.put("sel", [P, TILES, N_EXP], F32)
        prb = d.put("prb", [P, TILES, N_EXP], F32)
        tmp = [d.put(f"tmp{i}", [P, TILES, BLOCKS], F32) for i in range(3)]
        pair = d.put("pair", [P, TILES * N_GRP, 6], F32)
        small = d.put("small", [P, 16, TILES, N_GRP], F32)
        onehot = [d.put(f"onehot{i}", [P, TILES, N_EXP], F32) for i in range(2)]
        member = d.put("member", [P, TILES, N_EXP], F32)
        before = d.put("before", [P, TILES + 1, N_EXP], F32)
        slots = d.put("slots", [P, TILES, N_EXP], F32)
        blk = d.put("blk", [P, 8, N_EXP], F32)
        cnt_ge = d.put("cnt_ge", [P, N_EXP, BLOCKS], F32)
        at_pos = [d.put(f"at_pos{i}", [P, TILES, P], F32) for i in range(2)]
        at_blk = [d.put(f"at_blk{i}", [P, TILES, 2, BLOCKS], F32) for i in range(2)]

        e = Map(nc, under, end)
        e_raw = e.put("e_raw", [P, 3 * 3, D], F32)
        gu_hi = e.put("gu_hi", [P, 3 * KD, 2, FF], F32R)
        gu_lo = e.put("gu_lo", [P, 3 * KD, 2, FF], F32R)
        dn_hi = e.put("dn_hi", [P, 3 * D], F32R)
        dn_lo = e.put("dn_lo", [P, 3 * D], F32R)
        y_out = [e.put(f"y_out{i}", [P, D], F32) for i in range(2)]
        e = Map(nc, at0, under)
        xg = [e.put(f"xg{i}", [P, D], F32) for i in range(2)]
        xt_hi = [e.put(f"xt_hi{i}", [P, KD, P], F32R) for i in range(2)]
        xt_lo = [e.put(f"xt_lo{i}", [P, KD, P], F32R) for i in range(2)]
        hid = [e.put(f"hid{i}", [P, 3, FF], F32) for i in range(2)]
        hid_hi = [e.put(f"hid_hi{i}", [P, P], F32R) for i in range(2)]
        hid_lo = [e.put(f"hid_lo{i}", [P, P], F32R) for i in range(2)]

        ps = ctx.enter_context(nc.psum_tensor("ps", [P, 8, 512], F32))

        pre = {n: ctx.enter_context(nc.semaphore("pre_" + n)) for n in
               ("const", "vec", "trans", "hi", "lo", "h_saved", "y_filled", "pad")
               + tuple(f"tile{n}" for n in range(TILES))}
        xg_in = [ctx.enter_context(nc.semaphore(f"xg_in{i}")) for i in range(2)]
        fy_in = [ctx.enter_context(nc.semaphore(f"fy_in{i}")) for i in range(3)]
        layer_sems = []

        def sem(name):
            s = ctx.enter_context(nc.semaphore(name))
            layer_sems.append(s)
            return s

        with nc.Block() as block:
            @block.sync
            def _(sp_):
                sp_.dma_start(cst[:], consts).then_inc(pre["const"], 16)
                sp_.dma_start(router[:], router_w.rearrange("(k p) e -> p k e", p=P)).then_inc(pre["const"], 16)
                sp_.dma_start(rbias[:], router_bias.rearrange("(a e) -> a e", a=1).to_broadcast([P, N_EXP])) \
                    .then_inc(pre["const"], 16)
                for n in range(XT):
                    sp_.dma_start(x_rows[:, n, :], x[0, n * P:(n + 1) * P, :]).then_inc(pre[f"tile{n}"], 16)
                sp_.wait_ge(pre["pad"], 1)
                sp_.dma_start(x_rows[0:N_META, XT, :], meta_tokens).then_inc(pre[f"tile{XT}"], 16)
                sp_.wait_ge(pre[f"tile{XT}"], 16)
                sp_.dma_start(h_dram[XT * P:ROWS, :], x_rows[:, XT, :]).then_inc(pre["h_saved"], 16)

            @block.gpsimd
            def _(pool):
                pool.memset(x_rows[:, XT, :], 0.0).then_inc(pre["pad"], 1)

            @block.scalar
            def _(act):
                act.preload_act_table_set("natural_log_exp_and_others")
                for n in range(TILES):
                    for j in range(2):
                        act.wait_ge(pre["trans"], 2 * n + j + 1)
                        act.activation(act_hi[:, 4 * j:4 * j + 4, n * P:(n + 1) * P],
                                       ps[:, 2 * (n % 4) + j, :].rearrange("p (k t) -> p k t", k=4),
                                       ACT.Copy).then_inc(pre["hi"], 1)
                act.dma_start(h_dram[0:XT * P, :], x[0]).then_inc(pre["h_saved"], 16)

            @block.vector
            def _(dve):
                dve.wait_ge(pre["const"], 48)
                dve.memset(gathers[:], 0.0)
                dve.tensor_copy(suffix[:], C["suffix"]).then_inc(pre["vec"], 1)
                dve.tensor_copy(prefix[:], C["prefix"]).then_inc(pre["vec"], 1)
                dve.tensor_copy(ident_bf[:], C["ident"]).then_inc(pre["vec"], 1)
                dve.tensor_copy(negmask_bf[:], C["negmask"]).then_inc(pre["vec"], 1)
                for n in range(TILES):
                    for j in range(2):
                        dve.wait_ge(pre["hi"], 2 * n + j + 1)
                        dve.tensor_tensor(act_lo[:, 4 * j:4 * j + 4, n * P:(n + 1) * P],
                                          ps[:, 2 * (n % 4) + j, :].rearrange("p (k t) -> p k t", k=4),
                                          f32(act_hi[:, 4 * j:4 * j + 4, n * P:(n + 1) * P]),
                                          ALU.subtract).then_inc(pre["lo"], 1)

            @block.tensor
            def _(pe):
                pe.wait_ge(pre["const"], 48)
                for n in range(TILES):
                    pe.wait_ge(pre[f"tile{n}"], 16)
                    if n >= 4:
                        pe.wait_ge(pre["lo"], 2 * (n - 4) + 2)
                    for j in range(2):
                        for k in range(4):
                            last = pe.transpose(ps[:, 2 * (n % 4) + j, k * P:(k + 1) * P],
                                                x_rows[:, n, (4 * j + k) * P:(4 * j + k + 1) * P], C["ident"])
                        last.then_inc(pre["trans"], 1)


        pool_passed, dve_passed, pe_passed = sem("pool_passed"), sem("dve_passed"), sem("pe_passed")

        with nc.Fori(0, DEPTH) as layer:
            L = ds(layer, 1)

            w_loaded = [sem(f"w_loaded{i}") for i in range(3)]
            acc_taken = [sem(f"acc_taken{i}") for i in range(3)]
            w_hi_ready, w_lo_ready, acc_ready, conv_done, conv_link, taps_in = map(sem, (
                "w_hi_ready", "w_lo_ready", "acc_ready", "conv_done", "conv_link", "taps_in"))
            with nc.Block() as block:
                @block.sync
                def _(sp_):
                    sp_.dma_start(taps[:], conv_w[L].rearrange("a p (j t) -> p (a j) t", t=3)).then_inc(taps_in, 16)

                    def load(tile, r, col):
                        sp_.wait_ge(w_lo_ready, tile + 1)
                        sp_.dma_start(w_raw[r][:], w_in[L, :, ds(col, P)].rearrange(
                            "a (k p) c -> p (a k) c", p=P)).then_inc(w_loaded[r], 16)

                    with sp_.Fori(0, QKV_TILES // 3) as i:
                        for r in range(3):
                            load(3 * i + r, r, (3 * i + r) * P)
                    with sp_.Fori(0, CONV_TILES) as j:
                        for r in range(3):
                            load(QKV_TILES + 3 * j + r, r, CONV0 + r * CONV_W + j * P)

                @block.gpsimd
                def _(pool):
                    pool.sem_inc(w_lo_ready, 3)
                    with pool.Fori(0, (QKV_TILES + 3 * CONV_TILES) // 3) as i:
                        for r in range(3):
                            tile = 3 * i + r
                            wait_apart(pool, acc_ready, 3 * tile + 3, pool_passed)
                            wait_apart(pool, w_loaded[r], 16 * (i + 1), pool_passed)
                            pool.tensor_copy(w_hi[r][:], w_raw[r][:]).then_inc(w_hi_ready, 1)
                            pool.wait_ge(w_hi_ready, tile + 1)
                            pool.tensor_tensor(w_lo[r][:], w_raw[r][:], f32(w_hi[r][:]), ALU.subtract) \
                                .then_inc(w_lo_ready, 1)

                @block.tensor
                def _(pe):
                    pe.sem_inc(acc_ready, 9)
                    with pe.Fori(0, (QKV_TILES + 3 * CONV_TILES) // 3) as i:
                        for r in range(3):
                            tile = 3 * i + r
                            pe.wait_ge(w_lo_ready, 3 + tile + 1)
                            for n, (c0, c1) in enumerate(CHUNKS):
                                pe.wait_ge(acc_taken[n], tile + 1)
                                for k in range(KD):
                                    last = three_passes(pe, ps[:, n, 0:c1 - c0], w_hi[r][:, k, :],
                                                        w_lo[r][:, k, :], act_hi[:, k, c0:c1],
                                                        act_lo[:, k, c0:c1], k == 0, k == KD - 1)
                                last.then_inc(acc_ready, 1)

                @block.scalar
                def _(act):
                    for n in range(3):
                        act.sem_inc(acc_taken[n], 1)

                    def take(tile, n, dst):
                        act.wait_ge(acc_ready, 9 + 3 * tile + n + 1)
                        c0, c1 = CHUNKS[n]
                        act.activation(dst, ps[:, n, 0:c1 - c0], ACT.Copy).then_inc(acc_taken[n], 1)

                    with act.Fori(0, QKV_TILES // 3) as i:
                        for r in range(3):
                            for n, (c0, c1) in enumerate(CHUNKS):
                                take(3 * i + r, n, qkv[:, ds(3 * i + r, 1), c0:c1].rearrange("p a t -> p (a t)"))
                    with act.Fori(0, CONV_TILES) as j:
                        act.wait_ge(conv_done, j + 1)
                        for r, dst in enumerate((gate_b, gate_c)):
                            for n, (c0, c1) in enumerate(CHUNKS):
                                take(QKV_TILES + 3 * j + r, n, dst[:, c0:c1])

                @block.vector
                def _(dve):
                    dve.sem_inc(conv_done, 1)
                    dve.memset(conv_u[:, 0:2], 0.0).then_inc(conv_link, 1)
                    dve.wait_ge(conv_link, 1)
                    dve.wait_ge(taps_in, 16)
                    with dve.Fori(0, CONV_TILES) as j:
                        link = Link(dve, conv_link, 1 + 5 * j)
                        tile = QKV_TILES + 3 * j + 2
                        for n, (c0, c1) in enumerate(CHUNKS):
                            dve.wait_ge(acc_taken[n], tile + 1)
                            dve.wait_ge(acc_ready, 9 + 3 * tile + n + 1)
                            xs = min(c1, META0) - c0
                            if c1 > META0:
                                link(dve.tensor_tensor(conv_u[:, 2:2 + N_META], ps[:, n, xs:c1 - c0],
                                                       gate_c[:, META0:TOK], ALU.mult))
                            dve.tensor_tensor(conv_u[:, 2 + N_META + c0:2 + N_META + c0 + xs], ps[:, n, 0:xs],
                                              gate_c[:, c0:c0 + xs], ALU.mult).then_inc(acc_taken[n], 1)
                        dve.wait_ge(acc_taken[2], tile + 2)
                        tap = [taps[:, ds(j, 1), q:q + 1].rearrange("p a b -> p (a b)") for q in range(3)]
                        link(dve.tensor_scalar(conv_t[:], conv_u[:, 0:TOK], tap[0], None, ALU.mult))
                        for q in (1, 2):
                            link(dve.scalar_tensor_tensor(conv_t[:], conv_u[:, q:q + TOK], tap[q], conv_t[:],
                                                          ALU.mult, ALU.add))
                        y = conv_y[:, ds(j, 1), :].rearrange("p a t -> p (a t)")
                        dve.tensor_tensor(y[:, 0:SEQ], conv_t[:, N_META:TOK], gate_b[:, 0:SEQ], ALU.mult)
                        link(dve.tensor_tensor(y[:, META0:TOK], conv_t[:, 0:N_META], gate_b[:, META0:TOK], ALU.mult))
                        dve.sem_inc(conv_done, 1)

            v_trans, v_taken, q_hi_ready, q_lo_ready, k_pad = map(sem, (
                "v_trans", "v_taken", "q_hi_ready", "q_lo_ready", "k_pad"))
            z_ready, zs_ready, abs_ready, exp_ready, ln_ready = map(sem, (
                "z_ready", "zs_ready", "abs_ready", "exp_ready", "ln_ready"))
            sp_ready, sp_masked, sp_hi_ready, sp_lo_ready, tri_done = map(sem, (
                "sp_ready", "sp_masked", "sp_hi_ready", "sp_lo_ready", "tri_done"))
            tmp_ready, w_ready, w_masked, pv_done, o_taken = map(sem, (
                "tmp_ready", "w_ready", "w_masked", "pv_done", "o_taken"))
            S = len(SB_STEPS)
            DIAG = [n for n, s in enumerate(SB_STEPS) if s["diag"]]
            ENDS = [n for n, s in enumerate(SB_STEPS) if s["last"]]
            Z, SUM, OUT = 0, 2, 4

            def rows_of(s):
                return N_META if s["key"] == XT else P

            with nc.Block() as block:
                @block.sync
                def _(sp_):
                    with sp_.If(layer < 1):
                        for first in range(MIN_BLOCKS * P, BLOCKS * P, SEQ):
                            n = min(SEQ, BLOCKS * P - first)
                            sp_.dma_start(y_dram[first:first + n, :], x[0, 0:n, :]).then_inc(pre["y_filled"], 16)

                @block.tensor
                def _(pe):
                    for n in range(TILES):
                        rows = P if n < XT else N_META
                        if n >= 2:
                            pe.wait_ge(v_taken, n - 1)
                        for j in range(4):
                            tile = (SB_V, SB_V + 1, DF_V, DF_V + 1)[j]
                            last = pe.transpose(ps[0:rows, 6 + n % 2, j * P:(j + 1) * P],
                                                qkv[:, tile, n * P:n * P + rows], C["ident"])
                        last.then_inc(v_trans, 1)
                    pe.wait_ge(v_taken, TILES)
                    with pe.Fori(0, 2) as pr:
                        pe.wait_ge(q_lo_ready, pr + 1)

                        def scores(n):
                            s = SB_STEPS[n]
                            if n >= 2:
                                pe.wait_ge(zs_ready, pr * S + n - 1)
                            h0 = s["head"] * HD
                            key = slice(s["key"] * P, (s["key"] + 1) * P)
                            q = slice(s["tile0"] * P + s["lo"], s["tile0"] * P + s["hi"])
                            three_passes(pe, ps[:, Z + n % 2, s["lo"]:s["hi"]],
                                         k_hi[h0:h0 + HD, key], k_lo[h0:h0 + HD, key],
                                         q_hi[h0:h0 + HD, q], q_lo[h0:h0 + HD, q], True, True) \
                                .then_inc(z_ready, 1)

                        def sums(n):
                            s, bank = SB_STEPS[n], SUM + SB_STEPS[n]["head"]
                            if n >= 2:
                                pe.wait_ge(tmp_ready, pr * S + n - 1)
                            if not s["first"]:
                                b, r = SB_STEPS[n - 2], rows_of(SB_STEPS[n - 2])
                                for part in (sp_hi, sp_lo):
                                    pe.matmul(ps[:, bank, b["lo"]:b["hi"]], prefix[0:r, :],
                                              part[(n - 2) % 4][0:r, b["lo"]:b["hi"]],
                                              start=False, stop=True, skip_group_check=True)
                            pe.wait_ge(sp_lo_ready, pr * S + n + 1)
                            r = rows_of(s)
                            for j, part in enumerate((sp_hi, sp_lo)):
                                last = pe.matmul(ps[:, bank, s["lo"]:s["hi"]], suffix[0:r, :],
                                                 part[n % 4][0:r, s["lo"]:s["hi"]],
                                                 start=s["first"] and j == 0, stop=True, skip_group_check=True)
                            last.then_inc(tri_done, 1)

                        def weighted(n):
                            s, r = SB_STEPS[n], rows_of(SB_STEPS[n])
                            if s["diag"]:
                                pe.wait_ge(w_masked, pr * len(DIAG) + DIAG.index(n) + 1)
                            if s["first"] and n >= 2:
                                e_ = [x for x in ENDS if x < n and SB_STEPS[x]["head"] == s["head"]]
                                if e_:
                                    pe.wait_ge(o_taken, pr * len(ENDS) + ENDS.index(e_[-1]) + 1)
                            if s["key"] == XT:
                                wait_apart(pe, w_ready, pr * S + n + 1, pe_passed)
                            else:
                                pe.wait_ge(w_ready, pr * S + n + 1)
                            for t0 in range(s["lo"], s["hi"], P):
                                v = v_rows[0:r, s["key"], ds(pr * P + s["head"] * HD, HD)]
                                last = pe.matmul(ps[:, OUT + s["head"], t0 // 2:t0 // 2 + HD],
                                                 wt[n % 4][0:r, t0:t0 + P], v,
                                                 start=s["first"] and t0 == s["lo"], stop=True,
                                                 skip_group_check=True)
                            last.then_inc(pv_done, 1)

                        for n in range(S + 4):
                            if n < S:
                                scores(n)
                            if 0 <= n - 2 < S:
                                sums(n - 2)
                            if 0 <= n - 4 < S:
                                weighted(n - 4)

                @block.scalar
                def _(act):
                    for n in range(TILES):
                        rows = P if n < XT else N_META
                        act.wait_ge(v_trans, n + 1)
                        act.activation(v_rows[0:rows, n, :], ps[0:rows, 6 + n % 2, :], ACT.Copy).then_inc(v_taken, 1)
                    with act.Fori(0, 2) as pr:
                        act.wait_ge(pv_done, pr * S + 1)
                        act.activation(q_hi[:, 0:TOK], qkv[:, ds(SB_Q + pr, 1), :].rearrange("p a t -> p (a t)"),
                                       ACT.Copy, scale=SB_SCALE).then_inc(q_hi_ready, 1)
                        act.activation(k_hi[:, 0:TOK], qkv[:, ds(SB_K + pr, 1), :].rearrange("p a t -> p (a t)"),
                                       ACT.Copy).then_inc(q_hi_ready, 1)

                        def part(buf, n):
                            s = SB_STEPS[n]
                            return buf[0:rows_of(s), s["lo"]:s["hi"]]

                        for n in range(S + 3):
                            if n < S:
                                s = SB_STEPS[n]
                                if n >= 4:
                                    act.wait_ge(tmp_ready, pr * S + n - 3)
                                act.wait_ge(z_ready, pr * S + n + 1)
                                act.activation(part(zs[n % 4], n), ps[0:rows_of(s), Z + n % 2, s["lo"]:s["hi"]],
                                               ACT.Copy).then_inc(zs_ready, 1)
                            if 0 <= n - 1 < S:
                                b = n - 1
                                act.wait_ge(abs_ready, pr * S + b + 1)
                                act.activation(part(ez[b % 2], b), part(ez[b % 2], b), ACT.Exp, scale=-1.0) \
                                    .then_inc(exp_ready, 1)
                            if 0 <= n - 3 < S:
                                b = n - 3
                                act.wait_ge(tmp_ready, pr * S + b + 1)
                                act.activation(part(wt[b % 4], b), part(wt[b % 4], b), ACT.Exp).then_inc(w_ready, 1)
                            if 0 <= n - 1 < S:
                                b = n - 1
                                act.wait_ge(exp_ready, pr * S + b + 1)
                                act.activation(part(ez[b % 2], b), part(ez[b % 2], b), ACT.Ln, bias=1.0) \
                                    .then_inc(ln_ready, 1)

                @block.gpsimd
                def _(pool):
                    pool.memset(f32(q_hi[:, TOK:ROWS]), 0.0)
                    pool.memset(f32(q_lo[:, TOK:ROWS]), 0.0)
                    pool.memset(f32(k_hi[:, TOK:ROWS]), 0.0)
                    pool.memset(f32(k_lo[:, TOK:ROWS]), 0.0).then_inc(k_pad, 1)
                    pool.sem_inc(tri_done, 4)
                    with pool.Fori(0, 2) as pr:
                        def low_triangle(buf, n, sem_in, sem_out):
                            r, lo = rows_of(SB_STEPS[n]), SB_STEPS[n]["lo"]
                            wait_apart(pool, sem_in, pr * S + n + 1, pool_passed)
                            part = buf[0:r, lo:lo + P]
                            pool.affine_select(out=part, in_=part, pattern=[[1, P]], compare_op=ALU.is_gt,
                                               fill=0.0, base=0, channel_multiplier=-1).then_inc(sem_out, 1)

                        for n in range(S + 3):
                            if 0 <= n - 1 < S:
                                b = n - 1
                                s, r = SB_STEPS[b], rows_of(SB_STEPS[b])
                                if s["diag"]:
                                    low_triangle(sp[b % 2], b, sp_ready, sp_masked)
                                    wait_apart(pool, sp_masked, pr * len(DIAG) + DIAG.index(b) + 1, pool_passed)
                                wait_apart(pool, sp_ready, pr * S + b + 1, pool_passed)
                                wait_apart(pool, tri_done, pr * S + b - 1 + 4 if b >= 4 else pr * S + 4, pool_passed)
                                pool.tensor_copy(sp_hi[b % 4][0:r, s["lo"]:s["hi"]], sp[b % 2][0:r, s["lo"]:s["hi"]]) \
                                    .then_inc(sp_hi_ready, 1)
                            if 0 <= n - 3 < S and SB_STEPS[n - 3]["diag"]:
                                low_triangle(wt[(n - 3) % 4], n - 3, w_ready, w_masked)

                @block.vector
                def _(dve):
                    dve.sem_inc(pv_done, 1)
                    dve.wait_ge(k_pad, 1)
                    with dve.Fori(0, 2) as pr:
                        dve.wait_ge(q_hi_ready, 2 * pr + 2)
                        dve.scalar_tensor_tensor(q_lo[:, 0:TOK], qkv[:, ds(SB_Q + pr, 1), :].rearrange("p a t -> p (a t)"),
                                                 SB_SCALE, f32(q_hi[:, 0:TOK]), ALU.mult, ALU.subtract)
                        dve.tensor_tensor(k_lo[:, 0:TOK], qkv[:, ds(SB_K + pr, 1), :].rearrange("p a t -> p (a t)"),
                                          f32(k_hi[:, 0:TOK]), ALU.subtract).then_inc(q_lo_ready, 1)

                        def part(buf, n):
                            s = SB_STEPS[n]
                            return buf[0:rows_of(s), s["lo"]:s["hi"]]

                        def take_out(n):
                            s = SB_STEPS[n]
                            tiles = (s["hi"] - s["lo"]) // P
                            dve.wait_ge(pv_done, pr * S + n + 2)
                            dve.tensor_copy(y_sb[:, s["tile0"]:s["tile0"] + tiles, ds(pr * P + s["head"] * HD, HD)],
                                            ps[:, OUT + s["head"], 0:tiles * HD].rearrange("p (t c) -> p t c", c=HD)) \
                                .then_inc(o_taken, 1)

                        for n in range(S + 5):
                            if n < S:
                                if n >= 2:
                                    dve.wait_ge(sp_ready, pr * S + n - 1)
                                dve.wait_ge(zs_ready, pr * S + n + 1)
                                dve.tensor_scalar(part(ez[n % 2], n).bitcast(U32), part(zs[n % 4], n).bitcast(U32),
                                                  0x7FFFFFFF, None, ALU.bitwise_and) \
                                    .then_inc(abs_ready, 1)
                            if 0 <= n - 3 < S:
                                b = n - 3
                                s = SB_STEPS[b]
                                dve.wait_ge(tri_done, pr * S + b + 1 + 4)
                                if b >= 4:
                                    dve.wait_ge(pv_done, pr * S + b - 3 + 1)
                                dve.tensor_tensor(part(wt[b % 4], b), part(zs[b % 4], b),
                                                  ps[0:rows_of(s), SUM + s["head"], s["lo"]:s["hi"]],
                                                  ALU.subtract).then_inc(tmp_ready, 1)
                            if 0 <= n - 2 < S:
                                b = n - 2
                                dve.wait_ge(sp_hi_ready, pr * S + b + 1)
                                dve.tensor_tensor(part(sp_lo[b % 4], b), part(sp[b % 2], b),
                                                  f32(part(sp_hi[b % 4], b)), ALU.subtract).then_inc(sp_lo_ready, 1)
                            if 0 <= n - 1 < S:
                                b = n - 1
                                if b >= 2:
                                    dve.wait_ge(sp_lo_ready, pr * S + b - 1)
                                dve.wait_ge(ln_ready, pr * S + b + 1)
                                dve.scalar_tensor_tensor(part(sp[b % 2], b), part(zs[b % 4], b), 0.0,
                                                         part(ez[b % 2], b), ALU.max, ALU.add).then_inc(sp_ready, 1)
                            if n - 5 in ENDS:
                                take_out(n - 5)

            (df_loaded, df_link, lam_sum, lam_exp, rot_ready, rot_taken, rot_cos, rot_sum, dq_hi, dq_lo) = map(sem, (
                "df_loaded", "df_link", "lam_sum", "lam_exp", "rot_ready", "rot_taken", "rot_cos", "rot_sum",
                "dq_hi", "dq_lo"))
            s_ready = [sem(f"s_ready{i}") for i in range(2)]
            m_ready = [sem(f"m_ready{i}") for i in range(2)]
            p_ready = [sem(f"p_ready{i}") for i in range(2)]
            a_ready, at_ready, at_taken, dpv_done, df_o_taken = map(sem, (
                "a_ready", "at_ready", "at_taken", "dpv_done", "df_o_taken"))
            UNITS = [(i, hh) for i in DIFF_ROWS for hh in range(2)]
            U = len(UNITS)
            GROUPS = [-(-len(key_tiles(i)) // 4) for i, _ in UNITS]
            G0 = [sum(GROUPS[:u]) for u in range(U + 1)]
            AT_BANK, DO_BANK = 6, 7

            with nc.Block() as block:
                @block.sync
                def _(sp_):
                    for n, v in enumerate((lambda_q1, lambda_k1, lambda_q2, lambda_k2)):
                        sp_.dma_start(lam_in[:, n, :], v[L].to_broadcast([P, SUB])).then_inc(df_loaded, 16)
                    sp_.dma_start(lam[:, 4:6], lam_consts[L].to_broadcast([P, 2])).then_inc(df_loaded, 16)
                    sp_.dma_start(norm_g[:], diff_norm_g[L].to_broadcast([P, HD])).then_inc(df_loaded, 16)
                    sp_.dma_start(cos_t[:], rope[0]).then_inc(df_loaded, 16)
                    sp_.dma_start(sin_t[:], rope[1]).then_inc(df_loaded, 16)

                @block.tensor
                def _(pe):
                    with pe.Fori(0, 2) as pr:
                        for j, first in enumerate((DF_Q, DF_K)):
                            for n, (c0, c1) in enumerate(CHUNKS):
                                last = pe.matmul(ps[:, 3 * j + n, 0:c1 - c0], C["rotate"],
                                                 qkv[:, ds(first + pr, 1), c0:c1].rearrange("p a t -> p (a t)"),
                                                 start=True, stop=True)
                            last.then_inc(rot_ready, 1)
                        pe.wait_ge(dq_lo, 2 * pr + 2)

                        def scores(u, s):
                            i, hh = UNITS[u]
                            pieces, w = row_pieces(i)
                            if u >= 1:
                                pe.wait_ge(p_ready[s], pr * U + u)
                            r0 = hh * HD + s * SUB
                            mask0 = N_META + i * P if i < XT else 0
                            for n in range(pieces):
                                bank = 3 * s + n
                                a0, a1 = max(mask0, n * w), (n + 1) * w
                                last = three_passes(pe, ps[:, bank, 0:w],
                                                    q_hi[r0:r0 + SUB, i * P:(i + 1) * P],
                                                    q_lo[r0:r0 + SUB, i * P:(i + 1) * P],
                                                    k_hi[r0:r0 + SUB, n * w:(n + 1) * w],
                                                    k_lo[r0:r0 + SUB, n * w:(n + 1) * w], True, True)
                                if a0 < a1:
                                    last = pe.matmul(ps[:, bank, a0 - n * w:a1 - n * w], ident_bf[:],
                                                     negmask_bf[:, a0 - mask0:a1 - mask0],
                                                     start=False, stop=True, skip_group_check=True)
                            last.then_inc(s_ready[s], 1)

                        def weighted(u):
                            i, hh = UNITS[u]
                            tiles = key_tiles(i)
                            pe.wait_ge(a_ready, pr * U + u + 1)
                            for g in range(GROUPS[u]):
                                if G0[u] + g >= 1:
                                    pe.wait_ge(at_taken, pr * G0[U] + G0[u] + g)
                                for j, (_, k0, nk) in enumerate(tiles[4 * g:4 * g + 4]):
                                    last = pe.transpose(ps[0:nk, AT_BANK, j * P:(j + 1) * P],
                                                        prob[u % 2][0][:, k0:k0 + nk], C["ident"])
                                last.then_inc(at_ready, 1)
                            if u >= 1:
                                pe.wait_ge(df_o_taken, pr * U + u)
                            wait_apart(pe, at_taken, pr * G0[U] + G0[u + 1], pe_passed)
                            for j, (vt, _, nk) in enumerate(tiles):
                                last = pe.matmul(ps[:, DO_BANK, 0:HD], a_t[u % 2][0:nk, j, :],
                                                 v_rows[0:nk, vt, ds(256 + pr * P + hh * HD, HD)],
                                                 start=j == 0, stop=j == len(tiles) - 1)
                            last.then_inc(dpv_done, 1)

                        for u in range(U + 1):
                            if u < U:
                                scores(u, 0)
                                scores(u, 1)
                            if u >= 1:
                                weighted(u - 1)

                @block.scalar
                def _(act):
                    act.wait_ge(lam_sum, 1)
                    act.activation(lam[:, 2:4], lam[:, 0:2], ACT.Exp).then_inc(lam_exp, 1)
                    with act.Fori(0, 2) as pr:
                        act.wait_ge(rot_sum, 2 * pr + 1)
                        act.activation(q_hi[:, 0:TOK], rot_a[:], ACT.Copy).then_inc(dq_hi, 1)
                        act.wait_ge(rot_sum, 2 * pr + 2)
                        act.activation(k_hi[:, 0:N_META], rot_a[:, META0:TOK], ACT.Copy)
                        act.activation(k_hi[:, N_META:TOK], rot_a[:, 0:SEQ], ACT.Copy).then_inc(dq_hi, 1)

                        def exps(u, s):
                            pieces, w = row_pieces(UNITS[u][0])
                            if u >= 2:
                                act.wait_ge(at_ready, pr * G0[U] + G0[u - 1])
                            act.wait_ge(m_ready[s], pr * U + u + 1)
                            st = df_stat[u % 2]
                            act.activation(prob[u % 2][s][:, 0:pieces * w].rearrange("p (n w) -> p n w", w=w),
                                           ps[:, 3 * s:3 * s + pieces, 0:w], ACT.Exp, bias=st[:, 2 + s:3 + s],
                                           scale=DF_SCALE, accum_out=st[:, 4 + s:5 + s]).then_inc(p_ready[s], 1)

                        for u in range(U + 1):
                            if u < U:
                                exps(u, 0)
                                exps(u, 1)
                            if u >= 1:
                                b_ = u - 1
                                nt = len(key_tiles(UNITS[b_][0]))
                                for g in range(GROUPS[b_]):
                                    n = min(4, nt - 4 * g)
                                    if b_ >= 2:
                                        act.wait_ge(dpv_done, pr * U + b_ - 1)
                                    act.wait_ge(at_ready, pr * G0[U] + G0[b_] + g + 1)
                                    act.activation(a_t[b_ % 2][:, 4 * g:4 * g + n, :],
                                                   ps[:, AT_BANK, 0:n * P].rearrange("p (n k) -> p n k", k=P),
                                                   ACT.Copy).then_inc(at_taken, 1)

                @block.gpsimd
                def _(pool):
                    pool.wait_ge(df_loaded, 16 * 8)
                    with pool.Fori(0, 2) as pr:
                        for j, first in enumerate((DF_Q, DF_K)):
                            wait_apart(pool, rot_taken, 2 * pr + j + 1, pool_passed)
                            pool.tensor_tensor(rot_b[:], qkv[:, ds(first + pr, 1), :].rearrange("p a t -> p (a t)"),
                                               cos_t[:], ALU.mult).then_inc(rot_cos, 1)

                @block.vector
                def _(dve):
                    dve.wait_ge(df_loaded, 16 * 8)
                    dve.sem_inc(rot_taken, 1)
                    link = Link(dve, df_link)
                    for n in (0, 2):
                        link(dve.tensor_tensor(lam_in[:, n, :], lam_in[:, n, :], lam_in[:, n + 1, :], ALU.mult))
                    dve.tensor_reduce(lam[:, 0:2], lam_in[:, 0:4:2, :], AX, ALU.add).then_inc(lam_sum, 1)
                    dve.wait_ge(lam_exp, 1)
                    link(dve.tensor_tensor(lam[:, 6:7], lam[:, 2:3], lam[:, 3:4], ALU.subtract))
                    link(dve.tensor_tensor(lam[:, 6:7], lam[:, 6:7], lam[:, 4:5], ALU.add))
                    link(dve.tensor_scalar(norm_g[:], norm_g[:], lam[:, 5:6], None, ALU.mult))
                    with dve.Fori(0, 2) as pr:
                        LINKS = 2 * 3 + U * 5
                        link = Link(dve, df_link, 5 + pr * LINKS)
                        for j in range(2):
                            dve.wait_ge(rot_ready, 2 * pr + j + 1)
                            for n, (c0, c1) in enumerate(CHUNKS):
                                link(dve.tensor_tensor(rot_a[:, c0:c1], ps[:, 3 * j + n, 0:c1 - c0], sin_t[:, c0:c1],
                                                       ALU.mult))
                            dve.wait_ge(rot_cos, 2 * pr + j + 1)
                            dve.tensor_tensor(rot_a[:], rot_b[:], rot_a[:], ALU.add).then_inc(rot_sum, 1)
                            dve.wait_ge(dq_hi, 2 * pr + j + 1)
                            if j == 0:
                                dve.tensor_tensor(q_lo[:, 0:TOK], rot_a[:], f32(q_hi[:, 0:TOK]), ALU.subtract) \
                                    .then_inc(dq_lo, 1)
                            else:
                                dve.tensor_tensor(k_lo[:, 0:N_META], rot_a[:, META0:TOK], f32(k_hi[:, 0:N_META]),
                                                  ALU.subtract)
                                dve.tensor_tensor(k_lo[:, N_META:TOK], rot_a[:, 0:SEQ], f32(k_hi[:, N_META:TOK]),
                                                  ALU.subtract).then_inc(dq_lo, 1)
                            dve.wait_ge(dq_lo, 2 * pr + j + 1)
                            dve.sem_inc(rot_taken, 1)

                        def maxima(u, s):
                            pieces, w = row_pieces(UNITS[u][0])
                            st = df_stat[u % 2]
                            dve.wait_ge(s_ready[s], pr * U + u + 1)
                            link(dve.tensor_reduce(st[:, s:s + 1], ps[:, 3 * s:3 * s + pieces, 0:w],
                                                   mybir.AxisListType.XY, ALU.max))
                            dve.tensor_scalar(st[:, 2 + s:3 + s], st[:, s:s + 1], -DF_SCALE, None, ALU.mult) \
                                .then_inc(m_ready[s], 1)

                        def difference(u):
                            pieces, w = row_pieces(UNITS[u][0])
                            st, (p0, p1) = df_stat[u % 2], [x[:, 0:pieces * w] for x in prob[u % 2]]
                            for s in range(2):
                                dve.wait_ge(p_ready[s], pr * U + u + 1)
                            link(dve.reciprocal(st[:, 6:8], st[:, 4:6]))
                            link(dve.tensor_tensor(st[:, 8:9], st[:, 7:8], lam[:, 6:7], ALU.mult))
                            link(dve.tensor_scalar(p1, p1, st[:, 8:9], None, ALU.mult))
                            dve.scalar_tensor_tensor(p0, p0, st[:, 6:7], p1, ALU.mult, ALU.subtract) \
                                .then_inc(a_ready, 1)

                        for u in range(U + 1):
                            if u < U:
                                maxima(u, 0)
                                maxima(u, 1)
                                difference(u)
                            if u >= 1:
                                i, hh = UNITS[u - 1]
                                dve.wait_ge(dpv_done, pr * U + u)
                                dve.tensor_copy(y_df[:, i, ds(pr * P + hh * HD, HD)], ps[:, DO_BANK, 0:HD]) \
                                    .then_inc(df_o_taken, 1)
                        assert link.n == LINKS, (link.n, LINKS)

            mix_link, mix_var, mix_rms, mix_normed, mix_trans, mix_hi, mix_lo, conv_hi, mix_pad = map(sem, (
                "mix_link", "mix_var", "mix_rms", "mix_normed", "mix_trans", "mix_hi", "mix_lo", "conv_hi", "mix_pad"))
            y_heads = y_df[:].rearrange("p t (h c) -> p (t h) c", c=HD)
            with nc.Block() as block:
                @block.gpsimd
                def _(pool):
                    pool.memset(f32(act_hi[:, :, TOK:ROWS]), 0.0)
                    pool.memset(f32(act_lo[:, :, TOK:ROWS]), 0.0).then_inc(mix_pad, 1)
                    pool.wait_ge(mix_var, 1)
                    pool.tensor_tensor(rms[:], ms[:], C["half"].to_broadcast([P, TILES * 4]), ALU.pow) \
                        .then_inc(mix_rms, 1)
                    pool.wait_ge(mix_pad, 1)

                @block.tensor
                def _(pe):
                    pe.wait_ge(mix_normed, 1)
                    for n in range(TILES):
                        rows = P if n < XT else N_META
                        if n >= 2:
                            pe.wait_ge(mix_lo, n - 1)
                        for j in range(4):
                            src = (y_sb, y_sb, y_df, y_df)[j]
                            last = pe.transpose(ps[:, n % 2, j * P:j * P + rows],
                                                src[0:rows, n, (j % 2) * P:(j % 2 + 1) * P], C["ident"][0:rows, 0:rows])
                        last.then_inc(mix_trans, 1)

                @block.scalar
                def _(act):
                    for j in range(CONV_TILES):
                        act.activation(act_hi[:, 4 + j, 0:TOK], conv_y[:, j, :], ACT.Copy).then_inc(conv_hi, 1)
                    for n in range(TILES):
                        rows = P if n < XT else N_META
                        act.wait_ge(mix_trans, n + 1)
                        act.activation(act_hi[:, 0:4, n * P:n * P + rows],
                                       ps[:, n % 2, :].rearrange("p (k t) -> p k t", k=4)[:, :, 0:rows],
                                       ACT.Copy).then_inc(mix_hi, 1)

                @block.vector
                def _(dve):
                    link = Link(dve, mix_link)
                    link(dve.tensor_tensor(sq[:], y_heads, y_heads, ALU.mult))
                    link(dve.tensor_reduce(ms[:], sq[:], AX, ALU.add))
                    dve.tensor_scalar(ms[:], ms[:], 1.0 / HD, EPS, ALU.mult, ALU.add).then_inc(mix_var, 1)
                    dve.wait_ge(mix_rms, 1)
                    link(dve.tensor_tensor(y_heads, y_heads, rms[:].unsqueeze(2).to_broadcast([P, TILES * 4, HD]),
                                           ALU.mult))
                    dve.tensor_tensor(y_heads, y_heads, norm_g[:].unsqueeze(1).to_broadcast([P, TILES * 4, HD]),
                                      ALU.mult).then_inc(mix_normed, 1)
                    for j in range(CONV_TILES):
                        dve.wait_ge(conv_hi, j + 1)
                        dve.tensor_tensor(act_lo[:, 4 + j, 0:TOK], conv_y[:, j, :], f32(act_hi[:, 4 + j, 0:TOK]),
                                          ALU.subtract)
                    for n in range(TILES):
                        rows = P if n < XT else N_META
                        dve.wait_ge(mix_hi, n + 1)
                        dve.tensor_tensor(act_lo[:, 0:4, n * P:n * P + rows],
                                          ps[:, n % 2, :].rearrange("p (k t) -> p k t", k=4)[:, :, 0:rows],
                                          f32(act_hi[:, 0:4, n * P:n * P + rows]), ALU.subtract).then_inc(mix_lo, 1)

            wo_loaded = [sem(f"wo_loaded{i}") for i in range(2)]
            res_in = [sem(f"res_in{i}") for i in range(3)]
            h1_saved = [sem(f"h1_saved{i}") for i in range(3)]
            (wo_hi_ready, wo_lo_ready, ln_in, mix_ready, res_ready, ln_link, var_ready, rstd_ready, scaled, normed,
             h1_trans, h1_taken, lg_ready, lg_taken) = map(sem, (
                 "wo_hi_ready", "wo_lo_ready", "ln_in", "mix_ready", "res_ready", "ln_link", "var_ready",
                 "rstd_ready", "scaled", "normed", "h1_trans", "h1_taken", "lg_ready", "lg_taken"))
            T_BANK, LG_BANK = 6, 7

            def norm_statistics(dve, link, rows_in, st, var_sem):
                link(dve.bn_stats(st[:, 0:6], rows_in[:, 0:512]))
                link(dve.bn_stats(st[:, 6:12], rows_in[:, 512:1024]))
                dve.sem_inc(dve_passed, 1)
                link(dve.bn_aggr(st[:, 12:14], st[:, 0:12]))
                dve.tensor_scalar(st[:, 14:15], st[:, 13:14], EPS, None, ALU.add).then_inc(var_sem, 1)

            with nc.Block() as block:
                @block.sync
                def _(sp_):
                    with sp_.Fori(0, KD // 2) as i:
                        for r in range(2):
                            sp_.wait_ge(wo_lo_ready, 2 * i + r + 1)
                            sp_.dma_start(wo_raw[r][:], w_out[L, ds((2 * i + r) * P, P), :].rearrange(
                                "a p n -> p (a n)")).then_inc(wo_loaded[r], 16)
                    sp_.dma_start(ln_g[:], ln1_g[L].to_broadcast([P, D])).then_inc(ln_in, 16)
                    sp_.dma_start(ln_b[:], ln1_b[L].to_broadcast([P, D])).then_inc(ln_in, 16)
                    sp_.wait_ge(pre["h_saved"], 32)
                    with sp_.Fori(0, TILES // 3) as i:
                        for r in range(3):
                            n = 3 * i + r
                            sp_.wait_ge(scaled, n + 1)
                            sp_.dma_start(res[r][:], h_dram[ds(n * P, P), :]).then_inc(res_in[r], 16)

                @block.gpsimd
                def _(pool):
                    pool.wait_ge(ln_in, 32)
                    with pool.Fori(0, TILES // 3) as i:
                        for r in range(3):
                            n = 3 * i + r
                            pool.wait_ge(var_ready, n + 1)
                            pool.tensor_tensor(stat[:, r, 15:16], stat[:, r, 14:15], C["half"], ALU.pow) \
                                .then_inc(rstd_ready, 1)
                            pool.wait_ge(scaled, 3 + n + 1)
                            pool.tensor_tensor(nrm[r][:], nrm[r][:], ln_b[:], ALU.add).then_inc(normed, 1)

                @block.tensor
                def _(pe):
                    pe.sem_inc(h1_trans, 6)

                    def project(n):
                        for half in range(2):
                            bank = 2 * (n % 3) + half
                            if half == 0 and n >= 3:
                                pe.wait_ge(res_ready, n - 2)
                            for k in range(KD):
                                if n == 0 and half == 0:
                                    pe.wait_ge(wo_lo_ready, 2 + k + 1)
                                cols = slice(512 * half, 512 * half + 512)
                                rows = slice(n * P, (n + 1) * P)
                                last = three_passes(pe, ps[:, bank, :], act_hi[:, k, rows], act_lo[:, k, rows],
                                                    wo_hi[:, k, cols], wo_lo[:, k, cols], k == 0, k == KD - 1)
                        last.then_inc(mix_ready, 1)

                    def route(n):
                        pe.wait_ge(normed, n + 1)
                        for j in range(2):
                            if 2 * n + j >= 1:
                                pe.wait_ge(h1_taken, 2 * n + j)
                            for k in range(4):
                                kk = 4 * j + k
                                last = pe.transpose(ps[:, T_BANK, k * P:(k + 1) * P],
                                                    nrm[n % 3][:, kk * P:(kk + 1) * P], C["ident"])
                            last.then_inc(h1_trans, 1)
                        if n >= 1:
                            pe.wait_ge(lg_taken, n)
                        pe.wait_ge(h1_taken, 2 * n + 2)
                        for k in range(KD):
                            last = pe.matmul(ps[:, LG_BANK, 0:N_EXP], h1_t[:, k, :], router[:, k, :],
                                             start=k == 0, stop=k == KD - 1)
                        last.then_inc(lg_ready, 1)

                    for n in range(TILES + 1):
                        if n < TILES:
                            project(n)
                        if n >= 1:
                            route(n - 1)

                @block.scalar
                def _(act):
                    with act.Fori(0, KD // 2) as i:
                        for r in range(2):
                            act.wait_ge(wo_loaded[r], 16 * (i + 1))
                            act.activation(wo_hi[:, ds(2 * i + r, 1), :].rearrange("p a n -> p (a n)"), wo_raw[r][:],
                                           ACT.Copy).then_inc(wo_hi_ready, 1)
                    for r in range(3):
                        act.sem_inc(h1_saved[r], 16)
                    with act.Fori(0, TILES // 3) as i:
                        for r in range(3):
                            n = 3 * i + r
                            for j in range(2):
                                act.wait_ge(h1_trans, 6 + 2 * n + j + 1)
                                act.activation(h1_t[:, 4 * j:4 * j + 4, :],
                                               ps[:, T_BANK, :].rearrange("p (k t) -> p k t", k=4), ACT.Copy) \
                                    .then_inc(h1_taken, 1)
                            act.dma_start(h1_dram[ds(n * P, P), :], nrm[r][:]).then_inc(h1_saved[r], 16)
                            act.wait_ge(lg_ready, n + 1)
                            act.activation(logits[:, ds(n, 1), :].rearrange("p a e -> p (a e)"),
                                           ps[:, LG_BANK, 0:N_EXP], ACT.Copy).then_inc(lg_taken, 1)
                    for r in range(3):
                        act.wait_ge(h1_saved[r], 16 + 16 * TILES // 3)
                    act.wait_ge(lg_taken, TILES)

                @block.vector
                def _(dve):
                    dve.sem_inc(wo_lo_ready, 2)
                    dve.sem_inc(scaled, 3)
                    with dve.Fori(0, KD // 2) as i:
                        for r in range(2):
                            dve.wait_ge(wo_hi_ready, 2 * i + r + 1)
                            k = ds(2 * i + r, 1)
                            dve.tensor_tensor(wo_lo[:, k, :].rearrange("p a n -> p (a n)"), wo_raw[r][:],
                                              f32(wo_hi[:, k, :]).rearrange("p a n -> p (a n)"), ALU.subtract) \
                                .then_inc(wo_lo_ready, 1)
                    dve.wait_ge(ln_in, 32)

                    def norm_tile(n, r, link, link_base):
                        dve.wait_ge(res_in[r], 16 * (link_base + 1))
                        dve.wait_ge(mix_ready, n + 1)
                        dve.scalar_tensor_tensor(res[r][:, 0:512], res[r][:, 0:512], ALPHA, ps[:, 2 * r, :],
                                                 ALU.mult, ALU.add)
                        dve.scalar_tensor_tensor(res[r][:, 512:1024], res[r][:, 512:1024], ALPHA, ps[:, 2 * r + 1, :],
                                                 ALU.mult, ALU.add).then_inc(res_ready, 1)
                        dve.wait_ge(res_ready, n + 1)
                        norm_statistics(dve, link, res[r], stat[:, r, :], var_ready)
                        dve.wait_ge(rstd_ready, n + 1)

                    with dve.Fori(0, TILES // 3) as i:
                        link = Link(dve, ln_link, 12 * i)
                        for r in range(3):
                            n = 3 * i + r
                            norm_tile(n, r, link, i)
                            dve.wait_ge(h1_saved[r], 16 * i + 16)
                            dve.wait_ge(h1_trans, 2 * n + 2)
                            link(dve.tensor_scalar(nrm[r][:], res[r][:], stat[:, r, 12:13], stat[:, r, 15:16],
                                                   ALU.subtract, ALU.mult))
                            dve.tensor_tensor(nrm[r][:], nrm[r][:], ln_g[:], ALU.mult).then_inc(scaled, 1)

            rt_link, rt_shifted, rt_exp, rt_member, rt_counts, rt_places, rt_maps = map(sem, (
                "rt_link", "rt_shifted", "rt_exp", "rt_member", "rt_counts", "rt_places", "rt_maps"))

            with nc.Block() as block:
                @block.scalar
                def _(act):
                    act.wait_ge(rt_shifted, 1)
                    act.activation(prb[:], sel[:], ACT.Exp).then_inc(rt_exp, 1)

                @block.tensor
                def _(pe):
                    pe.wait_ge(rt_member, 1)
                    pe.matmul(ps[:, 0, 0:TILES * N_EXP], C["prefix"], member[:], start=True, stop=True)
                    pe.matmul(ps[:, 1, 0:TILES * N_EXP], C["ones"], member[:], start=True, stop=True) \
                        .then_inc(rt_counts, 1)
                    pe.wait_ge(rt_places, 1)
                    for k in range(2):
                        for n in range(TILES):
                            last = pe.matmul(ps[:, 2, 0:2 * BLOCKS], at_pos[k][:, n, :], at_blk[k][:, n, :, :],
                                             start=k == 0 and n == 0, stop=k == 1 and n == TILES - 1)
                    last.then_inc(rt_maps, 1)

                @block.vector
                def _(dve):
                    link = Link(dve, rt_link)
                    tt, red = dve.tensor_tensor, dve.tensor_reduce
                    wide = [P, TILES, N_EXP]
                    col = [small[:, n, :, 0] for n in range(16)]
                    grp = lambda n: small[:, n, :, :]

                    def over(ap, shape):
                        return ap.unsqueeze(2).to_broadcast(shape)

                    def first_max(vals, prio, n, out_oh, c0, c1):
                        shape = [P, TILES, n]
                        link(red(col[c0], vals, AX, ALU.max))
                        link(tt(out_oh, vals, over(col[c0], shape), ALU.is_ge))
                        link(tt(out_oh, out_oh, prio.unsqueeze(1).to_broadcast(shape), ALU.mult))
                        link(red(col[c1], out_oh, AX, ALU.max))
                        link(tt(out_oh, out_oh, over(col[c1], shape), ALU.is_equal))

                    link(red(col[0], logits[:], AX, ALU.max))
                    tt(sel[:], logits[:], over(col[0], wide), ALU.subtract).then_inc(rt_shifted, 1)
                    dve.wait_ge(rt_exp, 1)
                    link(red(col[0], prb[:], AX, ALU.add))
                    link(dve.reciprocal(col[1], col[0]))
                    link(tt(prb[:], prb[:], over(col[1], wide), ALU.mult))
                    link(tt(sel[:], prb[:], rbias[:].unsqueeze(1).to_broadcast(wide), ALU.add))
                    g4 = sel[:].rearrange("p t (g e) -> p (t g) e", e=4)
                    tt(pair[:, :, 0:2], g4[:, :, 0:2], g4[:, :, 2:4], ALU.add)
                    tt(pair[:, :, 2:4], g4[:, :, 0:4:2], g4[:, :, 1:4:2], ALU.add)
                    tt(pair[:, :, 4:5], g4[:, :, 0:1], g4[:, :, 3:4], ALU.add)
                    link(tt(pair[:, :, 5:6], g4[:, :, 1:2], g4[:, :, 2:3], ALU.add))
                    link(red(grp(14).rearrange("p t g -> p (t g)"), pair[:], AX, ALU.max))
                    first_max(grp(14), C["prio4"], N_GRP, grp(15), 2, 3)
                    pen = grp(14).rearrange("p t g -> p (t g)")
                    link(dve.tensor_scalar(pen, grp(15).rearrange("p t g -> p (t g)"), -NEG, NEG, ALU.mult, ALU.add))
                    link(tt(g4, g4, pen.unsqueeze(2).to_broadcast([P, TILES * N_GRP, 4]), ALU.add))
                    first_max(sel[:], C["prio16"], N_EXP, onehot[0][:], 2, 3)
                    t0, t1 = tmp[0][:, :, 0:N_EXP], tmp[1][:, :, 0:N_EXP]
                    link(dve.tensor_scalar(t0, onehot[0][:], 4 * NEG, None, ALU.mult))
                    link(tt(sel[:], sel[:], t0, ALU.add))
                    first_max(sel[:], C["prio16"], N_EXP, onehot[1][:], 2, 3)
                    for k in range(2):
                        link(tt(t0, prb[:], onehot[k][:], ALU.mult))
                        link(red(col[4 + k], t0, AX, ALU.add))
                    link(tt(col[6], col[4], col[5], ALU.add))
                    link(dve.reciprocal(col[7], col[6]))
                    for k in range(2):
                        link(tt(col[4 + k], col[4 + k], col[7], ALU.mult))
                        link(tt(col[4 + k], col[4 + k], C["valid"], ALU.mult))
                        link(tt(onehot[k][:], onehot[k][:], over(C["valid"], wide), ALU.mult))
                    tt(member[:], onehot[0][:], onehot[1][:], ALU.add).then_inc(rt_member, 1)
                    dve.wait_ge(rt_counts, 1)
                    link(dve.memset(before[:, 0, :], 0.0))
                    for n in range(TILES):
                        link(tt(before[:, n + 1, :], before[:, n, :], ps[:, 1, n * N_EXP:(n + 1) * N_EXP], ALU.add))
                    link(tt(slots[:], ps[:, 0, 0:TILES * N_EXP].rearrange("p (t e) -> p t e", e=N_EXP),
                            before[:, 0:TILES, :], ALU.add))
                    nb, cum, excl, start = (blk[:, n, :] for n in range(4))
                    ge = cnt_ge[:, :, 0:TILES]
                    link(tt(ge, over(before[:, TILES, :], [P, N_EXP, TILES]),
                            C["thr"].unsqueeze(1).to_broadcast([P, N_EXP, TILES]), ALU.is_gt))
                    link(red(nb, ge, AX, ALU.add))
                    link(dve.tensor_scalar(nb, nb, 1.0, None, ALU.max))
                    link(dve.tensor_tensor_scan(cum, C["ones"][:, 0:N_EXP], nb, 0.0, ALU.mult, ALU.add))
                    link(tt(excl, cum, nb, ALU.subtract))
                    link(dve.tensor_scalar(start, excl, float(P), None, ALU.mult))
                    link(tt(slots[:], slots[:], start.unsqueeze(1).to_broadcast(wide), ALU.add))
                    cge = cnt_ge[:].rearrange("p e b -> p b e")
                    link(dve.tensor_scalar(tmp[2][:, 0, :], C["thr_blk"], 1.0 / P, -1.0, ALU.mult, ALU.add))
                    link(tt(cge, tmp[2][:, 0, :].unsqueeze(2).to_broadcast([P, BLOCKS, N_EXP]),
                            cum.unsqueeze(1).to_broadcast([P, BLOCKS, N_EXP]), ALU.is_ge))
                    link(red(tmp[2][:, 1, :], cge, AX, ALU.add))
                    word, ex_of, ex_cap = (tmp[k][:, 5:7, :].rearrange("p a b -> p (a b)") for k in range(3))
                    link(dve.memset(word, 0.0))
                    link(dve.memset(ex_of, N_EXP - 1.0))
                    link(dve.tensor_scalar(ex_of[:, 0:BLOCKS], tmp[2][:, 1, :], N_EXP - 1.0, None, ALU.min))
                    link(dve.tensor_scalar(ex_cap, ex_of, N_EXP - 3.0, None, ALU.min))
                    n = 2 * BLOCKS - 1
                    link(tt(word[:, 1:], ex_cap[:, 1:], ex_cap[:, 0:n], ALU.subtract))
                    link(dve.scalar_tensor_tensor(word[:, 1:], ex_of[:, 0:n], 2.0, word[:, 1:], ALU.mult, ALU.add))
                    link(dve.scalar_tensor_tensor(word[:, 1:], word[:, 1:], 16.0, ex_of[:, 1:], ALU.mult, ALU.add))
                    link(dve.scalar_tensor_tensor(pair_word[:], word[:, 2:BLOCKS + 2:2], 512.0,
                                                  word[:, 1:BLOCKS + 1:2], ALU.mult, ALU.add))
                    link(dve.tensor_scalar(col[12][:, 0:1], cum[:, N_EXP - 1:N_EXP], 0.5, None, ALU.mult))
                    link(tt(tmp[2][:, 4, :], col[12][:, 0:1].to_broadcast([P, BLOCKS]), tmp[2][:, 0, :], ALU.is_gt))
                    link(red(col[13][:, 0:1], tmp[2][:, 4, :], AX, ALU.add))
                    link(dve.tensor_scalar(counts[:, 0:1], col[13][:, 0:1], -2.0, None, ALU.add))
                    link(dve.tensor_copy(counts[:, 1:2], gathers[:, 0:1]))
                    link(dve.scalar_tensor_tensor(gathers[:, 0:1], col[13][:, 0:1], 16.0, gathers[:, 0:1],
                                                  ALU.mult, ALU.add))
                    for k in range(2):
                        s_, b_, p_ = col[8], col[9], col[10]
                        link(tt(t0, slots[:], onehot[k][:], ALU.mult))
                        link(red(s_, t0, AX, ALU.add))
                        link(dve.tensor_copy(slot_u[:, k, :], s_))
                        shape = [P, TILES, BLOCKS]
                        link(tt(tmp[0][:], over(s_, shape), C["thr_blk"].unsqueeze(1).to_broadcast(shape), ALU.is_ge))
                        link(red(b_, tmp[0][:], AX, ALU.add))
                        link(dve.scalar_tensor_tensor(p_, b_, -float(P), s_, ALU.mult, ALU.add))
                        link(tt(at_pos[k][:], over(p_, [P, TILES, P]),
                                C["iota"].unsqueeze(1).to_broadcast([P, TILES, P]), ALU.is_equal))
                        link(tt(tmp[0][:], over(b_, shape),
                                C["iota"][:, 0:BLOCKS].unsqueeze(1).to_broadcast(shape), ALU.is_equal))
                        link(tt(col[11], C["tokid"], C["valid"], ALU.mult))
                        link(tt(at_blk[k][:, :, 0, :], tmp[0][:], over(col[11], shape), ALU.mult))
                        ins = tt(at_blk[k][:, :, 1, :], tmp[0][:], over(col[4 + k], shape), ALU.mult)
                        if k == 0:
                            link(ins)
                    ins.then_inc(rt_places, 1)
                    dve.wait_ge(rt_maps, 1)
                    dve.tensor_copy(tokmap[:], ps[:, 2, 0:BLOCKS])
                    link(dve.tensor_copy(gatemap[:], ps[:, 2, BLOCKS:2 * BLOCKS]))

            y_saved = [sem(f"y_saved{i}") for i in range(2)]
            sp_passed, act_passed = sem("sp_passed"), sem("act_passed")
            (e_gu_in, e_dn_in, idx_ready, gu_hi_ready, gu_lo_ready, dn_hi_ready, dn_lo_ready, xt_trans, xt_hi_ready, xt_lo_ready,
             gu_ready, e_exp, e_link, hid_ready, ht_trans, ht_hi_ready, ht_lo_ready, dn_ready, y_ready) = \
                map(sem, ("e_gu_in", "e_dn_in", "idx_ready", "gu_hi_ready", "gu_lo_ready", "dn_hi_ready", "dn_lo_ready", "xt_trans",
                          "xt_hi_ready", "xt_lo_ready", "gu_ready", "e_exp", "e_link", "hid_ready", "ht_trans",
                          "ht_hi_ready", "ht_lo_ready", "dn_ready", "y_ready"))
            XT_BANK, GU_BANK, HT_BANK, DN_BANK = 0, 2, 4, 5

            def loop_turns(eng):
                return eng.value_load(counts[0:1, 0:1], min_val=MIN_BLOCKS // 2 - 2, max_val=BLOCKS // 2 - 2)

            def step_words(eng, i):
                v = eng.value_load(pair_word[0:1, ds(i, 1)], min_val=0, max_val=2 ** 18 - 1)
                return [((v >> at) & 15, (v >> (at + 4)) & 1, (v >> (at + 5)) & 15) for at in (0, 9)]

            with nc.Block() as block:
                @block.sync
                def _(sp_):
                    def load(ex, u):
                        wait_apart(sp_, gu_lo_ready, ex + 1, sp_passed)
                        sp_.wait_ge(e_gu_in, 32 * ex)
                        for j, wsrc in enumerate((w_gate, w_up)):
                            sp_.dma_start(e_raw[:, 3 * u + j, :].rearrange("p (k f) -> p k f", f=FF),
                                          wsrc[L, ds(ex, 1)].rearrange("a e (k p) f -> p (a e k) f", p=P)) \
                                .then_inc(e_gu_in, 16)
                        wait_apart(sp_, dn_lo_ready, ex + 1, sp_passed)
                        sp_.wait_ge(e_dn_in, 16 * ex)
                        sp_.dma_start(e_raw[:, 3 * u + 2, :], w_down[L, ds(ex, 1)].rearrange("a e f n -> (a e f) n")) \
                            .then_inc(e_dn_in, 16)

                    with sp_.Fori(0, N_EXP // 3) as i:
                        for u in range(3):
                            load(i * 3 + u, u)
                    for ex in range(N_EXP // 3 * 3, N_EXP):
                        load(ex, ex % 3)

                @block.gpsimd
                def _(pool):
                    def rows(b_, u):
                        wait_apart(pool, xt_trans, 2 * b_ + 2, pool_passed)
                        pool.tensor_copy(idx[u][:], tokmap[:, ds(b_, 1)]).then_inc(idx_ready, 1)
                        wait_apart(pool, idx_ready, b_ + 1, pool_passed)
                        pool.indirect_dma_start(xg[u][:], None, h1_dram, bass.IndirectOffsetOnAxis(
                            ap=idx[u][:], axis=0)).then_inc(xg_in[u], 16)

                    def down_low(ex, at):
                        wait_apart(pool, dn_hi_ready, ex + 1, pool_passed)
                        pool.tensor_tensor(dn_lo[:, ds(at * D, D)],
                                           e_raw[:, ds(3 * at + 2, 1), :].rearrange("p a n -> p (a n)"),
                                           f32(dn_hi[:, ds(at * D, D)]), ALU.subtract).then_inc(dn_lo_ready, 1)

                    def new_down_low(word):
                        ex, new, _before = word
                        with pool.If(new > 0):
                            down_low(ex + 2, (ex + 2) % 3)

                    turns = loop_turns(pool)
                    pool.sem_inc(dn_lo_ready, 3)
                    for n in range(3):
                        rows(n, n % 2)
                    down_low(0, 0)
                    down_low(1, 1)
                    rows(3, 1)
                    rows(4, 0)
                    down_low(2, 2)
                    with pool.Fori(0, turns - 1) as i:
                        words = step_words(pool, i)
                        for r in range(2):
                            rows(2 * i + 5 + r, (1 + r) % 2)
                            new_down_low(words[r])
                    rows(2 * turns + 3, 1)
                    for words in (step_words(pool, turns - 1), step_words(pool, turns)):
                        for word in words:
                            new_down_low(word)

                @block.tensor
                def _(pe):
                    turns = loop_turns(pe)
                    gathered = pe.value_load(counts[0:1, 1:2], min_val=0, max_val=(DEPTH - 1) * 16 * BLOCKS // 2)
                    pe.sem_inc(xt_trans, 4)
                    pe.sem_inc(gu_ready, 2)
                    pe.sem_inc(dn_ready, 2)

                    def rows_in(b_, u, i):
                        pe.wait_ge(xg_in[u], gathered + 16 * i + 16)
                        pe.wait_ge(xt_lo_ready, 2 * b_ + 1)
                        for j in range(2):
                            if j:
                                pe.wait_ge(xt_lo_ready, 2 * b_ + 2)
                            for k in range(4):
                                kk = 4 * j + k
                                last = pe.transpose(ps[:, XT_BANK + j, k * P:(k + 1) * P],
                                                    xg[u][:, kk * P:(kk + 1) * P], C["ident"])
                            last.then_inc(xt_trans, 1)

                    def gate_up(b_, u, ex):
                        kd = (ex % 3) * KD
                        pe.wait_ge(gu_lo_ready, ex + 4)
                        pe.wait_ge(xt_lo_ready, 2 + 2 * b_ + 2)
                        pe.wait_ge(hid_ready, b_ + 1)
                        for k in range(KD):
                            last = three_passes(pe, ps[:, GU_BANK + u, 0:2 * FF], xt_hi[u][:, k, :], xt_lo[u][:, k, :],
                                                gu_hi[:, ds(kd + k, 1), :, :], gu_lo[:, ds(kd + k, 1), :, :],
                                                k == 0, k == KD - 1)
                        last.then_inc(gu_ready, 1)

                    def hidden_in(b_, u):
                        pe.wait_ge(hid_ready, 2 + b_ + 1)
                        pe.wait_ge(ht_lo_ready, b_ + 1)
                        pe.transpose(ps[:, HT_BANK, 0:P], hid[u][:, 2, :], C["ident"]).then_inc(ht_trans, 1)

                    def down(b_, u, ex):
                        pe.wait_ge(ht_lo_ready, 1 + b_ + 1)
                        pe.wait_ge(dn_lo_ready, ex + 4)
                        pe.wait_ge(y_ready, b_ + 1)
                        for half in range(2):
                            cols = ds((ex % 3) * D + 512 * half, 512)
                            last = three_passes(pe, ps[:, DN_BANK + half, :], hid_hi[u][:], hid_lo[u][:],
                                                dn_hi[:, cols], dn_lo[:, cols], True, True)
                        last.then_inc(dn_ready, 1)

                    rows_in(0, 0, 0)
                    rows_in(1, 1, 0)
                    words = step_words(pe, 0)
                    gate_up(0, 0, words[0][2])
                    rows_in(2, 0, 1)
                    with pe.Fori(0, turns) as i:
                        words = step_words(pe, i)
                        for r in range(2):
                            b_, u = 2 * i + 1 + r, (1 + r) % 2
                            ex, _new, before_ex = words[r]
                            gate_up(b_, u, ex)
                            hidden_in(b_ - 1, 1 - u)
                            rows_in(b_ + 2, u, i + 1 + r)
                            down(b_ - 1, 1 - u, before_ex)
                    words = step_words(pe, turns) + step_words(pe, turns + 1)
                    for r in range(3):
                        b_, u = 2 * turns + 1 + r, (1 + r) % 2
                        ex, _new, before_ex = words[r]
                        gate_up(b_, u, ex)
                        hidden_in(b_ - 1, 1 - u)
                        if r == 0:
                            rows_in(b_ + 2, u, turns + 1)
                        down(b_ - 1, 1 - u, before_ex)
                    hidden_in(b_, u)
                    down(b_, u, ex)

                def xt_high(act, b_, u):
                    for j in range(2):
                        act.wait_ge(xt_trans, 4 + 2 * b_ + j + 1)
                        act.wait_ge(gu_ready, b_ + 1)
                        act.activation(xt_hi[u][:, 4 * j:4 * j + 4, :],
                                       ps[:, XT_BANK + j, :].rearrange("p (k t) -> p k t", k=4), ACT.Copy) \
                            .then_inc(xt_hi_ready, 1)

                @block.scalar
                def _(act):
                    def ht_high(b_, u):
                        act.wait_ge(ht_trans, b_ + 1)
                        act.wait_ge(dn_ready, b_ + 1)
                        act.activation(hid_hi[u][:], ps[:, HT_BANK, 0:P], ACT.Copy).then_inc(ht_hi_ready, 1)

                    def gate_up_high(ex, par, b_):
                        act.wait_ge(e_gu_in, 32 * ex + 32)
                        act.wait_ge(gu_ready, 2 + b_)
                        for j in range(2):
                            last = act.activation(gu_hi[:, ds(par * KD, KD), j, :],
                                                  e_raw[:, ds(3 * par + j, 1), :]
                                                  .rearrange("p a (k f) -> p (a k) f", f=FF), ACT.Copy)
                            last.then_inc(gu_hi_ready, 1)

                    def down_high(ex, par, b_):
                        act.wait_ge(e_dn_in, 16 * ex + 16)
                        act.wait_ge(dn_ready, 2 + b_)
                        act.activation(dn_hi[:, ds(par * D, D)],
                                       e_raw[:, ds(3 * par + 2, 1), :].rearrange("p a n -> p (a n)"), ACT.Copy) \
                            .then_inc(dn_hi_ready, 1)

                    def gate_exp(b_, u):
                        act.wait_ge(gu_ready, 2 + b_ + 1)
                        act.activation(hid[u][:, 0, :], ps[:, GU_BANK + u, 0:FF], ACT.Exp, scale=-1.0) \
                            .then_inc(e_exp, 1)

                    def y_take(b_, u, i):
                        act.wait_ge(dn_ready, 2 + b_ + 1)
                        act.wait_ge(y_saved[u], 16 * i + 16)
                        act.activation(y_out[u][:], ps[:, DN_BANK:DN_BANK + 2, :].rearrange("p a n -> p (a n)"),
                                       ACT.Copy).then_inc(y_ready, 1)
                        act.wait_ge(y_ready, 1 + b_ + 1)
                        act.dma_start(y_dram[ds(b_ * P, P), :], y_out[u][:]).then_inc(y_saved[u], 16)

                    act.wait_ge(pre["y_filled"], 16 * -(-(BLOCKS - MIN_BLOCKS) // XT))
                    turns = loop_turns(act)
                    for u in range(2):
                        act.sem_inc(y_saved[u], 16)
                    act.sem_inc(y_ready, 1)
                    xt_high(act, 0, 0)
                    gate_up_high(0, 0, 0)
                    xt_high(act, 1, 1)
                    down_high(0, 0, 0)
                    gate_up_high(1, 1, 0)
                    down_high(1, 1, 0)
                    gate_exp(0, 0)
                    xt_high(act, 2, 0)
                    gate_up_high(2, 2, 0)
                    down_high(2, 2, 0)

                    def step(b_, u, i, word, more):
                        ex, new, _before = word
                        gate_exp(b_, u)
                        ht_high(b_ - 1, 1 - u)
                        if more:
                            xt_high(act, b_ + 2, u)
                        with act.If(new > 0):
                            gate_up_high(ex + 2, (ex + 2) % 3, b_)
                        y_take(b_ - 1, 1 - u, i)
                        with act.If(new > 0):
                            down_high(ex + 2, (ex + 2) % 3, b_)

                    with act.Fori(0, turns) as i:
                        words = step_words(act, i)
                        for r in range(2):
                            step(2 * i + 1 + r, (1 + r) % 2, i, words[r], True)
                    words = step_words(act, turns)
                    step(2 * turns + 1, 1, turns, words[0], True)
                    step(2 * turns + 2, 0, turns, words[1], False)
                    b_, u, i = 2 * turns + 3, 1, turns + 1
                    gate_exp(b_, u)
                    ht_high(b_ - 1, 1 - u)
                    y_take(b_ - 1, 1 - u, i)
                    ht_high(b_, u)
                    y_take(b_, u, i)
                    for u in range(2):
                        wait_apart(act, y_saved[u], 16 * turns + 48, act_passed)

                @block.vector
                def _(dve):
                    def xt_low(b_, u):
                        for j in range(2):
                            dve.wait_ge(xt_hi_ready, 2 * b_ + j + 1)
                            part = slice(4 * j, 4 * j + 4)
                            dve.tensor_tensor(xt_lo[u][:, part, :], ps[:, XT_BANK + j, :].rearrange("p (k t) -> p k t", k=4),
                                              f32(xt_hi[u][:, part, :]), ALU.subtract).then_inc(xt_lo_ready, 1)

                    def ht_low(b_, u):
                        dve.wait_ge(ht_hi_ready, b_ + 1)
                        dve.tensor_tensor(hid_lo[u][:], ps[:, HT_BANK, 0:P], f32(hid_hi[u][:]), ALU.subtract) \
                            .then_inc(ht_lo_ready, 1)

                    def gate_up_low(ex, par):
                        for j in range(2):
                            dve.wait_ge(gu_hi_ready, 2 * ex + j + 1)
                            last = dve.tensor_tensor(gu_lo[:, ds(par * KD, KD), j, :],
                                                     e_raw[:, ds(3 * par + j, 1), :]
                                                     .rearrange("p a (k f) -> p (a k) f", f=FF),
                                                     f32(gu_hi[:, ds(par * KD, KD), j, :]), ALU.subtract)
                        last.then_inc(gu_lo_ready, 1)

                    def hidden(b_, u):
                        link = Link(dve, e_link, 3 * b_)
                        dve.wait_ge(e_exp, b_ + 1)
                        link(dve.tensor_scalar(hid[u][:, 1, :], hid[u][:, 0, :], 1.0, None, ALU.add))
                        link(dve.reciprocal(hid[u][:, 0, :], hid[u][:, 1, :]))
                        link(dve.tensor_tensor(hid[u][:, 1, :], ps[:, GU_BANK + u, 0:FF], hid[u][:, 0, :], ALU.mult))
                        dve.scalar_tensor_tensor(hid[u][:, 2, :], ps[:, GU_BANK + u, FF:2 * FF],
                                                 gatemap[:, ds(b_, 1)], hid[u][:, 1, :], ALU.mult, ALU.mult) \
                            .then_inc(hid_ready, 1)

                    turns = loop_turns(dve)
                    dve.sem_inc(gu_lo_ready, 3)
                    dve.sem_inc(xt_lo_ready, 2)
                    dve.sem_inc(hid_ready, 2)
                    dve.sem_inc(ht_lo_ready, 1)
                    xt_low(0, 0)
                    gate_up_low(0, 0)
                    xt_low(1, 1)
                    gate_up_low(1, 1)
                    hidden(0, 0)
                    xt_low(2, 0)
                    gate_up_low(2, 2)

                    def step(b_, u, word, more):
                        ex, new, _before = word
                        ht_low(b_ - 1, 1 - u)
                        hidden(b_, u)
                        if more:
                            xt_low(b_ + 2, u)
                        with dve.If(new > 0):
                            gate_up_low(ex + 2, (ex + 2) % 3)

                    with dve.Fori(0, turns) as i:
                        words = step_words(dve, i)
                        for r in range(2):
                            step(2 * i + 1 + r, (1 + r) % 2, words[r], True)
                    words = step_words(dve, turns)
                    step(2 * turns + 1, 1, words[0], True)
                    step(2 * turns + 2, 0, words[1], False)
                    b_, u = 2 * turns + 3, 1
                    ht_low(b_ - 1, 1 - u)
                    hidden(b_, u)
                    ht_low(b_, u)

            f_in = [sem(f"f_in{i}") for i in range(3)]
            f_saved = [sem(f"f_saved{i}") for i in range(3)]
            (f_ln_in, f_idx, f_link, f_summed, f_var, f_rstd, f_scaled, f_normed, f_trans, f_hi, f_lo) = map(sem, (
                "f_ln_in", "f_idx", "f_link", "f_summed", "f_var", "f_rstd", "f_scaled", "f_normed", "f_trans",
                "f_hi", "f_lo"))

            with nc.Block() as block:
                @block.sync
                def _(sp_):
                    sp_.dma_start(ln_g[:], ln2_g[L].to_broadcast([P, D])).then_inc(f_ln_in, 16)
                    sp_.dma_start(ln_b[:], ln2_b[L].to_broadcast([P, D])).then_inc(f_ln_in, 16)
                    with sp_.Fori(0, TILES // 3) as i:
                        for r in range(3):
                            n = 3 * i + r
                            sp_.wait_ge(f_scaled, n + 1)
                            sp_.dma_start(res[r][:], h1_dram[ds(n * P, P), :]).then_inc(f_in[r], 16)

                @block.gpsimd
                def _(pool):
                    pool.wait_ge(f_ln_in, 32)

                    def gather(n, r):
                        wait_apart(pool, f_summed, n + 1, pool_passed)
                        pool.tensor_copy(f_idx_t[r][:, 0:1], slot_u[:, 0, ds(n, 1)])
                        pool.tensor_copy(f_idx_t[r][:, 1:2], slot_u[:, 1, ds(n, 1)]).then_inc(f_idx, 1)
                        wait_apart(pool, f_idx, n + 1, pool_passed)
                        for k, y in enumerate((y_a, y_b)):
                            pool.indirect_dma_start(y[r][:], None, y_dram, bass.IndirectOffsetOnAxis(
                                ap=f_idx_t[r][:, k:k + 1], axis=0)).then_inc(fy_in[r], 16)

                    def finish(n, r):
                        pool.wait_ge(f_var, n + 1)
                        pool.tensor_tensor(stat[:, r, 15:16], stat[:, r, 14:15], C["half"], ALU.pow).then_inc(f_rstd, 1)
                        pool.wait_ge(f_scaled, 3 + n + 1)
                        pool.tensor_tensor(nrm[r][:], nrm[r][:], ln_b[:], ALU.add).then_inc(f_normed, 1)

                    gather(0, 0)
                    gather(1, 1)
                    with pool.Fori(0, TILES // 3 - 1) as i:
                        for r in range(3):
                            gather(3 * i + r + 2, (r + 2) % 3)
                            finish(3 * i + r, r)
                    gather(TILES - 1, 2)
                    for r in range(3):
                        finish(TILES - 3 + r, r)

                @block.tensor
                def _(pe):
                    pe.sem_inc(f_trans, 6)
                    with pe.Fori(0, TILES // 3) as i:
                        for r in range(3):
                            n = 3 * i + r
                            pe.wait_ge(f_normed, n + 1)
                            pe.wait_ge(f_lo, 2 * n + 2)
                            for j in range(2):
                                for k in range(4):
                                    kk = 4 * j + k
                                    last = pe.transpose(ps[:, 2 * r + j, k * P:(k + 1) * P],
                                                        nrm[r][:, kk * P:(kk + 1) * P], C["ident"])
                                last.then_inc(f_trans, 1)

                @block.scalar
                def _(act):
                    for r in range(3):
                        act.sem_inc(f_saved[r], 32)
                    act.wait_ge(f_ln_in, 32)

                    def tile(n, r, with_out):
                        act.wait_ge(f_normed, n + 1)
                        act.dma_start(h_dram[ds(n * P, P), :], nrm[r][:]).then_inc(f_saved[r], 16)
                        if with_out:
                            act.dma_start(out[0, ds(n * P, P), :], nrm[r][:]).then_inc(f_saved[r], 16)
                        for j in range(2):
                            act.wait_ge(f_trans, 6 + 2 * n + j + 1)
                            act.activation(act_hi[:, 4 * j:4 * j + 4, ds(n * P, P)],
                                           ps[:, 2 * r + j, :].rearrange("p (k t) -> p k t", k=4), ACT.Copy) \
                                .then_inc(f_hi, 1)

                    with act.Fori(0, TILES // 3 - 1) as i:
                        for r in range(3):
                            tile(3 * i + r, r, True)
                    for n in range(TILES - 3, TILES):
                        tile(n, n % 3, n < XT)
                    for r in range(3):
                        act.wait_ge(f_saved[r], 32 + 32 * TILES // 3 - 16 * (r == XT % 3))
                    act.wait_ge(f_hi, 2 * TILES)

                @block.vector
                def _(dve):
                    dve.sem_inc(f_summed, 3)
                    dve.sem_inc(f_scaled, 3)
                    dve.sem_inc(f_lo, 6)
                    dve.wait_ge(f_ln_in, 32)
                    with dve.Fori(0, TILES // 3) as i:
                        link = Link(dve, f_link, 15 * i)
                        for r in range(3):
                            n = 3 * i + r
                            dve.wait_ge(fy_in[r], layer * (32 * TILES // 3) + 32 * i + 32)
                            dve.tensor_tensor(y_a[r][:], y_a[r][:], y_b[r][:], ALU.add).then_inc(f_summed, 1)
                            dve.wait_ge(f_in[r], 16 * i + 16)
                            dve.wait_ge(f_summed, 3 + n + 1)
                            link(dve.scalar_tensor_tensor(res[r][:], res[r][:], ALPHA, y_a[r][:], ALU.mult, ALU.add))
                            norm_statistics(dve, link, res[r], stat[:, r, :], f_var)
                            dve.wait_ge(f_rstd, n + 1)
                            dve.wait_ge(f_saved[r], 32 * i + 32)
                            dve.wait_ge(f_trans, 2 * n + 2)
                            link(dve.tensor_scalar(nrm[r][:], res[r][:], stat[:, r, 12:13], stat[:, r, 15:16],
                                                   ALU.subtract, ALU.mult))
                            dve.tensor_tensor(nrm[r][:], nrm[r][:], ln_g[:], ALU.mult).then_inc(f_scaled, 1)
                            for j in range(2):
                                dve.wait_ge(f_hi, 2 * n + j + 1)
                                dve.tensor_tensor(act_lo[:, 4 * j:4 * j + 4, ds(n * P, P)],
                                                  ps[:, 2 * r + j, :].rearrange("p (k t) -> p k t", k=4),
                                                  f32(act_hi[:, 4 * j:4 * j + 4, ds(n * P, P)]), ALU.subtract) \
                                    .then_inc(f_lo, 1)

            nc.all_engine_barrier()
            nc.gpsimd.sem_clear(range(layer_sems[0].num, layer_sems[-1].num + 1))
            nc.all_engine_barrier()


_INS = ["x", "meta_tokens", "w_in", "conv_w", "lambda_q1", "lambda_k1", "lambda_q2", "lambda_k2", "diff_norm_g",
        "w_out", "ln1_g", "ln1_b", "router_w", "router_bias", "w_gate", "w_up", "w_down", "ln2_g", "ln2_b"]


def kernel(**inputs):
    import numpy as _np
    import concourse.bacc as _bacc
    from concourse import mybir as _mybir
    from concourse.bass_utils import run_bass_kernel_spmd as _run

    nc = _bacc.Bacc("TRN2", target_bir_lowering=False, num_devices=1)
    arrays, args = {}, []
    given = {name: inputs[name] for name in _INS}
    given["conv_w"] = _np.asarray(inputs["conv_w"]).reshape(DEPTH, 3, CONV_TILES, P).transpose(0, 3, 2, 1) \
        .reshape(DEPTH, P, CONV_TILES * 3)
    given.update(consts=shape_constants(), rope=rope_constants(), lam_consts=layer_constants())
    for name, value in given.items():
        a = _np.ascontiguousarray(value)
        arrays[f"in_{name}_dram"] = a
        args.append(nc.dram_tensor(f"in_{name}_dram", a.shape, _mybir.dt.from_np(a.dtype), kind="ExternalInput").ap())
    args.append(nc.dram_tensor("out_0_dram", (1, SEQ, D), _mybir.dt.float32, kind="ExternalOutput").ap())
    build_trunk(nc, *args)
    r = _run(nc, [arrays], core_ids=[0])
    return r.results[0]["out_0_dram"]
```

```python
import math
from contextlib import ExitStack

import numpy as np

import concourse.bass as bass
from concourse import mybir

F32 = mybir.dt.float32
F32R = mybir.dt.float32r
BF16 = mybir.dt.bfloat16
I32 = mybir.dt.int32
U32 = mybir.dt.uint32
ALU = mybir.AluOpType
ACT = mybir.ActivationFunctionType
AX = mybir.AxisListType.X
ds = bass.ds

P = 128
D = 1024
KD = D // P
SEQ = 1024
N_META = 16
TOK = SEQ + N_META
TILES = -(-TOK // P)
ROWS = TILES * P
XT = SEQ // P
META0 = SEQ
DEPTH = 2
IN_COLS = 3072
HD = 64
QKV_TILES = 12
CONV_TILES = 4
CONV0 = QKV_TILES * P
CONV_W = CONV_TILES * P
SB_Q, SB_K, SB_V, DF_Q, DF_K, DF_V = range(0, 12, 2)
SUB = 32
ROPE = 8
N_EXP = 16
N_GRP = 4
FF = 128
BLOCKS = N_EXP + (2 * TOK - N_EXP) // P
MIN_BLOCKS = 2 * -(-2 * TOK // (2 * P))
ALPHA = (2.0 * DEPTH) ** 0.25
EPS = 1e-5
NEG = -1e30
SB_SCALE = HD ** -0.5
DF_SCALE = SUB ** -0.5

CHUNKS = [(0, 348), (348, 694), (694, TOK)]

CONST_COLS = dict(ident=P, suffix=P, prefix=P, ones=P, rotate=P, negmask=P + 4, iota=P, tokid=TILES,
                  valid=TILES, prio16=16, prio4=4, thr=TILES, thr_blk=BLOCKS, half=1)


def const_slices():
    at, out = 0, {}
    for name, n in CONST_COLS.items():
        out[name] = slice(at, at + n)
        at += n
    return out, at


def shape_constants():
    where, total = const_slices()
    c = np.zeros((P, total), np.float32)
    r = np.arange(P)
    c[:, where["ident"]] = np.eye(P)
    c[:, where["suffix"]] = r[:, None] >= r[None, :]
    c[:, where["prefix"]] = r[:, None] < r[None, :]
    c[:, where["ones"]] = 1.0
    rot = np.zeros((P, P), np.float32)
    for p in range(P):
        j = p % SUB
        if j < ROPE // 2:
            rot[p + ROPE // 2, p] = -1.0
        elif j < ROPE:
            rot[p - ROPE // 2, p] = 1.0
    c[:, where["rotate"]] = rot
    neg = np.full((P, P + 4), NEG, np.float32)
    neg[:, :P] = np.where(r[None, :] <= r[:, None], 0.0, NEG)
    c[:, where["negmask"]] = neg
    c[:, where["iota"]] = r[None, :]
    tok = np.arange(TILES)[None, :] * P + r[:, None]
    c[:, where["tokid"]] = tok
    c[:, where["valid"]] = tok < TOK
    c[:, where["prio16"]] = 16 - np.arange(16)
    c[:, where["prio4"]] = 4 - np.arange(4)
    c[:, where["thr"]] = np.arange(TILES) * P
    c[:, where["thr_blk"]] = (np.arange(BLOCKS) + 1) * P
    c[:, where["half"]] = -0.5
    return c


def rope_constants():
    pos = np.concatenate([np.arange(SEQ) + N_META, np.arange(N_META)]).astype(np.float32)
    inv = (500000.0 ** (-np.arange(0, ROPE, 2) / ROPE)).astype(np.float32)
    ang = (pos[None, :] * inv[:, None]).astype(np.float32).astype(np.float64)
    cos, sin = np.ones((P, TOK)), np.zeros((P, TOK))
    for p in range(P):
        j = p % SUB
        if j < ROPE:
            cos[p], sin[p] = np.cos(ang[j % (ROPE // 2)]), np.sin(ang[j % (ROPE // 2)])
    return np.stack([cos, sin]).astype(np.float32)


def layer_constants():
    lam = [0.8 - 0.6 * math.exp(-0.3 * l) for l in range(DEPTH)]
    return np.array([[v, 1.0 - v] for v in lam], np.float32)


def row_pieces(i):
    if i == XT:
        return 1, N_META
    keys = N_META + (i + 1) * P
    n = -(-keys // 512)
    w = -(-keys // n)
    return n, w + w % 2


DIFF_ROWS = [XT] + list(range(XT))
DIFF_KEYS = max(n * w for n, w in map(row_pieces, DIFF_ROWS))


def key_tiles(i):
    out = [(XT, 0, N_META)]
    if i < XT:
        out += [(n, N_META + n * P, P) for n in range(i + 1)]
    return out


def sb_steps():
    out = []
    for first_tile in (4, 0):
        for n in list(range(first_tile + 3, -1, -1)) + [XT]:
            lo = max(0, n - first_tile) * P if n < XT else 0
            out.append(dict(tile0=first_tile, lo=lo, hi=512, key=n,
                            diag=n < XT and n >= first_tile,
                            first=n == first_tile + 3, last=n == XT))
    out.append(dict(tile0=XT, lo=0, hi=P, key=XT, diag=True, first=True, last=True))
    return out


SB_STEPS = [dict(s, head=h) for s in sb_steps() for h in range(2)]


class Map:

    def __init__(self, nc, at, end):
        self.nc, self.at, self.end = nc, at, end

    def put(self, name, shape, dt, size=4):
        n = size
        for s in shape[1:]:
            n *= s
        t = self.nc.alloc_sbuf_tensor_at(name, shape, dt, offset=self.at)
        self.at += (n + 31) // 32 * 32
        assert self.at <= self.end, (name, self.at, self.end)
        return t


def f32(ap):
    return ap.bitcast(F32)


def wait_apart(eng, sem, value, passed):
    eng.wait_ge(sem, value)
    eng.sem_inc(passed, 1)


class Link:

    def __init__(self, eng, sem, base=0):
        self.eng, self.sem, self.base, self.n = eng, sem, base, 0

    def __call__(self, ins):
        self.n += 1
        ins.then_inc(self.sem, 1)
        self.eng.wait_ge(self.sem, self.base + self.n)


def three_passes(pe, out, stat_hi, stat_lo, mov_hi, mov_lo, start, stop):
    pe.matmul(out, stat_lo, mov_hi, start=start, stop=False)
    pe.matmul(out, stat_hi, mov_lo, start=False, stop=False)
    return pe.matmul(out, stat_hi, mov_hi, start=False, stop=stop)


def build_trunk(nc, x, meta_tokens, w_in, conv_w, lambda_q1, lambda_k1, lambda_q2, lambda_k2,
                diff_norm_g, w_out, ln1_g, ln1_b, router_w, router_bias, w_gate, w_up, w_down,
                ln2_g, ln2_b, consts, rope, lam_consts, out):
    h_dram = nc.dram_tensor("h_rows", [ROWS, D], F32, kind="Internal").ap()
    h1_dram = nc.dram_tensor("h1_rows", [ROWS, D], F32, kind="Internal").ap()
    y_dram = nc.dram_tensor("y_slots", [BLOCKS * P, D], F32, kind="Internal").ap()

    ctx = ExitStack()
    with ctx:
        base = (nc.sbuf_base + 63) // 64 * 64
        end = nc.sbuf_usable_end
        m = Map(nc, base, end)
        where, n_const = const_slices()
        cst = m.put("cst", [P, n_const], F32)
        C = {k: cst[:, v] for k, v in where.items()}
        suffix = m.put("suffix", [P, P], F32R)
        prefix = m.put("prefix", [P, P], F32R)
        ident_bf = m.put("ident_bf", [P, P], BF16, 2)
        negmask_bf = m.put("negmask_bf", [P, P + 4], BF16, 2)
        router = m.put("router", [P, KD, N_EXP], F32)
        rbias = m.put("rbias", [P, N_EXP], F32)
        logits = m.put("logits", [P, TILES, N_EXP], F32)
        slot_u = m.put("slot_u", [P, 2, TILES], U32)
        tokmap = m.put("tokmap", [P, BLOCKS], U32)
        gatemap = m.put("gatemap", [P, BLOCKS], F32)
        idx = [m.put(f"idx{i}", [P, 1], U32) for i in range(2)]
        f_idx_t = [m.put(f"f_idx_t{i}", [P, 2], U32) for i in range(3)]
        pair_word = m.put("pair_word", [P, BLOCKS // 2], I32)
        counts = m.put("counts", [P, 2], I32)
        gathers = m.put("gathers", [P, 2], F32)
        stat = m.put("stat", [P, 3, 16], F32)
        m.at = (m.at + 63) // 64 * 64
        at0 = m.at
        act_hi = m.put("act_hi", [P, KD, ROWS], F32R)
        act_lo = m.put("act_lo", [P, KD, ROWS], F32R)
        under = m.at

        x_rows = Map(nc, under, end).put("x_rows", [P, TILES, D], F32)

        a = Map(nc, under, end)
        qkv = a.put("qkv", [P, QKV_TILES, TOK], F32)
        conv_y = a.put("conv_y", [P, CONV_TILES, TOK], F32)
        after_qkv = behind_conv = a.at
        w_raw = [a.put(f"w_raw{b}", [P, KD, P], F32) for b in range(3)]
        w_hi = [a.put(f"w_hi{b}", [P, KD, P], F32R) for b in range(3)]
        w_lo = [a.put(f"w_lo{b}", [P, KD, P], F32R) for b in range(3)]
        gate_b = a.put("gate_b", [P, TOK], F32)
        gate_c = a.put("gate_c", [P, TOK], F32)
        conv_u = a.put("conv_u", [P, TOK + 2], F32)
        conv_t = a.put("conv_t", [P, TOK], F32)
        taps = a.put("taps", [P, CONV_TILES, 3], F32)

        b = Map(nc, after_qkv, end)
        v_rows = b.put("v_rows", [P, TILES, 512], F32)
        y_sb = b.put("y_sb", [P, TILES, 256], F32)
        y_df = b.put("y_df", [P, TILES, 256], F32)
        q_hi_at = b.at
        q_hi = b.put("q_hi", [P, ROWS], F32R)
        q_lo = b.put("q_lo", [P, ROWS], F32R)
        lam_in = b.put("lam_in", [P, 4, SUB], F32)
        lam = b.put("lam", [P, 8], F32)
        norm_g = b.put("norm_g", [P, HD], F32)
        t = Map(nc, at0, under)
        k_hi = t.put("k_hi", [P, ROWS], F32R)
        k_lo = t.put("k_lo", [P, ROWS], F32R)
        after_k = t.at
        zs = [t.put(f"zs{i}", [P, 512], F32) for i in range(6)]
        ez = [t.put(f"ez{i}", [P, 512], F32) for i in range(2)]
        sp = [t.put(f"sp{i}", [P, 512], F32) for i in range(4)]
        sp_hi = [t.put(f"sp_hi{i}", [P, 512], F32R) for i in range(6)]
        sp_lo = [t.put(f"sp_lo{i}", [P, 512], F32R) for i in range(6)]
        wt = [t.put(f"wt{i}", [P, 512], F32) for i in range(4)]
        t = Map(nc, after_k, under)
        prob = [[t.put(f"prob{u}{s}", [P, DIFF_KEYS], F32) for s in range(2)] for u in range(2)]
        a_t = [t.put(f"a_t{u}", [P, TILES, P], F32) for u in range(2)]
        df_stat = [t.put(f"df_stat{u}", [P, 16], F32) for u in range(4)]
        after_norm_g = b.at
        cos_t = b.put("cos_t", [P, TOK], F32)
        sin_t = b.put("sin_t", [P, TOK], F32)
        rot_a = b.put("rot_a", [P, TOK], F32)
        rot_b = b.put("rot_b", [P, TOK], F32)
        t = Map(nc, q_hi_at, after_norm_g)
        sq = t.put("sq", [P, TILES * 4, HD], F32)
        t = Map(nc, after_norm_g, end)
        ms = t.put("ms", [P, TILES * 4], F32)
        rms = t.put("rms", [P, TILES * 4], F32)
        behind_rms = t.at

        c = Map(nc, under, end)
        wo_hi = c.put("wo_hi", [P, KD, D], F32R)
        wo_lo = c.put("wo_lo", [P, KD, D], F32R)
        after_wo = c.at
        c.at = max(c.at, behind_conv)
        wo_raw = [c.put(f"wo_raw{i}", [P, D], F32) for i in range(2)]
        ln_g = c.put("ln_g", [P, D], F32)
        ln_b = c.put("ln_b", [P, D], F32)
        res = [c.put(f"res{i}", [P, D], F32) for i in range(3)]
        nrm = [c.put(f"nrm{i}", [P, D], F32) for i in range(3)]
        h1_t = c.put("h1_t", [P, KD, P], F32)
        ahead = Map(nc, behind_rms, end)
        wo_raw = wo_raw + [ahead.put(f"wo_ahead{i}", [P, D], F32) for i in range(4)] + res[0:2]
        f = Map(nc, under, after_wo)
        y_a = [f.put(f"y_a{i}", [P, D], F32) for i in range(3)]
        y_b = [f.put(f"y_b{i}", [P, D], F32) for i in range(3)]

        d = Map(nc, at0, under)
        sel = d.put("sel", [P, TILES, N_EXP], F32)
        prb = d.put("prb", [P, TILES, N_EXP], F32)
        tmp = [d.put(f"tmp{i}", [P, TILES, BLOCKS], F32) for i in range(3)]
        pair = d.put("pair", [P, TILES * N_GRP, 6], F32)
        small = d.put("small", [P, 16, TILES, N_GRP], F32)
        onehot = [d.put(f"onehot{i}", [P, TILES, N_EXP], F32) for i in range(2)]
        member = d.put("member", [P, TILES, N_EXP], F32)
        before = d.put("before", [P, TILES + 1, N_EXP], F32)
        slots = d.put("slots", [P, TILES, N_EXP], F32)
        blk = d.put("blk", [P, 8, N_EXP], F32)
        cnt_ge = d.put("cnt_ge", [P, N_EXP, BLOCKS], F32)
        at_pos = [d.put(f"at_pos{i}", [P, TILES, P], F32) for i in range(2)]
        at_blk = [d.put(f"at_blk{i}", [P, TILES, 2, BLOCKS], F32) for i in range(2)]

        e = Map(nc, under, end)
        e_raw = e.put("e_raw", [P, 3 * 3, D], F32)
        gu_hi = e.put("gu_hi", [P, 3 * KD, 2, FF], F32R)
        gu_lo = e.put("gu_lo", [P, 3 * KD, 2, FF], F32R)
        dn_hi = e.put("dn_hi", [P, 3 * D], F32R)
        dn_lo = e.put("dn_lo", [P, 3 * D], F32R)
        y_out = [e.put(f"y_out{i}", [P, D], F32) for i in range(2)]
        e = Map(nc, at0, under)
        xg = [e.put(f"xg{i}", [P, D], F32) for i in range(2)]
        xt_hi = [e.put(f"xt_hi{i}", [P, KD, P], F32R) for i in range(2)]
        xt_lo = [e.put(f"xt_lo{i}", [P, KD, P], F32R) for i in range(2)]
        hid = [e.put(f"hid{i}", [P, 3, FF], F32) for i in range(2)]
        hid_hi = [e.put(f"hid_hi{i}", [P, P], F32R) for i in range(2)]
        hid_lo = [e.put(f"hid_lo{i}", [P, P], F32R) for i in range(2)]

        ps = ctx.enter_context(nc.psum_tensor("ps", [P, 8, 512], F32))

        pre = {n: ctx.enter_context(nc.semaphore("pre_" + n)) for n in
               ("const", "vec", "trans", "hi", "lo", "h_saved", "y_filled", "pad")
               + tuple(f"tile{n}" for n in range(3))}
        xg_in = [ctx.enter_context(nc.semaphore(f"xg_in{i}")) for i in range(2)]
        fy_in = [ctx.enter_context(nc.semaphore(f"fy_in{i}")) for i in range(3)]
        layer_sems = []

        def sem(name):
            s = ctx.enter_context(nc.semaphore(name))
            layer_sems.append(s)
            return s

        with nc.Block() as block:
            @block.sync
            def _(sp_):
                sp_.dma_start(cst[:], consts).then_inc(pre["const"], 16)
                sp_.dma_start(router[:], router_w.rearrange("(k p) e -> p k e", p=P)).then_inc(pre["const"], 16)
                sp_.dma_start(rbias[:], router_bias.rearrange("(a e) -> a e", a=1).to_broadcast([P, N_EXP])) \
                    .then_inc(pre["const"], 16)
                for n in range(XT):
                    if n >= 3:
                        sp_.wait_ge(pre[f"tile{n % 3}"], 16 * (n // 3))
                    sp_.dma_start(x_rows[:, n, :], x[0, n * P:(n + 1) * P, :]).then_inc(pre[f"tile{n % 3}"], 16)
                sp_.wait_ge(pre["pad"], 1)
                sp_.wait_ge(pre[f"tile{XT % 3}"], 16 * (XT // 3))
                sp_.dma_start(x_rows[0:N_META, XT, :], meta_tokens).then_inc(pre[f"tile{XT % 3}"], 16)
                sp_.wait_ge(pre[f"tile{XT % 3}"], 16 * (XT // 3 + 1))
                sp_.dma_start(h_dram[XT * P:ROWS, :], x_rows[:, XT, :]).then_inc(pre["h_saved"], 16)

            @block.gpsimd
            def _(pool):
                pool.memset(x_rows[:, XT, :], 0.0).then_inc(pre["pad"], 1)

            @block.scalar
            def _(act):
                act.preload_act_table_set("natural_log_exp_and_others")
                for n in range(TILES):
                    for j in range(2):
                        act.wait_ge(pre["trans"], 2 * n + j + 1)
                        act.activation(act_hi[:, 4 * j:4 * j + 4, n * P:(n + 1) * P],
                                       ps[:, 2 * (n % 4) + j, :].rearrange("p (k t) -> p k t", k=4),
                                       ACT.Copy).then_inc(pre["hi"], 1)
                act.dma_start(h_dram[0:XT * P, :], x[0]).then_inc(pre["h_saved"], 16)

            @block.vector
            def _(dve):
                dve.wait_ge(pre["const"], 48)
                dve.memset(gathers[:], 0.0)
                dve.tensor_copy(suffix[:], C["suffix"]).then_inc(pre["vec"], 1)
                dve.tensor_copy(prefix[:], C["prefix"]).then_inc(pre["vec"], 1)
                dve.tensor_copy(ident_bf[:], C["ident"]).then_inc(pre["vec"], 1)
                dve.tensor_copy(negmask_bf[:], C["negmask"]).then_inc(pre["vec"], 1)
                for n in range(TILES):
                    for j in range(2):
                        dve.wait_ge(pre["hi"], 2 * n + j + 1)
                        dve.tensor_tensor(act_lo[:, 4 * j:4 * j + 4, n * P:(n + 1) * P],
                                          ps[:, 2 * (n % 4) + j, :].rearrange("p (k t) -> p k t", k=4),
                                          f32(act_hi[:, 4 * j:4 * j + 4, n * P:(n + 1) * P]),
                                          ALU.subtract).then_inc(pre["lo"], 1)

            @block.tensor
            def _(pe):
                pe.wait_ge(pre["const"], 48)
                for n in range(TILES):
                    pe.wait_ge(pre[f"tile{n % 3}"], 16 * (n // 3 + 1))
                    if n >= 4:
                        pe.wait_ge(pre["lo"], 2 * (n - 4) + 2)
                    for j in range(2):
                        for k in range(4):
                            last = pe.transpose(ps[:, 2 * (n % 4) + j, k * P:(k + 1) * P],
                                                x_rows[:, n, (4 * j + k) * P:(4 * j + k + 1) * P], C["ident"])
                        last.then_inc(pre["trans"], 1)


        pool_passed, dve_passed, pe_passed = sem("pool_passed"), sem("dve_passed"), sem("pe_passed")

        with nc.Fori(0, DEPTH) as layer:
            L = ds(layer, 1)

            w_loaded = [sem(f"w_loaded{i}") for i in range(3)]
            acc_taken = [sem(f"acc_taken{i}") for i in range(3)]
            w_hi_ready, w_lo_ready, acc_ready, conv_done, conv_link, taps_in = map(sem, (
                "w_hi_ready", "w_lo_ready", "acc_ready", "conv_done", "conv_link", "taps_in"))
            with nc.Block() as block:
                @block.sync
                def _(sp_):
                    sp_.dma_start(taps[:], conv_w[L].rearrange("a p (j t) -> p (a j) t", t=3)).then_inc(taps_in, 16)

                    def load(tile, r, col):
                        sp_.wait_ge(w_lo_ready, tile + 1)
                        sp_.dma_start(w_raw[r][:], w_in[L, :, ds(col, P)].rearrange(
                            "a (k p) c -> p (a k) c", p=P)).then_inc(w_loaded[r], 16)

                    with sp_.Fori(0, QKV_TILES // 3) as i:
                        for r in range(3):
                            load(3 * i + r, r, (3 * i + r) * P)
                    with sp_.Fori(0, CONV_TILES) as j:
                        for r in range(3):
                            load(QKV_TILES + 3 * j + r, r, CONV0 + r * CONV_W + j * P)

                @block.gpsimd
                def _(pool):
                    pool.sem_inc(w_lo_ready, 3)
                    with pool.Fori(0, (QKV_TILES + 3 * CONV_TILES) // 3) as i:
                        for r in range(3):
                            tile = 3 * i + r
                            wait_apart(pool, acc_ready, 3 * tile + 3, pool_passed)
                            wait_apart(pool, w_loaded[r], 16 * (i + 1), pool_passed)
                            pool.tensor_copy(w_hi[r][:], w_raw[r][:]).then_inc(w_hi_ready, 1)
                            pool.wait_ge(w_hi_ready, tile + 1)
                            pool.tensor_tensor(w_lo[r][:], w_raw[r][:], f32(w_hi[r][:]), ALU.subtract) \
                                .then_inc(w_lo_ready, 1)

                @block.tensor
                def _(pe):
                    pe.sem_inc(acc_ready, 9)
                    with pe.Fori(0, (QKV_TILES + 3 * CONV_TILES) // 3) as i:
                        for r in range(3):
                            tile = 3 * i + r
                            pe.wait_ge(w_lo_ready, 3 + tile + 1)
                            for n, (c0, c1) in enumerate(CHUNKS):
                                pe.wait_ge(acc_taken[n], tile + 1)
                                for k in range(KD):
                                    last = three_passes(pe, ps[:, n, 0:c1 - c0], w_hi[r][:, k, :],
                                                        w_lo[r][:, k, :], act_hi[:, k, c0:c1],
                                                        act_lo[:, k, c0:c1], k == 0, k == KD - 1)
                                last.then_inc(acc_ready, 1)

                @block.scalar
                def _(act):
                    for n in range(3):
                        act.sem_inc(acc_taken[n], 1)

                    def take(tile, n, dst):
                        act.wait_ge(acc_ready, 9 + 3 * tile + n + 1)
                        c0, c1 = CHUNKS[n]
                        act.activation(dst, ps[:, n, 0:c1 - c0], ACT.Copy).then_inc(acc_taken[n], 1)

                    with act.Fori(0, QKV_TILES // 3) as i:
                        for r in range(3):
                            for n, (c0, c1) in enumerate(CHUNKS):
                                take(3 * i + r, n, qkv[:, ds(3 * i + r, 1), c0:c1].rearrange("p a t -> p (a t)"))
                    with act.Fori(0, CONV_TILES) as j:
                        act.wait_ge(conv_done, j + 1)
                        for r, dst in enumerate((gate_b, gate_c)):
                            for n, (c0, c1) in enumerate(CHUNKS):
                                take(QKV_TILES + 3 * j + r, n, dst[:, c0:c1])

                @block.vector
                def _(dve):
                    dve.sem_inc(conv_done, 1)
                    dve.memset(conv_u[:, 0:2], 0.0).then_inc(conv_link, 1)
                    dve.wait_ge(conv_link, 1)
                    dve.wait_ge(taps_in, 16)
                    with dve.Fori(0, CONV_TILES) as j:
                        link = Link(dve, conv_link, 1 + 5 * j)
                        tile = QKV_TILES + 3 * j + 2
                        for n, (c0, c1) in enumerate(CHUNKS):
                            dve.wait_ge(acc_taken[n], tile + 1)
                            dve.wait_ge(acc_ready, 9 + 3 * tile + n + 1)
                            xs = min(c1, META0) - c0
                            if c1 > META0:
                                link(dve.tensor_tensor(conv_u[:, 2:2 + N_META], ps[:, n, xs:c1 - c0],
                                                       gate_c[:, META0:TOK], ALU.mult))
                            dve.tensor_tensor(conv_u[:, 2 + N_META + c0:2 + N_META + c0 + xs], ps[:, n, 0:xs],
                                              gate_c[:, c0:c0 + xs], ALU.mult).then_inc(acc_taken[n], 1)
                        dve.wait_ge(acc_taken[2], tile + 2)
                        tap = [taps[:, ds(j, 1), q:q + 1].rearrange("p a b -> p (a b)") for q in range(3)]
                        link(dve.tensor_scalar(conv_t[:], conv_u[:, 0:TOK], tap[0], None, ALU.mult))
                        for q in (1, 2):
                            link(dve.scalar_tensor_tensor(conv_t[:], conv_u[:, q:q + TOK], tap[q], conv_t[:],
                                                          ALU.mult, ALU.add))
                        y = conv_y[:, ds(j, 1), :].rearrange("p a t -> p (a t)")
                        dve.tensor_tensor(y[:, 0:SEQ], conv_t[:, N_META:TOK], gate_b[:, 0:SEQ], ALU.mult)
                        link(dve.tensor_tensor(y[:, META0:TOK], conv_t[:, 0:N_META], gate_b[:, META0:TOK], ALU.mult))
                        dve.sem_inc(conv_done, 1)

            v_trans, v_taken, q_hi_ready, q_lo_ready, k_pad = map(sem, (
                "v_trans", "v_taken", "q_hi_ready", "q_lo_ready", "k_pad"))
            z_ready, zs_ready, abs_ready, exp_ready, ln_ready = map(sem, (
                "z_ready", "zs_ready", "abs_ready", "exp_ready", "ln_ready"))
            sp_ready, sp_masked, sp_hi_ready, sp_lo_ready, tri_done = map(sem, (
                "sp_ready", "sp_masked", "sp_hi_ready", "sp_lo_ready", "tri_done"))
            tmp_ready, w_ready, w_masked, pv_done, o_taken = map(sem, (
                "tmp_ready", "w_ready", "w_masked", "pv_done", "o_taken"))
            df_loaded, lam_link, lam_sum, lam_exp, rot_ready, rot_cos, rot_sin, rot_sum = map(sem, (
                "df_loaded", "lam_link", "lam_sum", "lam_exp", "rot_ready", "rot_cos", "rot_sin", "rot_sum"))
            ROT = [(first, c0, c1) for first in (DF_Q, DF_K) for c0, c1 in CHUNKS]
            ROT_AT = [4 + 4 * c for c in range(len(ROT))]
            S = len(SB_STEPS)
            DIAG = [n for n, s in enumerate(SB_STEPS) if s["diag"]]
            ENDS = [n for n, s in enumerate(SB_STEPS) if s["last"]]
            Z, SUM, OUT, ROT_BANK = 0, 2, 4, 6

            def rows_of(s):
                return N_META if s["key"] == XT else P

            with nc.Block() as block:
                @block.sync
                def _(sp_):
                    for n, v in enumerate((lambda_q1, lambda_k1, lambda_q2, lambda_k2)):
                        sp_.dma_start(lam_in[:, n, :], v[L].to_broadcast([P, SUB])).then_inc(df_loaded, 16)
                    sp_.dma_start(lam[:, 4:6], lam_consts[L].to_broadcast([P, 2])).then_inc(df_loaded, 16)
                    sp_.dma_start(norm_g[:], diff_norm_g[L].to_broadcast([P, HD])).then_inc(df_loaded, 16)
                    sp_.dma_start(cos_t[:], rope[0]).then_inc(df_loaded, 16)
                    sp_.dma_start(sin_t[:], rope[1]).then_inc(df_loaded, 16)
                    with sp_.If(layer < 1):
                        for first in range(MIN_BLOCKS * P, BLOCKS * P, SEQ):
                            n = min(SEQ, BLOCKS * P - first)
                            sp_.dma_start(y_dram[first:first + n, :], x[0, 0:n, :]).then_inc(pre["y_filled"], 16)

                @block.tensor
                def _(pe):
                    for n in range(TILES):
                        rows = P if n < XT else N_META
                        if n >= 2:
                            pe.wait_ge(v_taken, n - 1)
                        for j in range(4):
                            tile = (SB_V, SB_V + 1, DF_V, DF_V + 1)[j]
                            last = pe.transpose(ps[0:rows, 6 + n % 2, j * P:(j + 1) * P],
                                                qkv[:, tile, n * P:n * P + rows], C["ident"])
                        last.then_inc(v_trans, 1)
                    pe.wait_ge(v_taken, TILES)
                    with pe.Fori(0, 2) as pr:
                        pe.wait_ge(q_lo_ready, pr + 1)

                        def scores(n):
                            s = SB_STEPS[n]
                            if n >= 2:
                                pe.wait_ge(zs_ready, pr * S + n - 1)
                            h0 = s["head"] * HD
                            key = slice(s["key"] * P, (s["key"] + 1) * P)
                            q = slice(s["tile0"] * P + s["lo"], s["tile0"] * P + s["hi"])
                            three_passes(pe, ps[:, Z + n % 2, s["lo"]:s["hi"]],
                                         k_hi[h0:h0 + HD, key], k_lo[h0:h0 + HD, key],
                                         q_hi[h0:h0 + HD, q], q_lo[h0:h0 + HD, q], True, True) \
                                .then_inc(z_ready, 1)

                        def sums(n):
                            s, bank = SB_STEPS[n], SUM + SB_STEPS[n]["head"]
                            if n >= 2:
                                pe.wait_ge(tmp_ready, pr * S + n - 1)
                            if not s["first"]:
                                b, r = SB_STEPS[n - 2], rows_of(SB_STEPS[n - 2])
                                for part in (sp_hi, sp_lo):
                                    pe.matmul(ps[:, bank, b["lo"]:b["hi"]], prefix[0:r, :],
                                              part[(n - 2) % 6][0:r, b["lo"]:b["hi"]],
                                              start=False, stop=True, skip_group_check=True)
                            pe.wait_ge(sp_lo_ready, pr * S + n + 1)
                            r = rows_of(s)
                            for j, part in enumerate((sp_hi, sp_lo)):
                                last = pe.matmul(ps[:, bank, s["lo"]:s["hi"]], suffix[0:r, :],
                                                 part[n % 6][0:r, s["lo"]:s["hi"]],
                                                 start=s["first"] and j == 0, stop=True, skip_group_check=True)
                            last.then_inc(tri_done, 1)

                        def weighted(n):
                            s, r = SB_STEPS[n], rows_of(SB_STEPS[n])
                            if s["diag"]:
                                pe.wait_ge(w_masked, pr * len(DIAG) + DIAG.index(n) + 1)
                            if s["first"] and n >= 2:
                                e_ = [x for x in ENDS if x < n and SB_STEPS[x]["head"] == s["head"]]
                                if e_:
                                    pe.wait_ge(o_taken, pr * len(ENDS) + ENDS.index(e_[-1]) + 1)
                            if s["key"] == XT:
                                wait_apart(pe, w_ready, pr * S + n + 1, pe_passed)
                            else:
                                pe.wait_ge(w_ready, pr * S + n + 1)
                            for t0 in range(s["lo"], s["hi"], P):
                                v = v_rows[0:r, s["key"], ds(pr * P + s["head"] * HD, HD)]
                                last = pe.matmul(ps[:, OUT + s["head"], t0 // 2:t0 // 2 + HD],
                                                 wt[n % 4][0:r, t0:t0 + P], v,
                                                 start=s["first"] and t0 == s["lo"], stop=True,
                                                 skip_group_check=True)
                            last.then_inc(pv_done, 1)

                        def rotate(c):
                            first, c0, c1 = ROT[c]
                            pe.wait_ge(rot_sin, pr * len(ROT) + c + 1)
                            pe.matmul(ps[:, ROT_BANK + c % 2, 0:c1 - c0], C["rotate"],
                                      qkv[:, ds(first + pr, 1), c0:c1].rearrange("p a t -> p (a t)"),
                                      start=True, stop=True).then_inc(rot_ready, 1)

                        for n in range(S + 6):
                            if n < S:
                                scores(n)
                            if 0 <= n - 4 < S:
                                sums(n - 4)
                            if n in ROT_AT:
                                rotate(ROT_AT.index(n))
                            if 0 <= n - 6 < S:
                                weighted(n - 6)

                @block.scalar
                def _(act):
                    def high_parts(pair):
                        act.activation(q_hi[:, 0:TOK], qkv[:, ds(SB_Q + pair, 1), :].rearrange("p a t -> p (a t)"),
                                       ACT.Copy, scale=SB_SCALE).then_inc(q_hi_ready, 1)
                        act.activation(k_hi[:, 0:TOK], qkv[:, ds(SB_K + pair, 1), :].rearrange("p a t -> p (a t)"),
                                       ACT.Copy).then_inc(q_hi_ready, 1)

                    high_parts(0)
                    for n in range(TILES):
                        rows = P if n < XT else N_META
                        act.wait_ge(v_trans, n + 1)
                        act.activation(v_rows[0:rows, n, :], ps[0:rows, 6 + n % 2, :], ACT.Copy).then_inc(v_taken, 1)
                    act.wait_ge(lam_sum, 1)
                    act.activation(lam[:, 2:4], lam[:, 0:2], ACT.Exp).then_inc(lam_exp, 1)
                    with act.Fori(0, 2) as pr:
                        def part(buf, n):
                            s = SB_STEPS[n]
                            return buf[0:rows_of(s), s["lo"]:s["hi"]]

                        for n in range(S + 5):
                            if n < S:
                                s = SB_STEPS[n]
                                if n >= 6:
                                    act.wait_ge(tmp_ready, pr * S + n - 5)
                                act.wait_ge(z_ready, pr * S + n + 1)
                                act.activation(part(zs[n % 6], n), ps[0:rows_of(s), Z + n % 2, s["lo"]:s["hi"]],
                                               ACT.Copy).then_inc(zs_ready, 1)
                            if 0 <= n - 1 < S:
                                b = n - 1
                                act.wait_ge(abs_ready, pr * S + b + 1)
                                act.activation(part(ez[b % 2], b), part(ez[b % 2], b), ACT.Exp, scale=-1.0) \
                                    .then_inc(exp_ready, 1)
                            if 0 <= n - 2 < S:
                                b = n - 2
                                s = SB_STEPS[b]
                                if s["diag"]:
                                    act.wait_ge(sp_masked, pr * len(DIAG) + DIAG.index(b) + 1)
                                act.wait_ge(sp_ready, pr * S + b + 1)
                                act.wait_ge(tri_done, pr * S + b - 3 + 4 if b >= 4 else pr * S + 4)
                                act.activation(part(sp_hi[b % 6], b), part(sp[b % 4], b), ACT.Copy) \
                                    .then_inc(sp_hi_ready, 1)
                            if 0 <= n - 5 < S:
                                b = n - 5
                                act.wait_ge(tmp_ready, pr * S + b + 1)
                                act.activation(part(wt[b % 4], b), part(wt[b % 4], b), ACT.Exp).then_inc(w_ready, 1)
                            if 0 <= n - 1 < S:
                                b = n - 1
                                act.wait_ge(exp_ready, pr * S + b + 1)
                                act.activation(part(ez[b % 2], b), part(ez[b % 2], b), ACT.Ln, bias=1.0) \
                                    .then_inc(ln_ready, 1)
                            if n == S + 1:
                                with act.If(pr < 1):
                                    high_parts(pr + 1)

                @block.gpsimd
                def _(pool):
                    pool.memset(f32(q_hi[:, TOK:ROWS]), 0.0)
                    pool.memset(f32(q_lo[:, TOK:ROWS]), 0.0)
                    pool.memset(f32(k_hi[:, TOK:ROWS]), 0.0)
                    pool.memset(f32(k_lo[:, TOK:ROWS]), 0.0).then_inc(k_pad, 1)
                    pool.sem_inc(tri_done, 4)
                    pool.wait_ge(df_loaded, 16 * 8)
                    with pool.Fori(0, 2) as pr:
                        def low_triangle(buf, n, sem_in, sem_out):
                            r, lo = rows_of(SB_STEPS[n]), SB_STEPS[n]["lo"]
                            wait_apart(pool, sem_in, pr * S + n + 1, pool_passed)
                            part = buf[0:r, lo:lo + P]
                            pool.affine_select(out=part, in_=part, pattern=[[1, P]], compare_op=ALU.is_gt,
                                               fill=0.0, base=0, channel_multiplier=-1).then_inc(sem_out, 1)

                        def times_cosines(c):
                            first, c0, c1 = ROT[c]
                            wait_apart(pool, rot_sum, pr * len(ROT) + c + 1, pool_passed)
                            pool.tensor_tensor(rot_b[:, c0:c1],
                                               qkv[:, ds(first + pr, 1), c0:c1].rearrange("p a t -> p (a t)"),
                                               cos_t[:, c0:c1], ALU.mult).then_inc(rot_cos, 1)

                        for n in range(S + 5):
                            if 0 <= n - 1 < S and SB_STEPS[n - 1]["diag"]:
                                low_triangle(sp[(n - 1) % 4], n - 1, sp_ready, sp_masked)
                            if 0 <= n - 5 < S and SB_STEPS[n - 5]["diag"]:
                                low_triangle(wt[(n - 5) % 4], n - 5, w_ready, w_masked)
                            if n in ROT_AT:
                                times_cosines(ROT_AT.index(n))

                @block.vector
                def _(dve):
                    dve.sem_inc(pv_done, 1)
                    dve.sem_inc(rot_sin, 2)
                    dve.sem_inc(rot_sum, len(ROT))
                    def low_parts(pair):
                        dve.wait_ge(q_hi_ready, 2 * pair + 2)
                        dve.scalar_tensor_tensor(q_lo[:, 0:TOK], qkv[:, ds(SB_Q + pair, 1), :].rearrange("p a t -> p (a t)"),
                                                 SB_SCALE, f32(q_hi[:, 0:TOK]), ALU.mult, ALU.subtract)
                        dve.tensor_tensor(k_lo[:, 0:TOK], qkv[:, ds(SB_K + pair, 1), :].rearrange("p a t -> p (a t)"),
                                          f32(k_hi[:, 0:TOK]), ALU.subtract).then_inc(q_lo_ready, 1)

                    dve.wait_ge(k_pad, 1)
                    low_parts(0)
                    dve.wait_ge(df_loaded, 16 * 8)
                    link = Link(dve, lam_link)
                    for n in (0, 2):
                        link(dve.tensor_tensor(lam_in[:, n, :], lam_in[:, n, :], lam_in[:, n + 1, :], ALU.mult))
                    dve.tensor_reduce(lam[:, 0:2], lam_in[:, 0:4:2, :], AX, ALU.add).then_inc(lam_sum, 1)
                    dve.wait_ge(lam_exp, 1)
                    link(dve.tensor_tensor(lam[:, 6:7], lam[:, 3:4], lam[:, 2:3], ALU.subtract))
                    link(dve.tensor_tensor(lam[:, 6:7], lam[:, 6:7], lam[:, 4:5], ALU.subtract))
                    link(dve.tensor_scalar(norm_g[:], norm_g[:], lam[:, 5:6], None, ALU.mult))
                    with dve.Fori(0, 2) as pr:
                        def part(buf, n):
                            s = SB_STEPS[n]
                            return buf[0:rows_of(s), s["lo"]:s["hi"]]

                        def take_out(n):
                            s = SB_STEPS[n]
                            tiles = (s["hi"] - s["lo"]) // P
                            dve.wait_ge(pv_done, pr * S + n + 2)
                            dve.tensor_copy(y_sb[:, s["tile0"]:s["tile0"] + tiles, ds(pr * P + s["head"] * HD, HD)],
                                            ps[:, OUT + s["head"], 0:tiles * HD].rearrange("p (t c) -> p t c", c=HD)) \
                                .then_inc(o_taken, 1)

                        def times_sines(c):
                            first, c0, c1 = ROT[c]
                            dve.wait_ge(rot_ready, pr * len(ROT) + c + 1)
                            dve.wait_ge(rot_sum, pr * len(ROT) + c + 1)
                            dve.tensor_tensor(rot_a[:, c0:c1], ps[:, ROT_BANK + c % 2, 0:c1 - c0], sin_t[:, c0:c1],
                                              ALU.mult).then_inc(rot_sin, 1)

                        def rotated(c):
                            first, c0, c1 = ROT[c]
                            dve.wait_ge(rot_cos, pr * len(ROT) + c + 1)
                            dve.wait_ge(rot_sin, pr * len(ROT) + c + 1 + 2)
                            dve.tensor_tensor(qkv[:, ds(first + pr, 1), c0:c1].rearrange("p a t -> p (a t)"),
                                              rot_a[:, c0:c1], rot_b[:, c0:c1], ALU.add).then_inc(rot_sum, 1)

                        for n in range(S + 7):
                            if n < S:
                                if n >= 2:
                                    dve.wait_ge(sp_ready, pr * S + n - 1)
                                dve.wait_ge(zs_ready, pr * S + n + 1)
                                dve.tensor_scalar(part(ez[n % 2], n).bitcast(U32), part(zs[n % 6], n).bitcast(U32),
                                                  0x7FFFFFFF, None, ALU.bitwise_and) \
                                    .then_inc(abs_ready, 1)
                            if 0 <= n - 5 < S:
                                b = n - 5
                                s = SB_STEPS[b]
                                dve.wait_ge(tri_done, pr * S + b + 1 + 4)
                                if b >= 4:
                                    dve.wait_ge(pv_done, pr * S + b - 3 + 1)
                                dve.tensor_tensor(part(wt[b % 4], b), part(zs[b % 6], b),
                                                  ps[0:rows_of(s), SUM + s["head"], s["lo"]:s["hi"]],
                                                  ALU.subtract).then_inc(tmp_ready, 1)
                            if 0 <= n - 3 < S:
                                b = n - 3
                                dve.wait_ge(sp_hi_ready, pr * S + b + 1)
                                dve.tensor_tensor(part(sp_lo[b % 6], b), part(sp[b % 4], b),
                                                  f32(part(sp_hi[b % 6], b)), ALU.subtract).then_inc(sp_lo_ready, 1)
                            if 0 <= n - 1 < S:
                                b = n - 1
                                if b >= 4:
                                    dve.wait_ge(sp_lo_ready, pr * S + b - 3)
                                dve.wait_ge(ln_ready, pr * S + b + 1)
                                dve.scalar_tensor_tensor(part(sp[b % 4], b), part(zs[b % 6], b), 0.0,
                                                         part(ez[b % 2], b), ALU.max, ALU.add).then_inc(sp_ready, 1)
                            if n - 1 in ROT_AT:
                                times_sines(ROT_AT.index(n - 1))
                            if n - 2 in ROT_AT:
                                rotated(ROT_AT.index(n - 2))
                            if n - 7 in ENDS:
                                take_out(n - 7)
                            if n == S + 2:
                                with dve.If(pr < 1):
                                    low_parts(pr + 1)

            df_link, dq_hi, dq_lo = map(sem, ("df_link", "dq_hi", "dq_lo"))
            s_ready = [sem(f"s_ready{i}") for i in range(2)]
            m_ready = [sem(f"m_ready{i}") for i in range(2)]
            p_ready = [sem(f"p_ready{i}") for i in range(2)]
            a_ready, at_ready, at_taken, dpv_done, df_o_taken = map(sem, (
                "a_ready", "at_ready", "at_taken", "dpv_done", "df_o_taken"))
            UNITS = [(i, hh) for i in DIFF_ROWS for hh in range(2)]
            U = len(UNITS)
            GROUPS = [-(-len(key_tiles(i)) // 4) for i, _ in UNITS]
            G0 = [sum(GROUPS[:u]) for u in range(U + 1)]
            AT_BANK, DO_BANK = 6, 2

            with nc.Block() as block:
                @block.tensor
                def _(pe):
                    with pe.Fori(0, 2) as pr:
                        pe.wait_ge(dq_lo, 2 * pr + 2)

                        def scores(u, s):
                            i, hh = UNITS[u]
                            pieces, w = row_pieces(i)
                            if u >= 1:
                                pe.wait_ge(p_ready[s], pr * U + u)
                            if s == 0 and pieces == 3:
                                pe.wait_ge(df_o_taken, pr * U + 1 + u - 2)
                            r0 = hh * HD + s * SUB
                            mask0 = N_META + i * P if i < XT else 0
                            for n in range(pieces):
                                bank = 3 * s + n
                                a0, a1 = max(mask0, n * w), (n + 1) * w
                                last = three_passes(pe, ps[:, bank, 0:w],
                                                    q_hi[r0:r0 + SUB, i * P:(i + 1) * P],
                                                    q_lo[r0:r0 + SUB, i * P:(i + 1) * P],
                                                    k_hi[r0:r0 + SUB, n * w:(n + 1) * w],
                                                    k_lo[r0:r0 + SUB, n * w:(n + 1) * w], True, True)
                                if a0 < a1:
                                    last = pe.matmul(ps[:, bank, a0 - n * w:a1 - n * w], ident_bf[:],
                                                     negmask_bf[:, a0 - mask0:a1 - mask0],
                                                     start=False, stop=True, skip_group_check=True)
                            last.then_inc(s_ready[s], 1)

                        def transposes(u):
                            tiles = key_tiles(UNITS[u][0])
                            pe.wait_ge(a_ready, pr * U + u + 1)
                            for g in range(GROUPS[u]):
                                if G0[u] + g >= 2:
                                    pe.wait_ge(at_taken, pr * G0[U] + G0[u] + g - 1)
                                for j, (_, k0, nk) in enumerate(tiles[4 * g:4 * g + 4]):
                                    last = pe.transpose(ps[0:nk, AT_BANK + (G0[u] + g) % 2, j * P:(j + 1) * P],
                                                        prob[u % 2][0][:, k0:k0 + nk], C["ident"])
                                last.then_inc(at_ready, 1)

                        def weighted(u):
                            i, hh = UNITS[u]
                            tiles = key_tiles(i)
                            if u >= 1:
                                pe.wait_ge(df_o_taken, pr * U + 1 + u)
                            issued = min(u + 2, U - 1)
                            if row_pieces(UNITS[issued][0])[0] == 3:
                                pe.wait_ge(p_ready[0], pr * U + issued + 1)
                            wait_apart(pe, at_taken, pr * G0[U] + G0[u + 1], pe_passed)
                            for j, (vt, _, nk) in enumerate(tiles):
                                last = pe.matmul(ps[:, DO_BANK, 0:HD], a_t[u % 2][0:nk, j, :],
                                                 v_rows[0:nk, vt, ds(256 + pr * P + hh * HD, HD)],
                                                 start=j == 0, stop=j == len(tiles) - 1)
                            last.then_inc(dpv_done, 1)

                        for u in range(U + 2):
                            if u < U:
                                scores(u, 0)
                                scores(u, 1)
                            if 0 <= u - 2:
                                weighted(u - 2)
                            if 0 <= u - 1 < U:
                                transposes(u - 1)

                @block.scalar
                def _(act):
                    def high_parts(pair):
                        act.activation(q_hi[:, 0:TOK], qkv[:, ds(DF_Q + pair, 1), :].rearrange("p a t -> p (a t)"),
                                       ACT.Copy).then_inc(dq_hi, 1)
                        act.activation(k_hi[:, 0:N_META],
                                       qkv[:, ds(DF_K + pair, 1), META0:TOK].rearrange("p a t -> p (a t)"), ACT.Copy)
                        act.activation(k_hi[:, N_META:TOK],
                                       qkv[:, ds(DF_K + pair, 1), 0:SEQ].rearrange("p a t -> p (a t)"), ACT.Copy) \
                            .then_inc(dq_hi, 1)

                    high_parts(0)
                    with act.Fori(0, 2) as pr:
                        def exps(u, s):
                            pieces, w = row_pieces(UNITS[u][0])
                            if u >= 2:
                                act.wait_ge(at_ready, pr * G0[U] + G0[u - 1])
                            act.wait_ge(m_ready[s], pr * U + u + 1)
                            st = df_stat[u % 4]
                            act.activation(prob[u % 2][s][:, 0:pieces * w].rearrange("p (n w) -> p n w", w=w),
                                           ps[:, 3 * s:3 * s + pieces, 0:w], ACT.Exp, bias=st[:, 2 + s:3 + s],
                                           scale=DF_SCALE, accum_out=st[:, 4 + s:5 + s]).then_inc(p_ready[s], 1)

                        for u in range(U + 1):
                            if u < U:
                                exps(u, 0)
                                exps(u, 1)
                            else:
                                with act.If(pr < 1):
                                    high_parts(pr + 1)
                            if u >= 1:
                                b_ = u - 1
                                nt = len(key_tiles(UNITS[b_][0]))
                                for g in range(GROUPS[b_]):
                                    n = min(4, nt - 4 * g)
                                    if b_ >= 2:
                                        act.wait_ge(dpv_done, pr * U + b_ - 1)
                                    act.wait_ge(at_ready, pr * G0[U] + G0[b_] + g + 1)
                                    act.activation(a_t[b_ % 2][:, 4 * g:4 * g + n, :],
                                                   ps[:, AT_BANK + (G0[b_] + g) % 2, 0:n * P].rearrange("p (n k) -> p n k", k=P),
                                                   ACT.Copy).then_inc(at_taken, 1)

                @block.vector
                def _(dve):
                    def low_parts(pair):
                        dve.wait_ge(dq_hi, 2 * pair + 1)
                        dve.tensor_tensor(q_lo[:, 0:TOK], qkv[:, ds(DF_Q + pair, 1), :].rearrange("p a t -> p (a t)"),
                                          f32(q_hi[:, 0:TOK]), ALU.subtract).then_inc(dq_lo, 1)
                        dve.wait_ge(dq_hi, 2 * pair + 2)
                        dve.tensor_tensor(k_lo[:, 0:N_META],
                                          qkv[:, ds(DF_K + pair, 1), META0:TOK].rearrange("p a t -> p (a t)"),
                                          f32(k_hi[:, 0:N_META]), ALU.subtract)
                        dve.tensor_tensor(k_lo[:, N_META:TOK],
                                          qkv[:, ds(DF_K + pair, 1), 0:SEQ].rearrange("p a t -> p (a t)"),
                                          f32(k_hi[:, N_META:TOK]), ALU.subtract).then_inc(dq_lo, 1)

                    dve.sem_inc(df_o_taken, 1)
                    low_parts(0)
                    with dve.Fori(0, 2) as pr:
                        LINKS = U * 4
                        link = Link(dve, df_link, pr * LINKS)
                        def maxima(u, s):
                            pieces, w = row_pieces(UNITS[u][0])
                            st = df_stat[u % 4]
                            dve.wait_ge(s_ready[s], pr * U + u + 1)
                            link(dve.tensor_reduce(st[:, s:s + 1], ps[:, 3 * s:3 * s + pieces, 0:w],
                                                   mybir.AxisListType.XY, ALU.max))
                            dve.tensor_scalar(st[:, 2 + s:3 + s], st[:, s:s + 1], -DF_SCALE, None, ALU.mult) \
                                .then_inc(m_ready[s], 1)

                        def difference(u):
                            pieces, w = row_pieces(UNITS[u][0])
                            st, (p0, p1) = df_stat[u % 4], [x[:, 0:pieces * w] for x in prob[u % 2]]
                            for s in range(2):
                                dve.wait_ge(p_ready[s], pr * U + u + 1)
                            link(dve.reciprocal(st[:, 6:8], st[:, 4:6]))
                            link(dve.scalar_tensor_tensor(st[:, 8:9], st[:, 7:8], lam[:, 6:7], st[:, 4:5],
                                                          ALU.mult, ALU.mult))
                            dve.scalar_tensor_tensor(p0, p1, st[:, 8:9], p0, ALU.mult, ALU.add) \
                                .then_inc(a_ready, 1)

                        def take_out(u):
                            i, hh = UNITS[u]
                            dve.wait_ge(dpv_done, pr * U + u + 1)
                            dve.tensor_scalar(y_df[:, i, ds(pr * P + hh * HD, HD)], ps[:, DO_BANK, 0:HD],
                                              df_stat[u % 4][:, 6:7], None, ALU.mult).then_inc(df_o_taken, 1)

                        for u in range(U + 2):
                            if u < U:
                                maxima(u, 0)
                                maxima(u, 1)
                                difference(u)
                            if u == U:
                                with dve.If(pr < 1):
                                    low_parts(pr + 1)
                            if 0 <= u - 2:
                                take_out(u - 2)
                        assert link.n == LINKS, (link.n, LINKS)

            mix_link, mix_var, mix_rms, mix_normed, mix_trans, mix_hi, mix_lo, conv_hi, mix_pad = map(sem, (
                "mix_link", "mix_var", "mix_rms", "mix_normed", "mix_trans", "mix_hi", "mix_lo", "conv_hi", "mix_pad"))
            y_heads = y_df[:].rearrange("p t (h c) -> p (t h) c", c=HD)
            wo_loaded = [sem(f"wo_loaded{i}") for i in range(4)]
            ln_in, wo_hi_ready, wo_lo_ready = sem("ln_in"), sem("wo_hi_ready"), sem("wo_lo_ready")

            def load_wo(sp_, k):
                if k >= 4:
                    sp_.wait_ge(wo_loaded[k % 4], 16)
                sp_.dma_start(wo_raw[k][:], w_out[L, k * P:(k + 1) * P, :].rearrange("a p n -> p (a n)")) \
                    .then_inc(wo_loaded[k % 4], 16)

            def wo_high(act, k):
                act.wait_ge(wo_loaded[k % 4], 16 * (k // 4 + 1))
                act.activation(wo_hi[:, k, :], wo_raw[k][:], ACT.Copy).then_inc(wo_hi_ready, 1)

            def wo_low(eng, k):
                eng.wait_ge(wo_hi_ready, k + 1)
                eng.tensor_tensor(wo_lo[:, k, :], wo_raw[k][:], f32(wo_hi[:, k, :]), ALU.subtract) \
                    .then_inc(wo_lo_ready, 1)

            WO_HI_AHEAD, WO_LO_AHEAD = KD - 2, 4

            with nc.Block() as block:
                @block.sync
                def _(sp_):
                    for k in range(KD - 2):
                        load_wo(sp_, k)
                    sp_.dma_start(ln_g[:], ln1_g[L].to_broadcast([P, D])).then_inc(ln_in, 16)
                    sp_.dma_start(ln_b[:], ln1_b[L].to_broadcast([P, D])).then_inc(ln_in, 16)

                @block.gpsimd
                def _(pool):
                    pool.memset(f32(act_hi[:, :, TOK:ROWS]), 0.0)
                    pool.memset(f32(act_lo[:, :, TOK:ROWS]), 0.0).then_inc(mix_pad, 1)
                    pool.wait_ge(mix_var, 1)
                    pool.tensor_tensor(rms[:], ms[:], C["half"].to_broadcast([P, TILES * 4]), ALU.pow) \
                        .then_inc(mix_rms, 1)
                    for j in range(CONV_TILES):
                        pool.wait_ge(conv_hi, j + 1)
                        pool.tensor_tensor(act_lo[:, 4 + j, 0:TOK], conv_y[:, j, :], f32(act_hi[:, 4 + j, 0:TOK]),
                                           ALU.subtract)
                    for k in range(WO_LO_AHEAD):
                        wo_low(pool, k)
                    pool.wait_ge(mix_pad, 1)

                @block.tensor
                def _(pe):
                    pe.wait_ge(mix_normed, 1)
                    for n in range(TILES):
                        rows = P if n < XT else N_META
                        if n >= 2:
                            pe.wait_ge(mix_lo, n - 1)
                        for j in range(4):
                            src = (y_sb, y_sb, y_df, y_df)[j]
                            last = pe.transpose(ps[:, n % 2, j * P:j * P + rows],
                                                src[0:rows, n, (j % 2) * P:(j % 2 + 1) * P], C["ident"][0:rows, 0:rows])
                        last.then_inc(mix_trans, 1)

                @block.scalar
                def _(act):
                    for j in range(CONV_TILES):
                        act.activation(act_hi[:, 4 + j, 0:TOK], conv_y[:, j, :], ACT.Copy).then_inc(conv_hi, 1)
                    for k in range(WO_HI_AHEAD):
                        wo_high(act, k)
                    for n in range(TILES):
                        rows = P if n < XT else N_META
                        act.wait_ge(mix_trans, n + 1)
                        act.activation(act_hi[:, 0:4, n * P:n * P + rows],
                                       ps[:, n % 2, :].rearrange("p (k t) -> p k t", k=4)[:, :, 0:rows],
                                       ACT.Copy).then_inc(mix_hi, 1)

                @block.vector
                def _(dve):
                    link = Link(dve, mix_link)
                    link(dve.tensor_tensor(sq[:], y_heads, y_heads, ALU.mult))
                    link(dve.tensor_reduce(ms[:], sq[:], AX, ALU.add))
                    dve.tensor_scalar(ms[:], ms[:], 1.0 / HD, EPS, ALU.mult, ALU.add).then_inc(mix_var, 1)
                    dve.wait_ge(mix_rms, 1)
                    link(dve.tensor_tensor(y_heads, y_heads, rms[:].unsqueeze(2).to_broadcast([P, TILES * 4, HD]),
                                           ALU.mult))
                    dve.tensor_tensor(y_heads, y_heads, norm_g[:].unsqueeze(1).to_broadcast([P, TILES * 4, HD]),
                                      ALU.mult).then_inc(mix_normed, 1)
                    for n in range(TILES):
                        rows = P if n < XT else N_META
                        dve.wait_ge(mix_hi, n + 1)
                        dve.tensor_tensor(act_lo[:, 0:4, n * P:n * P + rows],
                                          ps[:, n % 2, :].rearrange("p (k t) -> p k t", k=4)[:, :, 0:rows],
                                          f32(act_hi[:, 0:4, n * P:n * P + rows]), ALU.subtract).then_inc(mix_lo, 1)

            res_in = [sem(f"res_in{i}") for i in range(3)]
            h1_saved = [sem(f"h1_saved{i}") for i in range(3)]
            (mix_ready, res_ready, ln_link, var_ready, rstd_ready, scaled, normed,
             h1_trans, h1_taken, lg_ready, lg_taken) = map(sem, (
                 "mix_ready", "res_ready", "ln_link", "var_ready",
                 "rstd_ready", "scaled", "normed", "h1_trans", "h1_taken", "lg_ready", "lg_taken"))
            T_BANK, LG_BANK = 6, 7

            def norm_statistics(dve, link, rows_in, st, var_sem):
                link(dve.bn_stats(st[:, 0:6], rows_in[:, 0:512]))
                link(dve.bn_stats(st[:, 6:12], rows_in[:, 512:1024]))
                dve.sem_inc(dve_passed, 1)
                link(dve.bn_aggr(st[:, 12:14], st[:, 0:12]))
                dve.tensor_scalar(st[:, 14:15], st[:, 13:14], EPS, None, ALU.add).then_inc(var_sem, 1)

            with nc.Block() as block:
                @block.sync
                def _(sp_):
                    for k in range(KD - 2, KD):
                        load_wo(sp_, k)
                    sp_.wait_ge(wo_lo_ready, KD)
                    sp_.wait_ge(pre["h_saved"], 32)
                    with sp_.Fori(0, TILES // 3) as i:
                        for r in range(3):
                            n = 3 * i + r
                            sp_.wait_ge(scaled, n + 1)
                            sp_.dma_start(res[r][:], h_dram[ds(n * P, P), :]).then_inc(res_in[r], 16)

                @block.gpsimd
                def _(pool):
                    pool.wait_ge(ln_in, 32)
                    with pool.Fori(0, TILES // 3) as i:
                        for r in range(3):
                            n = 3 * i + r
                            pool.wait_ge(var_ready, n + 1)
                            pool.tensor_tensor(stat[:, r, 15:16], stat[:, r, 14:15], C["half"], ALU.pow) \
                                .then_inc(rstd_ready, 1)
                            pool.wait_ge(scaled, 3 + n + 1)
                            pool.tensor_tensor(nrm[r][:], nrm[r][:], ln_b[:], ALU.add).then_inc(normed, 1)

                @block.tensor
                def _(pe):
                    pe.sem_inc(h1_trans, 6)

                    def project(n):
                        for half in range(2):
                            bank = 2 * (n % 3) + half
                            if half == 0 and n >= 3:
                                pe.wait_ge(res_ready, n - 2)
                            for k in range(KD):
                                if n == 0 and half == 0:
                                    pe.wait_ge(wo_lo_ready, k + 1)
                                cols = slice(512 * half, 512 * half + 512)
                                rows = slice(n * P, (n + 1) * P)
                                last = three_passes(pe, ps[:, bank, :], act_hi[:, k, rows], act_lo[:, k, rows],
                                                    wo_hi[:, k, cols], wo_lo[:, k, cols], k == 0, k == KD - 1)
                        last.then_inc(mix_ready, 1)

                    def route(n):
                        pe.wait_ge(normed, n + 1)
                        for j in range(2):
                            if 2 * n + j >= 1:
                                pe.wait_ge(h1_taken, 2 * n + j)
                            for k in range(4):
                                kk = 4 * j + k
                                last = pe.transpose(ps[:, T_BANK, k * P:(k + 1) * P],
                                                    nrm[n % 3][:, kk * P:(kk + 1) * P], C["ident"])
                            last.then_inc(h1_trans, 1)
                        if n >= 1:
                            pe.wait_ge(lg_taken, n)
                        pe.wait_ge(h1_taken, 2 * n + 2)
                        for k in range(KD):
                            last = pe.matmul(ps[:, LG_BANK, 0:N_EXP], h1_t[:, k, :], router[:, k, :],
                                             start=k == 0, stop=k == KD - 1)
                        last.then_inc(lg_ready, 1)

                    for n in range(TILES + 1):
                        if n < TILES:
                            project(n)
                        if n >= 1:
                            route(n - 1)

                @block.scalar
                def _(act):
                    for k in range(WO_HI_AHEAD, KD):
                        wo_high(act, k)
                    for r in range(3):
                        act.sem_inc(h1_saved[r], 16)
                    with act.Fori(0, TILES // 3) as i:
                        for r in range(3):
                            n = 3 * i + r
                            for j in range(2):
                                act.wait_ge(h1_trans, 6 + 2 * n + j + 1)
                                act.activation(h1_t[:, 4 * j:4 * j + 4, :],
                                               ps[:, T_BANK, :].rearrange("p (k t) -> p k t", k=4), ACT.Copy) \
                                    .then_inc(h1_taken, 1)
                            act.dma_start(h1_dram[ds(n * P, P), :], nrm[r][:]).then_inc(h1_saved[r], 16)
                            act.wait_ge(lg_ready, n + 1)
                            act.activation(logits[:, ds(n, 1), :].rearrange("p a e -> p (a e)"),
                                           ps[:, LG_BANK, 0:N_EXP], ACT.Copy).then_inc(lg_taken, 1)
                    for r in range(3):
                        act.wait_ge(h1_saved[r], 16 + 16 * TILES // 3)
                    act.wait_ge(lg_taken, TILES)

                @block.vector
                def _(dve):
                    dve.sem_inc(scaled, 3)
                    for k in range(WO_LO_AHEAD, KD):
                        wo_low(dve, k)
                    dve.wait_ge(ln_in, 32)

                    def norm_tile(n, r, link, link_base):
                        dve.wait_ge(res_in[r], 16 * (link_base + 1))
                        dve.wait_ge(mix_ready, n + 1)
                        dve.scalar_tensor_tensor(res[r][:, 0:512], res[r][:, 0:512], ALPHA, ps[:, 2 * r, :],
                                                 ALU.mult, ALU.add)
                        dve.scalar_tensor_tensor(res[r][:, 512:1024], res[r][:, 512:1024], ALPHA, ps[:, 2 * r + 1, :],
                                                 ALU.mult, ALU.add).then_inc(res_ready, 1)
                        dve.wait_ge(res_ready, n + 1)
                        norm_statistics(dve, link, res[r], stat[:, r, :], var_ready)
                        dve.wait_ge(rstd_ready, n + 1)

                    with dve.Fori(0, TILES // 3) as i:
                        link = Link(dve, ln_link, 12 * i)
                        for r in range(3):
                            n = 3 * i + r
                            norm_tile(n, r, link, i)
                            dve.wait_ge(h1_saved[r], 16 * i + 16)
                            dve.wait_ge(h1_trans, 2 * n + 2)
                            link(dve.tensor_scalar(nrm[r][:], res[r][:], stat[:, r, 12:13], stat[:, r, 15:16],
                                                   ALU.subtract, ALU.mult))
                            dve.tensor_tensor(nrm[r][:], nrm[r][:], ln_g[:], ALU.mult).then_inc(scaled, 1)

            rt_link, rt_shifted, rt_exp, rt_member, rt_counts, rt_places, rt_maps = map(sem, (
                "rt_link", "rt_shifted", "rt_exp", "rt_member", "rt_counts", "rt_places", "rt_maps"))

            y_saved = [sem(f"y_saved{i}") for i in range(2)]
            sp_passed, act_passed = sem("sp_passed"), sem("act_passed")
            (e_gu_in, e_dn_in, idx_ready, gu_hi_ready, gu_lo_ready, dn_hi_ready, dn_lo_ready, xt_trans, xt_hi_ready, xt_lo_ready,
             gu_ready, e_exp, e_link, hid_ready, ht_trans, ht_hi_ready, ht_lo_ready, dn_ready, y_ready) = \
                map(sem, ("e_gu_in", "e_dn_in", "idx_ready", "gu_hi_ready", "gu_lo_ready", "dn_hi_ready", "dn_lo_ready", "xt_trans",
                          "xt_hi_ready", "xt_lo_ready", "gu_ready", "e_exp", "e_link", "hid_ready", "ht_trans",
                          "ht_hi_ready", "ht_lo_ready", "dn_ready", "y_ready"))

            def load_expert(sp_, ex, u):
                sp_.wait_ge(e_gu_in, 32 * ex)
                for j, wsrc in enumerate((w_gate, w_up)):
                    sp_.dma_start(e_raw[:, 3 * u + j, :].rearrange("p (k f) -> p k f", f=FF),
                                  wsrc[L, ds(ex, 1)].rearrange("a e (k p) f -> p (a e k) f", p=P)) \
                        .then_inc(e_gu_in, 16)

            def load_expert_down(sp_, ex, u):
                sp_.wait_ge(e_dn_in, 16 * ex)
                sp_.dma_start(e_raw[:, 3 * u + 2, :], w_down[L, ds(ex, 1)].rearrange("a e f n -> (a e f) n")) \
                    .then_inc(e_dn_in, 16)

            with nc.Block() as block:
                @block.sync
                def _(sp_):
                    for ex in range(3):
                        load_expert(sp_, ex, ex)
                        load_expert_down(sp_, ex, ex)

                @block.gpsimd
                def _(pool):
                    for ex in range(3):
                        for j in range(2):
                            pool.wait_ge(gu_hi_ready, 2 * ex + j + 1)
                            last = pool.tensor_tensor(gu_lo[:, KD * ex:KD * ex + KD, j, :],
                                                      e_raw[:, 3 * ex + j, :].rearrange("p (k f) -> p k f", f=FF),
                                                      f32(gu_hi[:, KD * ex:KD * ex + KD, j, :]), ALU.subtract)
                        last.then_inc(gu_lo_ready, 1)
                        pool.wait_ge(dn_hi_ready, ex + 1)
                        pool.tensor_tensor(dn_lo[:, ex * D:ex * D + D], e_raw[:, 3 * ex + 2, :],
                                           f32(dn_hi[:, ex * D:ex * D + D]), ALU.subtract).then_inc(dn_lo_ready, 1)

                @block.scalar
                def _(act):
                    act.wait_ge(rt_shifted, 1)
                    act.activation(prb[:], sel[:], ACT.Exp).then_inc(rt_exp, 1)
                    for ex in range(3):
                        act.wait_ge(e_gu_in, 32 * ex + 32)
                        for j in range(2):
                            act.activation(gu_hi[:, KD * ex:KD * ex + KD, j, :],
                                           e_raw[:, 3 * ex + j, :].rearrange("p (k f) -> p k f", f=FF), ACT.Copy) \
                                .then_inc(gu_hi_ready, 1)
                        act.wait_ge(e_dn_in, 16 * ex + 16)
                        act.activation(dn_hi[:, ex * D:ex * D + D], e_raw[:, 3 * ex + 2, :], ACT.Copy) \
                            .then_inc(dn_hi_ready, 1)

                @block.tensor
                def _(pe):
                    pe.wait_ge(rt_member, 1)
                    pe.matmul(ps[:, 0, 0:TILES * N_EXP], C["prefix"], member[:], start=True, stop=True)
                    pe.matmul(ps[:, 1, 0:TILES * N_EXP], C["ones"], member[:], start=True, stop=True) \
                        .then_inc(rt_counts, 1)
                    for k in range(2):
                        pe.wait_ge(rt_places, k + 1)
                        for n in range(TILES):
                            last = pe.matmul(ps[:, 2, 0:2 * BLOCKS], at_pos[k][:, n, :], at_blk[k][:, n, :, :],
                                             start=k == 0 and n == 0, stop=k == 1 and n == TILES - 1)
                    last.then_inc(rt_maps, 1)

                @block.vector
                def _(dve):
                    link = Link(dve, rt_link)
                    tt, red = dve.tensor_tensor, dve.tensor_reduce
                    wide = [P, TILES, N_EXP]
                    col = [small[:, n, :, 0] for n in range(16)]
                    grp = lambda n: small[:, n, :, :]

                    def over(ap, shape):
                        return ap.unsqueeze(2).to_broadcast(shape)

                    def first_max(vals, prio, n, out_oh, c0, c1):
                        shape = [P, TILES, n]
                        link(red(col[c0], vals, AX, ALU.max))
                        link(tt(out_oh, vals, over(col[c0], shape), ALU.is_ge))
                        link(tt(out_oh, out_oh, prio.unsqueeze(1).to_broadcast(shape), ALU.mult))
                        link(red(col[c1], out_oh, AX, ALU.max))
                        link(tt(out_oh, out_oh, over(col[c1], shape), ALU.is_equal))

                    link(red(col[0], logits[:], AX, ALU.max))
                    tt(sel[:], logits[:], over(col[0], wide), ALU.subtract).then_inc(rt_shifted, 1)
                    dve.wait_ge(rt_exp, 1)
                    link(red(col[0], prb[:], AX, ALU.add))
                    link(dve.reciprocal(col[1], col[0]))
                    link(tt(prb[:], prb[:], over(col[1], wide), ALU.mult))
                    link(tt(sel[:], prb[:], rbias[:].unsqueeze(1).to_broadcast(wide), ALU.add))
                    g4 = sel[:].rearrange("p t (g e) -> p (t g) e", e=4)
                    tt(pair[:, :, 0:2], g4[:, :, 0:2], g4[:, :, 2:4], ALU.add)
                    tt(pair[:, :, 2:4], g4[:, :, 0:4:2], g4[:, :, 1:4:2], ALU.add)
                    tt(pair[:, :, 4:5], g4[:, :, 0:1], g4[:, :, 3:4], ALU.add)
                    link(tt(pair[:, :, 5:6], g4[:, :, 1:2], g4[:, :, 2:3], ALU.add))
                    link(red(grp(14).rearrange("p t g -> p (t g)"), pair[:], AX, ALU.max))
                    first_max(grp(14), C["prio4"], N_GRP, grp(15), 2, 3)
                    pen = grp(14).rearrange("p t g -> p (t g)")
                    link(dve.tensor_scalar(pen, grp(15).rearrange("p t g -> p (t g)"), -NEG, NEG, ALU.mult, ALU.add))
                    link(tt(g4, g4, pen.unsqueeze(2).to_broadcast([P, TILES * N_GRP, 4]), ALU.add))
                    first_max(sel[:], C["prio16"], N_EXP, onehot[0][:], 2, 3)
                    t0, t1 = tmp[0][:, :, 0:N_EXP], tmp[1][:, :, 0:N_EXP]
                    link(dve.tensor_scalar(t0, onehot[0][:], 4 * NEG, None, ALU.mult))
                    link(tt(sel[:], sel[:], t0, ALU.add))
                    first_max(sel[:], C["prio16"], N_EXP, onehot[1][:], 2, 3)
                    for k in range(2):
                        link(tt(t0, prb[:], onehot[k][:], ALU.mult))
                        link(red(col[4 + k], t0, AX, ALU.add))
                    link(tt(col[6], col[4], col[5], ALU.add))
                    link(dve.reciprocal(col[7], col[6]))
                    for k in range(2):
                        link(tt(col[4 + k], col[4 + k], col[7], ALU.mult))
                        link(tt(col[4 + k], col[4 + k], C["valid"], ALU.mult))
                        link(tt(onehot[k][:], onehot[k][:], over(C["valid"], wide), ALU.mult))
                    tt(member[:], onehot[0][:], onehot[1][:], ALU.add).then_inc(rt_member, 1)
                    dve.wait_ge(rt_counts, 1)
                    link(dve.memset(before[:, 0, :], 0.0))
                    for n in range(TILES):
                        link(tt(before[:, n + 1, :], before[:, n, :], ps[:, 1, n * N_EXP:(n + 1) * N_EXP], ALU.add))
                    link(tt(slots[:], ps[:, 0, 0:TILES * N_EXP].rearrange("p (t e) -> p t e", e=N_EXP),
                            before[:, 0:TILES, :], ALU.add))
                    nb, cum, excl, start = (blk[:, n, :] for n in range(4))
                    ge = cnt_ge[:, :, 0:TILES]
                    link(tt(ge, over(before[:, TILES, :], [P, N_EXP, TILES]),
                            C["thr"].unsqueeze(1).to_broadcast([P, N_EXP, TILES]), ALU.is_gt))
                    link(red(nb, ge, AX, ALU.add))
                    link(dve.tensor_scalar(nb, nb, 1.0, None, ALU.max))
                    link(dve.tensor_tensor_scan(cum, C["ones"][:, 0:N_EXP], nb, 0.0, ALU.mult, ALU.add))
                    link(tt(excl, cum, nb, ALU.subtract))
                    link(dve.tensor_scalar(start, excl, float(P), None, ALU.mult))
                    link(tt(slots[:], slots[:], start.unsqueeze(1).to_broadcast(wide), ALU.add))
                    cge = cnt_ge[:].rearrange("p e b -> p b e")
                    link(dve.tensor_scalar(tmp[2][:, 0, :], C["thr_blk"], 1.0 / P, -1.0, ALU.mult, ALU.add))
                    link(tt(cge, tmp[2][:, 0, :].unsqueeze(2).to_broadcast([P, BLOCKS, N_EXP]),
                            cum.unsqueeze(1).to_broadcast([P, BLOCKS, N_EXP]), ALU.is_ge))
                    link(red(tmp[2][:, 1, :], cge, AX, ALU.add))
                    word, ex_of, ex_cap = (tmp[k][:, 5:7, :].rearrange("p a b -> p (a b)") for k in range(3))
                    link(dve.memset(word, 0.0))
                    link(dve.memset(ex_of, N_EXP - 1.0))
                    link(dve.tensor_scalar(ex_of[:, 0:BLOCKS], tmp[2][:, 1, :], N_EXP - 1.0, None, ALU.min))
                    link(dve.tensor_scalar(ex_cap, ex_of, N_EXP - 3.0, None, ALU.min))
                    n = 2 * BLOCKS - 1
                    link(tt(word[:, 1:], ex_cap[:, 1:], ex_cap[:, 0:n], ALU.subtract))
                    link(dve.scalar_tensor_tensor(word[:, 1:], ex_of[:, 0:n], 2.0, word[:, 1:], ALU.mult, ALU.add))
                    link(dve.scalar_tensor_tensor(word[:, 1:], word[:, 1:], 16.0, ex_of[:, 1:], ALU.mult, ALU.add))
                    link(dve.scalar_tensor_tensor(pair_word[:], word[:, 2:BLOCKS + 2:2], 512.0,
                                                  word[:, 1:BLOCKS + 1:2], ALU.mult, ALU.add))
                    link(dve.tensor_scalar(col[12][:, 0:1], cum[:, N_EXP - 1:N_EXP], 0.5, None, ALU.mult))
                    link(tt(tmp[2][:, 4, :], col[12][:, 0:1].to_broadcast([P, BLOCKS]), tmp[2][:, 0, :], ALU.is_gt))
                    link(red(col[13][:, 0:1], tmp[2][:, 4, :], AX, ALU.add))
                    link(dve.tensor_scalar(counts[:, 0:1], col[13][:, 0:1], -2.0, None, ALU.add))
                    link(dve.tensor_copy(counts[:, 1:2], gathers[:, 0:1]))
                    link(dve.scalar_tensor_tensor(gathers[:, 0:1], col[13][:, 0:1], 16.0, gathers[:, 0:1],
                                                  ALU.mult, ALU.add))
                    for k in range(2):
                        s_, b_, p_ = col[8], col[9], col[10]
                        link(tt(t0, slots[:], onehot[k][:], ALU.mult))
                        link(red(s_, t0, AX, ALU.add))
                        link(dve.tensor_copy(slot_u[:, k, :], s_))
                        shape = [P, TILES, BLOCKS]
                        link(tt(tmp[0][:], over(s_, shape), C["thr_blk"].unsqueeze(1).to_broadcast(shape), ALU.is_ge))
                        link(red(b_, tmp[0][:], AX, ALU.add))
                        link(dve.scalar_tensor_tensor(p_, b_, -float(P), s_, ALU.mult, ALU.add))
                        link(tt(at_pos[k][:], over(p_, [P, TILES, P]),
                                C["iota"].unsqueeze(1).to_broadcast([P, TILES, P]), ALU.is_equal))
                        link(tt(tmp[0][:], over(b_, shape),
                                C["iota"][:, 0:BLOCKS].unsqueeze(1).to_broadcast(shape), ALU.is_equal))
                        link(tt(col[11], C["tokid"], C["valid"], ALU.mult))
                        link(tt(at_blk[k][:, :, 0, :], tmp[0][:], over(col[11], shape), ALU.mult))
                        ins = tt(at_blk[k][:, :, 1, :], tmp[0][:], over(col[4 + k], shape), ALU.mult)
                        if k == 0:
                            link(ins)
                            dve.sem_inc(rt_places, 1)
                    ins.then_inc(rt_places, 1)
                    dve.wait_ge(rt_maps, 1)
                    dve.tensor_copy(tokmap[:], ps[:, 2, 0:BLOCKS])
                    link(dve.tensor_copy(gatemap[:], ps[:, 2, BLOCKS:2 * BLOCKS]))

            XT_BANK, GU_BANK, HT_BANK, DN_BANK = 0, 2, 4, 5

            def loop_turns(eng):
                return eng.value_load(counts[0:1, 0:1], min_val=MIN_BLOCKS // 2 - 2, max_val=BLOCKS // 2 - 2)

            def step_words(eng, i):
                v = eng.value_load(pair_word[0:1, ds(i, 1)], min_val=0, max_val=2 ** 18 - 1)
                return [((v >> at) & 15, (v >> (at + 4)) & 1, (v >> (at + 5)) & 15) for at in (0, 9)]

            with nc.Block() as block:
                @block.sync
                def _(sp_):
                    def load(ex, u):
                        wait_apart(sp_, gu_lo_ready, ex + 1, sp_passed)
                        load_expert(sp_, ex, u)
                        wait_apart(sp_, dn_lo_ready, ex + 1, sp_passed)
                        load_expert_down(sp_, ex, u)

                    with sp_.Fori(0, N_EXP // 3 - 1) as i:
                        for u in range(3):
                            load(i * 3 + 3 + u, u)
                    for ex in range(N_EXP // 3 * 3, N_EXP):
                        load(ex, ex % 3)

                @block.gpsimd
                def _(pool):
                    def rows(b_, u):
                        wait_apart(pool, xt_trans, 2 * b_ + 2, pool_passed)
                        pool.tensor_copy(idx[u][:], tokmap[:, ds(b_, 1)]).then_inc(idx_ready, 1)
                        wait_apart(pool, idx_ready, b_ + 1, pool_passed)
                        pool.indirect_dma_start(xg[u][:], None, h1_dram, bass.IndirectOffsetOnAxis(
                            ap=idx[u][:], axis=0)).then_inc(xg_in[u], 16)

                    def down_low(ex, at):
                        wait_apart(pool, dn_hi_ready, ex + 1, pool_passed)
                        pool.tensor_tensor(dn_lo[:, ds(at * D, D)],
                                           e_raw[:, ds(3 * at + 2, 1), :].rearrange("p a n -> p (a n)"),
                                           f32(dn_hi[:, ds(at * D, D)]), ALU.subtract).then_inc(dn_lo_ready, 1)

                    def new_down_low(word):
                        ex, new, _before = word
                        with pool.If(new > 0):
                            down_low(ex + 2, (ex + 2) % 3)

                    turns = loop_turns(pool)
                    pool.sem_inc(dn_lo_ready, 3)
                    for n in range(3):
                        rows(n, n % 2)
                    rows(3, 1)
                    rows(4, 0)
                    with pool.Fori(0, turns - 1) as i:
                        words = step_words(pool, i)
                        for r in range(2):
                            rows(2 * i + 5 + r, (1 + r) % 2)
                            new_down_low(words[r])
                    rows(2 * turns + 3, 1)
                    for words in (step_words(pool, turns - 1), step_words(pool, turns)):
                        for word in words:
                            new_down_low(word)

                @block.tensor
                def _(pe):
                    turns = loop_turns(pe)
                    gathered = pe.value_load(counts[0:1, 1:2], min_val=0, max_val=(DEPTH - 1) * 16 * BLOCKS // 2)
                    pe.sem_inc(xt_trans, 4)
                    pe.sem_inc(gu_ready, 2)
                    pe.sem_inc(dn_ready, 2)

                    def rows_in(b_, u, i):
                        pe.wait_ge(xg_in[u], gathered + 16 * i + 16)
                        pe.wait_ge(xt_lo_ready, 2 * b_ + 1)
                        for j in range(2):
                            if j:
                                pe.wait_ge(xt_lo_ready, 2 * b_ + 2)
                            for k in range(4):
                                kk = 4 * j + k
                                last = pe.transpose(ps[:, XT_BANK + j, k * P:(k + 1) * P],
                                                    xg[u][:, kk * P:(kk + 1) * P], C["ident"])
                            last.then_inc(xt_trans, 1)

                    def gate_up(b_, u, ex):
                        kd = (ex % 3) * KD
                        pe.wait_ge(gu_lo_ready, ex + 4)
                        pe.wait_ge(xt_lo_ready, 2 + 2 * b_ + 2)
                        pe.wait_ge(hid_ready, b_ + 1)
                        for k in range(KD):
                            last = three_passes(pe, ps[:, GU_BANK + u, 0:2 * FF], xt_hi[u][:, k, :], xt_lo[u][:, k, :],
                                                gu_hi[:, ds(kd + k, 1), :, :], gu_lo[:, ds(kd + k, 1), :, :],
                                                k == 0, k == KD - 1)
                        last.then_inc(gu_ready, 1)

                    def hidden_in(b_, u):
                        pe.wait_ge(hid_ready, 2 + b_ + 1)
                        pe.wait_ge(ht_lo_ready, b_ + 1)
                        pe.transpose(ps[:, HT_BANK, 0:P], hid[u][:, 2, :], C["ident"]).then_inc(ht_trans, 1)

                    def down(b_, u, ex):
                        pe.wait_ge(ht_lo_ready, 1 + b_ + 1)
                        pe.wait_ge(dn_lo_ready, ex + 4)
                        pe.wait_ge(y_ready, b_ + 1)
                        for half in range(2):
                            cols = ds((ex % 3) * D + 512 * half, 512)
                            last = three_passes(pe, ps[:, DN_BANK + half, :], hid_hi[u][:], hid_lo[u][:],
                                                dn_hi[:, cols], dn_lo[:, cols], True, True)
                        last.then_inc(dn_ready, 1)

                    rows_in(0, 0, 0)
                    rows_in(1, 1, 0)
                    words = step_words(pe, 0)
                    gate_up(0, 0, words[0][2])
                    rows_in(2, 0, 1)
                    with pe.Fori(0, turns) as i:
                        words = step_words(pe, i)
                        for r in range(2):
                            b_, u = 2 * i + 1 + r, (1 + r) % 2
                            ex, _new, before_ex = words[r]
                            gate_up(b_, u, ex)
                            hidden_in(b_ - 1, 1 - u)
                            rows_in(b_ + 2, u, i + 1 + r)
                            down(b_ - 1, 1 - u, before_ex)
                    words = step_words(pe, turns) + step_words(pe, turns + 1)
                    for r in range(3):
                        b_, u = 2 * turns + 1 + r, (1 + r) % 2
                        ex, _new, before_ex = words[r]
                        gate_up(b_, u, ex)
                        hidden_in(b_ - 1, 1 - u)
                        if r == 0:
                            rows_in(b_ + 2, u, turns + 1)
                        down(b_ - 1, 1 - u, before_ex)
                    hidden_in(b_, u)
                    down(b_, u, ex)

                def xt_high(act, b_, u):
                    for j in range(2):
                        act.wait_ge(xt_trans, 4 + 2 * b_ + j + 1)
                        act.wait_ge(gu_ready, b_ + 1)
                        act.activation(xt_hi[u][:, 4 * j:4 * j + 4, :],
                                       ps[:, XT_BANK + j, :].rearrange("p (k t) -> p k t", k=4), ACT.Copy) \
                            .then_inc(xt_hi_ready, 1)

                @block.scalar
                def _(act):
                    def ht_high(b_, u):
                        act.wait_ge(ht_trans, b_ + 1)
                        act.wait_ge(dn_ready, b_ + 1)
                        act.activation(hid_hi[u][:], ps[:, HT_BANK, 0:P], ACT.Copy).then_inc(ht_hi_ready, 1)

                    def gate_up_high(ex, par, b_):
                        act.wait_ge(e_gu_in, 32 * ex + 32)
                        act.wait_ge(gu_ready, 2 + b_)
                        for j in range(2):
                            last = act.activation(gu_hi[:, ds(par * KD, KD), j, :],
                                                  e_raw[:, ds(3 * par + j, 1), :]
                                                  .rearrange("p a (k f) -> p (a k) f", f=FF), ACT.Copy)
                            last.then_inc(gu_hi_ready, 1)

                    def down_high(ex, par, b_):
                        act.wait_ge(e_dn_in, 16 * ex + 16)
                        act.wait_ge(dn_ready, 2 + b_)
                        act.activation(dn_hi[:, ds(par * D, D)],
                                       e_raw[:, ds(3 * par + 2, 1), :].rearrange("p a n -> p (a n)"), ACT.Copy) \
                            .then_inc(dn_hi_ready, 1)

                    def gate_exp(b_, u):
                        act.wait_ge(gu_ready, 2 + b_ + 1)
                        act.activation(hid[u][:, 0, :], ps[:, GU_BANK + u, 0:FF], ACT.Exp, scale=-1.0) \
                            .then_inc(e_exp, 1)

                    def y_take(b_, u, i):
                        act.wait_ge(dn_ready, 2 + b_ + 1)
                        act.wait_ge(y_saved[u], 16 * i + 16)
                        act.activation(y_out[u][:], ps[:, DN_BANK:DN_BANK + 2, :].rearrange("p a n -> p (a n)"),
                                       ACT.Copy).then_inc(y_ready, 1)
                        act.wait_ge(y_ready, 1 + b_ + 1)
                        act.dma_start(y_dram[ds(b_ * P, P), :], y_out[u][:]).then_inc(y_saved[u], 16)

                    act.wait_ge(pre["y_filled"], 16 * -(-(BLOCKS - MIN_BLOCKS) // XT))
                    turns = loop_turns(act)
                    for u in range(2):
                        act.sem_inc(y_saved[u], 16)
                    act.sem_inc(y_ready, 1)
                    xt_high(act, 0, 0)
                    xt_high(act, 1, 1)
                    gate_exp(0, 0)
                    xt_high(act, 2, 0)

                    def step(b_, u, i, word, more):
                        ex, new, _before = word
                        gate_exp(b_, u)
                        ht_high(b_ - 1, 1 - u)
                        if more:
                            xt_high(act, b_ + 2, u)
                        with act.If(new > 0):
                            gate_up_high(ex + 2, (ex + 2) % 3, b_)
                            down_high(ex + 2, (ex + 2) % 3, b_)
                        y_take(b_ - 1, 1 - u, i)

                    with act.Fori(0, turns) as i:
                        words = step_words(act, i)
                        for r in range(2):
                            step(2 * i + 1 + r, (1 + r) % 2, i, words[r], True)
                    words = step_words(act, turns)
                    step(2 * turns + 1, 1, turns, words[0], True)
                    step(2 * turns + 2, 0, turns, words[1], False)
                    b_, u, i = 2 * turns + 3, 1, turns + 1
                    gate_exp(b_, u)
                    ht_high(b_ - 1, 1 - u)
                    y_take(b_ - 1, 1 - u, i)
                    ht_high(b_, u)
                    y_take(b_, u, i)
                    for u in range(2):
                        wait_apart(act, y_saved[u], 16 * turns + 48, act_passed)

                @block.vector
                def _(dve):
                    def xt_low(b_, u):
                        for j in range(2):
                            dve.wait_ge(xt_hi_ready, 2 * b_ + j + 1)
                            part = slice(4 * j, 4 * j + 4)
                            dve.tensor_tensor(xt_lo[u][:, part, :], ps[:, XT_BANK + j, :].rearrange("p (k t) -> p k t", k=4),
                                              f32(xt_hi[u][:, part, :]), ALU.subtract).then_inc(xt_lo_ready, 1)

                    def ht_low(b_, u):
                        dve.wait_ge(ht_hi_ready, b_ + 1)
                        dve.tensor_tensor(hid_lo[u][:], ps[:, HT_BANK, 0:P], f32(hid_hi[u][:]), ALU.subtract) \
                            .then_inc(ht_lo_ready, 1)

                    def gate_up_low(ex, par):
                        for j in range(2):
                            dve.wait_ge(gu_hi_ready, 2 * ex + j + 1)
                            last = dve.tensor_tensor(gu_lo[:, ds(par * KD, KD), j, :],
                                                     e_raw[:, ds(3 * par + j, 1), :]
                                                     .rearrange("p a (k f) -> p (a k) f", f=FF),
                                                     f32(gu_hi[:, ds(par * KD, KD), j, :]), ALU.subtract)
                        last.then_inc(gu_lo_ready, 1)

                    def hidden(b_, u):
                        link = Link(dve, e_link, 3 * b_)
                        dve.wait_ge(e_exp, b_ + 1)
                        link(dve.tensor_scalar(hid[u][:, 1, :], hid[u][:, 0, :], 1.0, None, ALU.add))
                        link(dve.reciprocal(hid[u][:, 0, :], hid[u][:, 1, :]))
                        link(dve.tensor_tensor(hid[u][:, 1, :], ps[:, GU_BANK + u, 0:FF], hid[u][:, 0, :], ALU.mult))
                        dve.scalar_tensor_tensor(hid[u][:, 2, :], ps[:, GU_BANK + u, FF:2 * FF],
                                                 gatemap[:, ds(b_, 1)], hid[u][:, 1, :], ALU.mult, ALU.mult) \
                            .then_inc(hid_ready, 1)

                    turns = loop_turns(dve)
                    dve.sem_inc(gu_lo_ready, 3)
                    dve.sem_inc(xt_lo_ready, 2)
                    dve.sem_inc(hid_ready, 2)
                    dve.sem_inc(ht_lo_ready, 1)
                    xt_low(0, 0)
                    xt_low(1, 1)
                    hidden(0, 0)
                    xt_low(2, 0)

                    def step(b_, u, word, more):
                        ex, new, _before = word
                        ht_low(b_ - 1, 1 - u)
                        hidden(b_, u)
                        if more:
                            xt_low(b_ + 2, u)
                        with dve.If(new > 0):
                            gate_up_low(ex + 2, (ex + 2) % 3)

                    with dve.Fori(0, turns) as i:
                        words = step_words(dve, i)
                        for r in range(2):
                            step(2 * i + 1 + r, (1 + r) % 2, words[r], True)
                    words = step_words(dve, turns)
                    step(2 * turns + 1, 1, words[0], True)
                    step(2 * turns + 2, 0, words[1], False)
                    b_, u = 2 * turns + 3, 1
                    ht_low(b_ - 1, 1 - u)
                    hidden(b_, u)
                    ht_low(b_, u)

            f_in = [sem(f"f_in{i}") for i in range(3)]
            f_saved = [sem(f"f_saved{i}") for i in range(3)]
            (f_ln_in, f_idx, f_link, f_summed, f_var, f_rstd, f_scaled, f_normed, f_trans, f_hi, f_lo) = map(sem, (
                "f_ln_in", "f_idx", "f_link", "f_summed", "f_var", "f_rstd", "f_scaled", "f_normed", "f_trans",
                "f_hi", "f_lo"))

            with nc.Block() as block:
                @block.sync
                def _(sp_):
                    sp_.dma_start(ln_g[:], ln2_g[L].to_broadcast([P, D])).then_inc(f_ln_in, 16)
                    sp_.dma_start(ln_b[:], ln2_b[L].to_broadcast([P, D])).then_inc(f_ln_in, 16)
                    with sp_.Fori(0, TILES // 3) as i:
                        for r in range(3):
                            n = 3 * i + r
                            sp_.wait_ge(f_scaled, n + 1)
                            sp_.dma_start(res[r][:], h1_dram[ds(n * P, P), :]).then_inc(f_in[r], 16)

                @block.gpsimd
                def _(pool):
                    def gather(n, r):
                        wait_apart(pool, f_summed, n + 1, pool_passed)
                        pool.tensor_copy(f_idx_t[r][:, 0:1], slot_u[:, 0, ds(n, 1)])
                        pool.tensor_copy(f_idx_t[r][:, 1:2], slot_u[:, 1, ds(n, 1)]).then_inc(f_idx, 1)
                        wait_apart(pool, f_idx, n + 1, pool_passed)
                        for k, y in enumerate((y_a, y_b)):
                            pool.indirect_dma_start(y[r][:], None, y_dram, bass.IndirectOffsetOnAxis(
                                ap=f_idx_t[r][:, k:k + 1], axis=0)).then_inc(fy_in[r], 16)

                    def rstd(n, r):
                        pool.wait_ge(f_var, n + 1)
                        pool.tensor_tensor(stat[:, r, 15:16], stat[:, r, 14:15], C["half"], ALU.pow).then_inc(f_rstd, 1)

                    def add_bias(n, r):
                        pool.wait_ge(f_scaled, 3 + n + 1)
                        pool.tensor_tensor(nrm[r][:], nrm[r][:], ln_b[:], ALU.add).then_inc(f_normed, 1)

                    for r in range(3):
                        gather(r, r)
                    pool.wait_ge(f_ln_in, 32)
                    with pool.Fori(0, TILES // 3 - 1) as i:
                        for r in range(3):
                            rstd(3 * i + r, r)
                            gather(3 * i + r + 3, r)
                            add_bias(3 * i + r, r)
                    for r in range(3):
                        rstd(TILES - 3 + r, r)
                        add_bias(TILES - 3 + r, r)

                @block.tensor
                def _(pe):
                    pe.sem_inc(f_trans, 6)
                    with pe.Fori(0, TILES // 3) as i:
                        for r in range(3):
                            n = 3 * i + r
                            pe.wait_ge(f_normed, n + 1)
                            pe.wait_ge(f_lo, 2 * n + 2)
                            for j in range(2):
                                for k in range(4):
                                    kk = 4 * j + k
                                    last = pe.transpose(ps[:, 2 * r + j, k * P:(k + 1) * P],
                                                        nrm[r][:, kk * P:(kk + 1) * P], C["ident"])
                                last.then_inc(f_trans, 1)

                @block.scalar
                def _(act):
                    for r in range(3):
                        act.sem_inc(f_saved[r], 16)
                    act.wait_ge(f_ln_in, 32)

                    def tile(n, r, with_out):
                        wait_apart(act, f_normed, n + 1, act_passed)
                        if with_out:
                            with act.If(layer > DEPTH - 2):
                                act.dma_start(out[0, ds(n * P, P), :], nrm[r][:]).then_inc(f_saved[r], 16)
                            with act.If(layer < DEPTH - 1):
                                act.dma_start(h_dram[ds(n * P, P), :], nrm[r][:]).then_inc(f_saved[r], 16)
                        else:
                            act.dma_start(h_dram[ds(n * P, P), :], nrm[r][:]).then_inc(f_saved[r], 16)
                        for j in range(2):
                            act.wait_ge(f_trans, 6 + 2 * n + j + 1)
                            act.activation(act_hi[:, 4 * j:4 * j + 4, ds(n * P, P)],
                                           ps[:, 2 * r + j, :].rearrange("p (k t) -> p k t", k=4), ACT.Copy) \
                                .then_inc(f_hi, 1)

                    with act.Fori(0, TILES // 3 - 1) as i:
                        for r in range(3):
                            tile(3 * i + r, r, True)
                    for n in range(TILES - 3, TILES):
                        tile(n, n % 3, n < XT)
                    for r in range(3):
                        act.wait_ge(f_saved[r], 16 + 16 * TILES // 3)
                    act.wait_ge(f_hi, 2 * TILES)

                @block.vector
                def _(dve):
                    dve.sem_inc(f_summed, 3)
                    dve.sem_inc(f_scaled, 3)
                    dve.sem_inc(f_lo, 6)
                    dve.wait_ge(f_ln_in, 32)

                    def summed(n, r, i, link):
                        dve.wait_ge(fy_in[r], layer * (32 * TILES // 3) + 32 * i + 32)
                        dve.tensor_tensor(y_a[r][:], y_a[r][:], y_b[r][:], ALU.add).then_inc(f_summed, 1)
                        dve.wait_ge(f_in[r], 16 * i + 16)
                        dve.wait_ge(f_summed, 3 + n + 1)
                        link(dve.scalar_tensor_tensor(res[r][:], res[r][:], ALPHA, y_a[r][:], ALU.mult, ALU.add))
                        norm_statistics(dve, link, res[r], stat[:, r, :], f_var)

                    def scaled_rows(n, r, i, link):
                        dve.wait_ge(f_rstd, n + 1)
                        dve.wait_ge(f_saved[r], 16 * i + 16)
                        dve.wait_ge(f_trans, 2 * n + 2)
                        link(dve.tensor_scalar(nrm[r][:], res[r][:], stat[:, r, 12:13], stat[:, r, 15:16],
                                               ALU.subtract, ALU.mult))
                        dve.tensor_tensor(nrm[r][:], nrm[r][:], ln_g[:], ALU.mult).then_inc(f_scaled, 1)

                    def low_parts(n, r):
                        for j in range(2):
                            dve.wait_ge(f_hi, 2 * n + j + 1)
                            dve.tensor_tensor(act_lo[:, 4 * j:4 * j + 4, ds(n * P, P)],
                                              ps[:, 2 * r + j, :].rearrange("p (k t) -> p k t", k=4),
                                              f32(act_hi[:, 4 * j:4 * j + 4, ds(n * P, P)]), ALU.subtract) \
                                .then_inc(f_lo, 1)

                    link = Link(dve, f_link)
                    summed(0, 0, 0, link)
                    summed(1, 1, 0, link)
                    scaled_rows(0, 0, 0, link)
                    summed(2, 2, 0, link)
                    scaled_rows(1, 1, 0, link)
                    low_parts(0, 0)
                    before_loop, per_tile = link.n, 5
                    with dve.Fori(0, TILES // 3 - 1) as i:
                        link = Link(dve, f_link, before_loop + 3 * per_tile * i)
                        for r in range(3):
                            n = 3 * i + 3 + r
                            summed(n, r, i + 1, link)
                            scaled_rows(3 * i + 2 + r, (r + 2) % 3, i + (1 if r else 0), link)
                            low_parts(3 * i + 1 + r, (r + 1) % 3)
                        assert link.n == 3 * per_tile
                    link = Link(dve, f_link, before_loop + per_tile * (TILES - 3))
                    scaled_rows(TILES - 1, 2, TILES // 3 - 1, link)
                    low_parts(TILES - 2, 1)
                    low_parts(TILES - 1, 2)

            nc.all_engine_barrier()
            nc.gpsimd.sem_clear(range(layer_sems[0].num, layer_sems[-1].num + 1))
            nc.all_engine_barrier()


_INS = ["x", "meta_tokens", "w_in", "conv_w", "lambda_q1", "lambda_k1", "lambda_q2", "lambda_k2", "diff_norm_g",
        "w_out", "ln1_g", "ln1_b", "router_w", "router_bias", "w_gate", "w_up", "w_down", "ln2_g", "ln2_b"]


def kernel(**inputs):
    import numpy as _np
    import concourse.bacc as _bacc
    from concourse import mybir as _mybir
    from concourse.bass_utils import run_bass_kernel_spmd as _run

    nc = _bacc.Bacc("TRN2", target_bir_lowering=False, num_devices=1)
    arrays, args = {}, []
    given = {name: inputs[name] for name in _INS}
    given["conv_w"] = _np.asarray(inputs["conv_w"]).reshape(DEPTH, 3, CONV_TILES, P).transpose(0, 3, 2, 1) \
        .reshape(DEPTH, P, CONV_TILES * 3)
    given.update(consts=shape_constants(), rope=rope_constants(), lam_consts=layer_constants())
    for name, value in given.items():
        a = _np.ascontiguousarray(value)
        arrays[f"in_{name}_dram"] = a
        args.append(nc.dram_tensor(f"in_{name}_dram", a.shape, _mybir.dt.from_np(a.dtype), kind="ExternalInput").ap())
    args.append(nc.dram_tensor("out_0_dram", (1, SEQ, D), _mybir.dt.float32, kind="ExternalOutput").ap())
    build_trunk(nc, *args)
    r = _run(nc, [arrays], core_ids=[0])
    return r.results[0]["out_0_dram"]
```
